# Optimizing a Trainium2 kernel written in Bass

```python
import math
import jax
import jax.numpy as jnp
from jax import lax
import numpy as np

D_MODEL = 1024
BATCH = 1
SEQ = 128
DEPTH = 2
DEC_BATCH = 1
DEC_SEQ = 1024
PAST_LEN = 128

GRID_W = 64
EPS = 1e-6
D_A = 512
SHORT_K = 3
EMB_DIM = 33
FILT_ORDER = 64
DECAY_TARGET = 1e-2
FAST_DECAY_PCT = 0.3
SLOW_DECAY_PCT = 1.5
MIN_DECAY = math.log(DECAY_TARGET) / SLOW_DECAY_PCT
MAX_DECAY = math.log(DECAY_TARGET) / FAST_DECAY_PCT
N_HEADS_B = 8
Q_RANK = 256
KV_RANK = 256
NOPE_DIM = 64
ROPE_DIM = 32
V_DIM = 64
ROPE_BASE = 10000.0
D_B = N_HEADS_B * V_DIM
QK_DIM = NOPE_DIM + ROPE_DIM
ATTN_SCALE = 1.0 / math.sqrt(QK_DIM)
Q_BLOCK = 128
D_C = 1024
N_GROUPS_C = 8
G_C = D_C // N_GROUPS_C
N_EVEN = (DEPTH + 1) // 2
N_ODD = DEPTH // 2
IN_E = 4 * D_A + Q_RANK + KV_RANK + ROPE_DIM + D_B
SPLIT_E = [3 * D_A, 4 * D_A, 4 * D_A + Q_RANK, 4 * D_A + Q_RANK + KV_RANK, 4 * D_A + Q_RANK + KV_RANK + ROPE_DIM]

kernel_name = 'hybrid_hyena_mla_fnet_prefix_step'

def rmsnorm(x, g):
    xf = x.astype(jnp.float32)
    y = xf * lax.rsqrt(jnp.mean(xf * xf, axis=-1, keepdims=True) + EPS)
    return (y * g.astype(jnp.float32)).astype(x.dtype)

def ada_params(cond, w_mod, b_mod):
    mod = jax.nn.silu(cond) @ w_mod + b_mod
    shift, scale, gate = jnp.split(mod[:, None, :], 3, axis=-1)
    return shift, scale, gate

def short_conv(u, w, b):
    L = u.shape[1]
    pad = SHORT_K // 2
    up = jnp.pad(u, ((0, 0), (pad, pad), (0, 0)))
    return b + sum(up[:, k:k + L] * w[k] for k in range(SHORT_K))

def hyena_filters(L, w1, b1, w2, b2, w3):
    f32 = jnp.float32
    t = jnp.linspace(0.0, 1.0, L, dtype=f32)[:, None]
    w = 2.0 * math.pi * jnp.arange(L, dtype=f32)[:, None] / L
    bands = (EMB_DIM - 1) // 2
    f = jnp.linspace(1e-4, bands - 1, bands, dtype=f32)[None, :]
    z = jnp.concatenate([t, jnp.cos(f * w), -jnp.sin(f * w)], axis=-1)
    h = jnp.sin(z @ w1.astype(f32) + b1.astype(f32))
    h = jnp.sin(h @ w2.astype(f32) + b2.astype(f32))
    h = (h @ w3.astype(f32)).reshape(L, 2, D_A)
    deltas = jnp.abs(jnp.linspace(MIN_DECAY, MAX_DECAY, D_A, dtype=f32))
    h = h * jnp.exp(-t * deltas)[:, None, :]
    h = h / jnp.sum(jnp.abs(h), axis=(0, 1), keepdims=True)
    return h[:, 0], h[:, 1]

def hyena(u, conv_w, conv_b, filt, skip):
    L = u.shape[1]
    u = short_conv(u, conv_w, conv_b)
    x0, x1, v = jnp.split(u, 3, axis=-1)
    v = v * x1
    h_fwd, h_bwd = hyena_filters(L, *filt)
    kern = jnp.concatenate([h_fwd, jnp.zeros((1, D_A), jnp.float32), h_bwd[:0:-1]], axis=0)
    vf = jnp.fft.rfft(v.astype(jnp.float32), n=2 * L, axis=1)
    kf = jnp.fft.rfft(kern, n=2 * L, axis=0)
    y = jnp.fft.irfft(vf * kf[None], n=2 * L, axis=1)[:, :L]
    y = y.astype(u.dtype) + v * skip
    return y * x0

def axial_rope_tables(L):
    rows = L // GRID_W
    row = jnp.repeat(jnp.arange(rows, dtype=jnp.float32), GRID_W)
    col = jnp.tile(jnp.arange(GRID_W, dtype=jnp.float32), rows)
    half = ROPE_DIM // 2
    inv = jnp.power(ROPE_BASE, -jnp.arange(0, half, 2, dtype=jnp.float32) / half)
    ang = jnp.stack([row[:, None] * inv, col[:, None] * inv], axis=1)
    return jnp.cos(ang), jnp.sin(ang)

def apply_axial_rope(x, cos, sin):
    nf = ROPE_DIM // 4
    xr = x.astype(jnp.float32).reshape(x.shape[:-1] + (2, 2, nf))
    shp = (cos.shape[0],) + (1,) * (x.ndim - 3) + (2, nf)
    c = cos.reshape(shp)
    s = sin.reshape(shp)
    x1, x2 = xr[..., 0, :], xr[..., 1, :]
    out = jnp.stack([x1 * c - x2 * s, x1 * s + x2 * c], axis=-2)
    return out.reshape(x.shape).astype(x.dtype)

def block_attention(q, k, v):
    B, Lq, H, Dq = q.shape
    nb = Lq // Q_BLOCK
    qb = q.reshape(B, nb, Q_BLOCK, H, Dq).transpose(1, 0, 2, 3, 4)

    def one_block(qi):
        s = jnp.einsum('bqhd,bkhd->bhqk', qi, k).astype(jnp.float32) * ATTN_SCALE
        p = jax.nn.softmax(s, axis=-1)
        return jnp.einsum('bhqk,bkhd->bqhd', p.astype(v.dtype), v)

    o = lax.map(one_block, qb)
    return o.transpose(1, 0, 2, 3, 4).reshape(B, Lq, H, v.shape[-1])

def even_mixer(h, ew, ctx_kv):
    (w_in, conv_w, conv_b, f_w1, f_b1, f_w2, f_b2, f_w3, skip, qg, kvg, w_uq, w_ukv, w_out) = ew
    B, L, _ = h.shape
    proj = h @ w_in
    u_a, g_a, cq, ckv, krope, g_b = jnp.split(proj, SPLIT_E, axis=-1)
    y_a = hyena(u_a, conv_w, conv_b, (f_w1, f_b1, f_w2, f_b2, f_w3), skip)
    cq = rmsnorm(cq, qg)
    ckv = rmsnorm(ckv, kvg)
    q = (cq @ w_uq).reshape(B, L, N_HEADS_B, QK_DIM)
    if ctx_kv is None:
        keys_c, keys_r = ckv, krope
    else:
        cos, sin = axial_rope_tables(L)
        q = jnp.concatenate([q[..., :NOPE_DIM], apply_axial_rope(q[..., NOPE_DIM:], cos, sin)], axis=-1)
        ctx_ckv, ctx_krope = ctx_kv
        keys_c = jnp.concatenate([ctx_ckv, ckv], axis=1)
        keys_r = jnp.concatenate([ctx_krope, apply_axial_rope(krope, cos, sin)], axis=1)
    Lk = keys_c.shape[1]
    kv = (keys_c @ w_ukv).reshape(B, Lk, N_HEADS_B, NOPE_DIM + V_DIM)
    k = jnp.concatenate([kv[..., :NOPE_DIM], jnp.broadcast_to(keys_r[:, :, None, :], (B, Lk, N_HEADS_B, ROPE_DIM))], axis=-1)
    v = kv[..., NOPE_DIM:]
    o_b = block_attention(q, k, v).reshape(B, L, D_B)
    y = jnp.concatenate([y_a * jax.nn.silu(g_a), o_b * jax.nn.silu(g_b)], axis=-1) @ w_out
    return y, ckv, krope

def odd_mixer(h, w_in, fnet_w, w_out):
    B, L, _ = h.shape
    u, g = jnp.split(h @ w_in, 2, axis=-1)
    uf = u.astype(jnp.float32).reshape(B, L, N_GROUPS_C, G_C)
    m = jnp.fft.fft2(uf, axes=(1, 3), norm='ortho').real.astype(h.dtype)
    y = jnp.einsum('blgc,gcd->blgd', m, fnet_w).reshape(B, L, D_C)
    return (y * jax.nn.silu(g)) @ w_out

def setup_inputs(seed: int = 0) -> dict:
    key = jax.random.key(seed)
    ks = jax.random.split(key, 32)
    f32 = jnp.float32

    def nrm(k, shape, s):
        return jax.random.normal(k, shape, f32) * s

    return {
        'x_prompt': nrm(ks[0], (BATCH, SEQ, D_MODEL), 1.0),
        'x_sample': nrm(ks[1], (DEC_BATCH, DEC_SEQ, D_MODEL), 1.0),
        'c': nrm(ks[2], (DEC_BATCH, D_MODEL), 1.0),
        'cache_ckv': nrm(ks[3], (DEC_BATCH, N_EVEN, PAST_LEN, KV_RANK), 1.0),
        'cache_krope': nrm(ks[4], (DEC_BATCH, N_EVEN, PAST_LEN, ROPE_DIM), 1.0),
        'c_ctx': nrm(ks[5], (D_MODEL,), 1.0),
        'norm_g': 1.0 + nrm(ks[6], (DEPTH, D_MODEL), 0.02),
        'w_mod': nrm(ks[7], (DEPTH, D_MODEL, 3 * D_MODEL), D_MODEL ** -0.5),
        'b_mod': nrm(ks[8], (DEPTH, 3 * D_MODEL), 0.02),
        'w_in_e': nrm(ks[9], (N_EVEN, D_MODEL, IN_E), D_MODEL ** -0.5),
        'conv_w': nrm(ks[10], (N_EVEN, SHORT_K, 3 * D_A), SHORT_K ** -0.5),
        'conv_b': nrm(ks[11], (N_EVEN, 3 * D_A), 0.02),
        'filt_w1': nrm(ks[12], (N_EVEN, EMB_DIM, FILT_ORDER), EMB_DIM ** -0.5),
        'filt_b1': nrm(ks[13], (N_EVEN, FILT_ORDER), 0.02),
        'filt_w2': nrm(ks[14], (N_EVEN, FILT_ORDER, FILT_ORDER), FILT_ORDER ** -0.5),
        'filt_b2': nrm(ks[15], (N_EVEN, FILT_ORDER), 0.02),
        'filt_w3': nrm(ks[16], (N_EVEN, FILT_ORDER, 2 * D_A), FILT_ORDER ** -0.5),
        'hyena_skip': nrm(ks[17], (N_EVEN, D_A), 1.0),
        'q_norm_g': 1.0 + nrm(ks[18], (N_EVEN, Q_RANK), 0.02),
        'kv_norm_g': 1.0 + nrm(ks[19], (N_EVEN, KV_RANK), 0.02),
        'w_uq': nrm(ks[20], (N_EVEN, Q_RANK, N_HEADS_B * QK_DIM), Q_RANK ** -0.5),
        'w_ukv': nrm(ks[21], (N_EVEN, KV_RANK, N_HEADS_B * (NOPE_DIM + V_DIM)), KV_RANK ** -0.5),
        'w_out_e': nrm(ks[22], (N_EVEN, D_A + D_B, D_MODEL), (D_A + D_B) ** -0.5),
        'w_in_o': nrm(ks[23], (N_ODD, D_MODEL, 2 * D_C), D_MODEL ** -0.5),
        'fnet_w': nrm(ks[24], (N_ODD, N_GROUPS_C, G_C, G_C), G_C ** -0.5),
        'w_out_o': nrm(ks[25], (N_ODD, D_C, D_MODEL), D_C ** -0.5),
        'final_g': 1.0 + nrm(ks[26], (D_MODEL,), 0.02),
    }

def reference(x_prompt, x_sample, c, cache_ckv, cache_krope, c_ctx, norm_g, w_mod, b_mod,
              w_in_e, conv_w, conv_b, filt_w1, filt_b1, filt_w2, filt_b2, filt_w3, hyena_skip,
              q_norm_g, kv_norm_g, w_uq, w_ukv, w_out_e, w_in_o, fnet_w, w_out_o, final_g):
    xp = x_prompt
    xs = x_sample
    new_ckv = []
    new_krope = []
    for i in range(DEPTH):
        j = i // 2
        sh_p, sc_p, gt_p = ada_params(c_ctx[None, :], w_mod[i], b_mod[i])
        sh_s, sc_s, gt_s = ada_params(c, w_mod[i], b_mod[i])
        hp = rmsnorm(xp, norm_g[i]) * (1.0 + sc_p) + sh_p
        hs = rmsnorm(xs, norm_g[i]) * (1.0 + sc_s) + sh_s
        if i % 2 == 0:
            ew = (w_in_e[j], conv_w[j], conv_b[j], filt_w1[j], filt_b1[j], filt_w2[j], filt_b2[j],
                  filt_w3[j], hyena_skip[j], q_norm_g[j], kv_norm_g[j], w_uq[j], w_ukv[j], w_out_e[j])
            yp, ckv_p, krope_p = even_mixer(hp, ew, None)
            ys, _, _ = even_mixer(hs, ew, (cache_ckv[:, j], cache_krope[:, j]))
            new_ckv.append(ckv_p)
            new_krope.append(krope_p)
        else:
            yp = odd_mixer(hp, w_in_o[j], fnet_w[j], w_out_o[j])
            ys = odd_mixer(hs, w_in_o[j], fnet_w[j], w_out_o[j])
        xp = xp + gt_p * yp
        xs = xs + gt_s * ys
    y_prompt = rmsnorm(xp, final_g)
    y_sample = rmsnorm(xs, final_g)
    state_ckv = jnp.stack(new_ckv, axis=1)
    state_krope = jnp.stack(new_krope, axis=1)
    return (y_prompt, y_sample, state_ckv, state_krope)


_drawn_inputs = setup_inputs


def setup_inputs(seed=0):
    import zlib

    import numpy as np

    out = dict(_drawn_inputs(seed))
    spreads = {}
    factors = {'cache_ckv': 8.0,
     'cache_krope': 8.0,
     'conv_b': 3.331,
     'filt_b1': 8.0,
     'filt_b2': 7.935,
     'q_norm_g': 8.0,
     'kv_norm_g': 2.92,
     'final_g': 2.753}
    for name, (base, spread) in spreads.items():
        noise = np.random.default_rng([zlib.crc32(name.encode()), seed]).standard_normal(out[name].shape)
        drawn = base * np.exp(spread * noise) if base else spread * noise
        out[name] = jnp.asarray(drawn.astype(out[name].dtype))
    for name, factor in factors.items():
        out[name] = (out[name] * factor).astype(out[name].dtype)
    return out
```

```python
import math
from contextlib import ExitStack

import numpy as np

import concourse.bass as bass
from concourse import mybir

F32 = mybir.dt.float32
ALU = mybir.AluOpType
ACT = mybir.ActivationFunctionType

P = 128
D = 1024
KT = D // P
LS, LP = 1024, 128
TOK = LS + LP
NT = TOK // P
PROMPT = NT - 1
CHUNKS = [(0, 512), (512, 512), (1024, 128)]
EPS = 1e-6
DA = 512
CA = DA // P
BANDS = 16
EMB = 2 * BANDS + 1
FO = 64
HEADS, NOPE, ROPE, VD, RANK = 8, 64, 32, 64, 256
QK = NOPE + ROPE
SCALE = 1.0 / math.sqrt(QK)
PAST = 128
KEYS = PAST + LS
ALLKEYS = KEYS + LP
KS3 = KEYS // 3
GRID_W = 64
HALF = LS // 2
NK = HALF // P
GROUPS = 8
FQ = HALF // 2 + 2
LAT = 2 * RANK + ROPE
R_BMOD, R_NG, R_CW, R_CB, R_SKIP, R_ALL = 0, 48, 64, 100, 112, 116
MAGIC = 1.5 * 2.0 ** 23
TWO_PI_HI = 6.28125
TWO_PI_LO = float(np.float32(2 * math.pi - 6.28125))
PI_IN = 3.1415925


def build(nc, T):
    ctx = ExitStack()
    with ctx:
        def sb(name, width):
            return ctx.enter_context(nc.sbuf_tensor(name, [P, width], F32))

        def sem(name):
            return ctx.enter_context(nc.semaphore(name))

        def sems(name, n):
            return [sem(f"{name}{i}") for i in range(n)]

        def split(ap, a):
            return ap.rearrange("p (a b) -> p a b", a=a)

        H = sb("H", 18432)
        H2 = 9216
        SCR = sb("SCR", 9600)
        WR = sb("WR", 5120)
        VR = sb("VR", 5120)
        KR_ = sb("KEYS", 7424)
        bank = ctx.enter_context(nc.psum_tensor("bank", [P, 8, 512], F32))

        def banks(b, n, lo, hi):
            return bank[:, b:b + n, :].rearrange("p a n -> p (a n)")[:, lo:hi]

        ident = sb("ident", P)
        ones = sb("ones", P)
        half_neg = sb("half_neg", 2)
        vec_rows = sb("vec_rows", P)
        cond_rows = sb("cond_rows", P)
        col = sb("col", R_ALL)
        cond = split(sb("cond", 16)[:, :], KT)
        modc = split(sb("modc", 96)[:, :], 48)
        gsc = split(sb("gsc", 32)[:, :], 16)
        lat_g = sb("lat_g", 2 * RANK)
        lat = [sb(f"lat{i}", 2 * RANK) for i in range(2)]
        rope_t = split(sb("rope_t", 512)[:, :], 2)
        rope_q = sb("rope_q", LS)
        kro = split(sb("kro", 10 * ROPE)[:, :], 10)
        krs = split(sb("krs", 8 * ROPE)[:, :], 8)
        krr = split(sb("krr", 10 * ROPE)[:, :], 10)
        fw1 = sb("fw1", FO)
        fw2 = sb("fw2", FO)
        fb = sb("fb", 2)
        fw3 = sb("fw3", 2 * DA)
        tp = split(sb("tp", 2 * P)[:, :], 2)
        tpi = split(sb("tpi", 2 * P)[:, :], 2)
        ssq = sb("ssq", 3 * NT)
        rstd = sb("rstd", 3 * NT)
        ssq2 = sb("ssq2", 2 * NT)
        rstd2 = sb("rstd2", 2 * NT)
        rnorm = sb("rnorm", 2 * CA)
        amax = sb("amax", 2)
        nmax = sb("nmax", 2)
        rsum = sb("rsum", 2)
        rinv = sb("rinv", 2)

        wm = [split(H[:, 4096 * i:4096 * (i + 1)], KT) for i in range(2)]
        hT = split(H[:, 0:KT * TOK], KT)
        w_lat = split(H[:, H2:H2 + KT * LAT], KT)
        sd = H[:, 0:NT * 2 * DA].rearrange("p (t s n) -> p t s n", t=NT, s=2)
        zz = H[:, H2:H2 + NK * 4 * DA].rearrange("p (k q n) -> p k q n", k=NK, q=4)
        yT = split(H[:, 0:KT * TOK], KT)
        w_oe = split(H[:, H2:H2 + KT * D], KT)
        xnH = split(H[:, H2:H2 + NT * D], NT)
        y1T = split(H[:, H2:H2 + KT * TOK], KT)
        w_oo = split(H[:, 0:KT * D], KT)

        xs = split(SCR[:, 0:NT * D], NT)
        u1 = SCR[:, 0:TOK]
        vt = SCR[:, TOK:2 * TOK]
        x0 = SCR[:, 2 * TOK:3 * TOK]
        ga = SCR[:, 3 * TOK:4 * TOK]
        gb = SCR[:, 4 * TOK:5 * TOK]
        f_z = SCR[:, 5 * TOK:6 * TOK]
        f_x = SCR[:, 6 * TOK:7 * TOK]
        f_r = SCR[:, 7 * TOK:8 * TOK]
        f_h = [split(SCR[:, 1024 * i:1024 * (i + 1)], 2) for i in range(2)]
        f_abs = split(SCR[:, 2048:3072], 2)
        f_mag = [split(SCR[:, 3072 + 1024 * i:4096 + 1024 * i], 2) for i in range(2)]
        ks = split(SCR[:, 0:2048], 4)
        vs = split(SCR[:, 2048:4096], 4)
        kp = split(SCR[:, 4096:6144], 4)
        vp = split(SCR[:, 6144:8192], 4)
        yp = split(SCR[:, 8192:9216], 2)
        ti = SCR[:, 0:8192].rearrange("p (k q n) -> p k q n", k=NK, q=4)
        qT = [SCR[:, TOK * i:TOK * (i + 1)] for i in range(2)]
        px = [SCR[:, TOK * (2 + i):TOK * (3 + i)] for i in range(2)]
        pT = [split(SCR[:, TOK * (4 + i):TOK * (5 + i)], NT) for i in range(2)]
        opair = split(SCR[:, TOK * 6:TOK * 7], NT)
        sgate = SCR[:, TOK * 7:TOK * 8]

        wr = [split(WR[:, 1024 * i:1024 * (i + 1)], KT) for i in range(5)]
        decay = split(WR[:, 0:NT * DA], NT)
        tf = [WR[:, 2048 * i:2048 * (i + 1)].rearrange("p (q n k) -> p q n k", q=4, n=NK) for i in range(2)]
        vf_in = [WR[:, TOK * i:TOK * (i + 1)] for i in range(2)]
        xg_in = [WR[:, TOK * (2 + i):TOK * (3 + i)] for i in range(2)]
        w_v = split(WR[:, 0:1024], 2)
        w_q = [split(WR[:, 1024 + 256 * i:1280 + 256 * i], 2) for i in range(2)]
        w_k = [split(WR[:, 1536 + 128 * i:1664 + 128 * i], 2) for i in range(2)]
        rtmp = WR[:, 1792:2304]
        csw = WR[:, 2048:2304]
        fw = WR[:, 2304:2432]
        gateb = split(WR[:, 2560:4608], 2)
        diag = split(WR[:, 4608:5120], 4)

        junk = [VR[:, 1024 * i:1024 * (i + 1)] for i in range(2)]
        ckc = VR[:, 4096:4352]
        vtm = split(VR[:, 0:NT * DA], NT)
        vall = split(VR[:, :], 10)
        uT = VR[:, 0:TOK]
        sg = VR[:, TOK:2 * TOK]
        ab = split(VR[:, 2304:4608], NT)
        fgb = VR[:, 4096:5120]

        cqT = split(KR_[:, 0:2304], 2)
        keysT = split(KR_[:, 2304:4864], 2)
        kT = [KR_[:, 4864 + 1280 * i:6144 + 1280 * i] for i in range(2)]
        tl = KR_[:, 0:16 * FQ].rearrange("p (n q k) -> p n q k", n=NK, q=4)
        cd = split(KR_[:, 4128:4644], 2)
        tt = split(KR_[:, 4644:5676], 4)
        yt = KR_[:, 5676:6828]
        cg = KR_[:, 6828:7084]
        tlp = split(KR_[:, 7084:7340], 2)

        consts_made = sem("consts_made")
        vec_in, small_in, wlat_in, ckc_in = sem("vec_in"), sem("small_in"), sem("wlat_in"), sem("ckc_in")
        vec_T, cols_made, cond_made = sem("vec_T"), sem("cols_made"), sem("cond_made")
        wm_in, wm_used, mod_made = sems("wm_in", 2), sems("wm_used", 2), sem("mod_made")
        x_in = sems("x_in", NT)
        x_sq, x_rs, x_n = sem("x_sq"), sem("x_rs"), sem("x_n")
        x_T, h_act, h_dve = sem("x_T"), sem("h_act"), sem("h_dve")
        l_mm, l_sq, l_rs, l_lat, l_T, l_cp = (sem(n) for n in ("l_mm", "l_sq", "l_rs", "l_lat", "l_T", "l_cp"))
        kr_in, kr_rot, kr_T, kr_cp = sem("kr_in"), sem("kr_rot"), sem("kr_T"), sem("kr_cp")
        st_ckv, st_kro = sem("st_ckv"), sem("st_kro")
        wr_in, d_mm, d_mid, d_rel = sems("wr_in", 5), sems("d_mm", 5), sems("d_mid", 3), sems("d_rel", 5)
        v_ready, v_T6, v_T7, v_rel6, v_rel7 = (sem(n) for n in ("v_ready", "v_T6", "v_T7", "v_rel6", "v_rel7"))
        xg_ready = sem("xg_ready")
        sp_v, sp_x, sp_g = sem("sp_v"), sem("sp_x"), sem("sp_g")
        f_in, f_mm, f_red, f_sin = sem("f_in"), sem("f_mm"), sem("f_red"), sem("f_sin")
        dec_in, fh_mm, fh_made, fh_abs, sd_made = (sem(n) for n in ("dec_in", "fh_mm", "fh_made", "fh_abs", "sd_made"))
        nrm_mm, nrm_made = sem("nrm_mm"), sem("nrm_made")
        tf_in = sems("tf_in", 2)
        k_mm, k_cp, v_mm, v_cp, kp_made, z_made = (sem(n) for n in ("k_mm", "k_cp", "v_mm", "v_cp", "kp_made", "z_made"))
        fh_mag = sem("fh_mag")
        ti_in, vf_in_s, xg_in_s, i_mm, i_done = sem("ti_in"), sems("vfr", 2), sems("xgr", 2), sem("i_mm"), sem("i_done")
        wv_in, wq_in, v_all_mm, v_all_cp = sem("wv_in"), sems("wq_in", 2), sem("v_all_mm"), sem("v_all_cp")
        dg_made, dg_mm, gb_cp = sem("dg_made"), sem("dg_mm"), sem("gb_cp")
        pj_mm, pj_q, pj_k = sem("pj_mm"), sem("pj_q"), sem("pj_k")
        rope1 = sem("rope1")
        s_mm, s_max, s_exp = sem("s_mm"), sem("s_max"), sem("s_exp")
        pt_mm = [sem("pt_mm0"), sem("pt_mm1"), sem("pt_mm2")]
        pt_cp = [sem("pt_cp0"), sem("pt_cp1"), sem("pt_cp2")]
        o_mm, o_cp = sem("o_mm"), sem("o_cp")
        ot_mm, ot_cp, sg_in = sem("ot_mm"), sem("ot_cp"), sem("sg_in")
        woe_in = sem("woe_in")
        g_mm, g_add = sem("g_mm"), sem("g_add")
        tl_in = sem("tl_in")
        ow_in, ow_used, fw_in = sems("ow_in", 2), sems("ow_used", 2), sem("fw_in")
        csw_mm, csw_cp, u_mm, u_cp, gt_mm, gt_cp = (sem(n) for n in ("csw_mm", "csw_cp", "u_mm", "u_cp", "gt_mm", "gt_cp"))
        ab_mm, ab_e, ab_o = sem("ab_mm"), sem("ab_e"), sem("ab_o")
        y_mm, cd_cp, y_done = sem("y_mm"), sem("cd_cp"), sem("y_done")
        woo_in, fg_in = sem("woo_in"), sem("fg_in")
        out_ready, st_out = sem("out_ready"), sem("st_out")
        dve_done, pool_done = sem("dve_done"), sem("pool_done")

        block = ctx.enter_context(nc.Block())

        class Chain:
            def __init__(self, eng, s):
                self.eng, self.s, self.n, self.i, self.per, self.k = eng, s, 0, None, 0, 0

            def loop(self, i, per):
                self.i, self.per, self.k = i, per, 0

            def end(self, trips):
                assert self.k == self.per, self.k
                self.n += trips * self.per
                self.i = None

            def __call__(self, ins):
                ins.then_inc(self.s, 1)
                if self.i is None:
                    self.n += 1
                    self.eng.wait_ge(self.s, self.n)
                else:
                    self.k += 1
                    self.eng.wait_ge(self.s, self.i * self.per + self.n + self.k)

        @block.sync
        def _(sp):
            sp.dma_start(vec_rows[0:R_ALL, :], T["vecs"]).then_inc(vec_in, 16)
            sp.dma_start(cond_rows[0:16, :], T["cond"]).then_inc(vec_in, 16)
            for i in range(2):
                sp.dma_start(wm[i], T["w_mod"][i]).then_inc(wm_in[i], 16)
            for t in range(4):
                sp.dma_start(xs[:, t, :], T["x_sample"][t * P:(t + 1) * P, :]).then_inc(x_in[t], 16)
            with sp.Fori(1, 6) as i:
                for s in range(2):
                    sp.wait_ge(wm_used[s], i)
                    sp.dma_start(wm[s].unsqueeze(1), T["w_mod"][bass.ds(i * 2 + s, 1)].rearrange("a p k n -> p a k n")).then_inc(wm_in[s], 16)
            for t in range(4, NT):
                src = T["x_prompt"] if t == PROMPT else T["x_sample"][t * P:(t + 1) * P, :]
                sp.dma_start(xs[:, t, :], src).then_inc(x_in[t], 16)
            sp.dma_start(w_lat, T["w_lat"]).then_inc(wlat_in, 16)
            smalls = [
                (lat_g[:, 0:RANK], T["qg"].partition_broadcast(P)), (lat_g[:, RANK:], T["kvg"].partition_broadcast(P)),
                (rope_t, T["rope_t"]), (rope_q[64:128, :], T["rope_q"]), (kro[:, 0, :], T["cache_krope"]),
            ]
            for d, s in smalls:
                sp.dma_start(d, s).then_inc(small_in, 16)
            for j in range(5):
                sp.dma_start(wr[j], T["w_in"][j, 0]).then_inc(wr_in[j], 16)
            sp.dma_start(ckc, T["cache_ckv"]).then_inc(ckc_in, 16)
            fsm = [(fw1[0:EMB, :], T["f_w1"]), (fw2[0:FO, :], T["f_w2"]), (fb[0:FO, :], T["f_b"]),
                   (fw3[0:FO, :], T["f_w3"]), (tp, T["tp"]), (tpi, T["tpi"])]
            for d, s in fsm:
                sp.dma_start(d, s).then_inc(f_in, 16)
            sp.wait_ge(l_lat, NT)
            sp.dma_start(T["state_ckv"], lat[PROMPT % 2][:, RANK:]).then_inc(st_ckv, 16)
            sp.dma_start(T["state_krope"], kro[:, 9, :]).then_inc(st_kro, 16)
            with sp.Fori(1, CA) as i:
                for j in range(5):
                    sp.wait_ge(d_mm[j], i)
                    sp.dma_start(wr[j].unsqueeze(1), T["w_in"][j, bass.ds(i, 1)].rearrange("a p k n -> p a k n")).then_inc(wr_in[j], 16)
            sp.wait_ge(x_n, NT)
            sp.wait_ge(x_T, 24)
            sp.dma_start(f_z[0:EMB, :], T["zT"]).then_inc(f_in, 16)
            sp.wait_ge(d_mm[4], CA)
            sp.dma_start(decay, T["decay"]).then_inc(dec_in, 16)
            sp.wait_ge(fh_abs, NT)
            for s in range(2):
                sp.dma_start(tf[s], T["tf"][s]).then_inc(tf_in[s], 16)
            for s in range(2):
                sp.wait_ge(v_mm, s + 1)
                sp.dma_start(tf[s], T["tf"][2 + s]).then_inc(tf_in[s], 16)
            sp.wait_ge(v_mm, NK)
            sp.wait_ge(sp_v, 16 * (CA + 1))
            sp.wait_ge(sp_x, 16 * (CA + 1))
            sp.wait_ge(sp_g, 16 * (CA + 1))
            for c in range(2):
                sp.dma_start(vf_in[c], T["sp_v"][c]).then_inc(vf_in_s[c], 16)
                sp.dma_start(xg_in[c], T["sp_x"][c]).then_inc(xg_in_s[c], 16)
            sp.wait_ge(z_made, NK + 1)
            sp.dma_start(ti, T["ti"]).then_inc(ti_in, 16)
            for c in range(2, CA):
                sp.wait_ge(i_done, c - 1)
                sp.dma_start(vf_in[c % 2], T["sp_v"][c]).then_inc(vf_in_s[c % 2], 16)
                sp.dma_start(xg_in[c % 2], T["sp_x"][c]).then_inc(xg_in_s[c % 2], 16)
            sp.wait_ge(i_done, CA)
            sp.dma_start(w_v, T["w_v"]).then_inc(wv_in, 16)
            for s in range(2):
                sp.dma_start(w_q[s], T["w_q"][s]).then_inc(wq_in[s], 16)
                sp.dma_start(w_k[s], T["w_k"][s]).then_inc(wq_in[s], 16)
            sp.dma_start(sgate, T["sp_g"][0]).then_inc(sg_in, 16)
            sp.dma_start(w_oe, T["w_oe"]).then_inc(woe_in, 16)
            with sp.Fori(1, HEADS // 2) as i:
                for s in range(2):
                    sp.wait_ge(pj_mm, i * 12 + (6 * s - 6))
                    sp.dma_start(w_q[s].unsqueeze(1), T["w_q"][bass.ds(i * 2 + s, 1)].rearrange("a p k n -> p a k n")).then_inc(wq_in[s], 16)
                    sp.dma_start(w_k[s].unsqueeze(1), T["w_k"][bass.ds(i * 2 + s, 1)].rearrange("a p k n -> p a k n")).then_inc(wq_in[s], 16)
                sp.wait_ge(ot_cp, i * 3)
                sp.dma_start(sgate.unsqueeze(1), T["sp_g"][bass.ds(i, 1)].rearrange("a p n -> p a n")).then_inc(sg_in, 16)
            sp.wait_ge(ot_cp, 3 * HEADS // 2)
            for t in range(NT):
                src = T["x_prompt"] if t == PROMPT else T["x_sample"][t * P:(t + 1) * P, :]
                sp.dma_start(xs[:, t, :], src).then_inc(x_in[t], 16)
            for d, s in ((tl, T["tl"]), (cg, T["cg"]), (tlp, T["tlp"])):
                sp.dma_start(d, s).then_inc(tl_in, 16)
            for j in range(2):
                sp.dma_start(wr[j], T["w_io"][j, 0]).then_inc(ow_in[j], 16)
            sp.dma_start(fw, T["fnet_w"][0]).then_inc(fw_in, 16)
            with sp.Fori(1, GROUPS) as i:
                for j in range(2):
                    sp.wait_ge((u_mm, gt_mm)[j], i)
                    sp.dma_start(wr[j].unsqueeze(1), T["w_io"][j, bass.ds(i, 1)].rearrange("a p k n -> p a k n")).then_inc(ow_in[j], 16)
                sp.wait_ge(csw_mm, i)
                sp.dma_start(fw.unsqueeze(1), T["fnet_w"][bass.ds(i, 1)].rearrange("a p n -> p a n")).then_inc(fw_in, 16)
            sp.wait_ge(gt_mm, GROUPS)
            sp.dma_start(w_oo, T["w_oo"]).then_inc(woo_in, 16)
            sp.wait_ge(y_done, GROUPS + 1)
            sp.dma_start(fgb, T["final_g"].partition_broadcast(P)).then_inc(fg_in, 16)
            for t in range(NT):
                sp.wait_ge(out_ready, t + 1)
                dst = T["y_prompt"] if t == PROMPT else T["y_sample"][t * P:(t + 1) * P, :]
                sp.dma_start(dst, xs[:, t, :]).then_inc(st_out, 16)
            sp.wait_ge(st_out, 16 * NT)
            sp.wait_ge(st_ckv, 16)
            sp.wait_ge(st_kro, 16)

        @block.tensor
        def _(pe):
            def product(out, pairs):
                for n, (l, r) in enumerate(pairs):
                    last = nc.tensor.matmul(out, l, r, start=(n == 0), stop=(n == len(pairs) - 1))
                return last

            pe.wait_ge(consts_made, 3)
            pe.wait_ge(vec_in, 32)
            nc.tensor.transpose(bank[:, 7, 0:R_ALL], vec_rows[0:R_ALL, :], ident[0:R_ALL, 0:R_ALL])
            nc.tensor.transpose(bank[:, 7, P:P + 16], cond_rows[0:16, :], ident[0:16, 0:16]).then_inc(vec_T, 1)
            pe.wait_ge(cond_made, 1)
            with pe.Fori(0, 6) as i:
                for s in range(2):
                    pe.wait_ge(wm_in[s], i * 16 + 16)
                    for q in range(4):
                        for k in range(KT):
                            last = nc.tensor.matmul(bank[:, 0, bass.ds(i * 16 + (s * 8 + q * 2), 2)], wm[s][:, k, q * P:(q + 1) * P],
                                                    cond[:, k, :], start=(k == 0), stop=(k == KT - 1))
                    last.then_inc(wm_used[s], 1)

            def layer_input_T(l, src):
                e = 0
                for ch, (_, width) in enumerate(CHUNKS):
                    tiles = range(4 * ch, 4 * ch + width // P)
                    pe.wait_ge(x_n, NT * l + tiles[-1] + 1)
                    for k in range(KT):
                        if e >= 6:
                            pe.wait_ge((h_act, h_dve)[e % 2], 12 * l + (e - 6) // 2 + 1)
                        for n, t in enumerate(tiles):
                            last = nc.tensor.transpose(bank[:, 1 + e % 6, n * P:(n + 1) * P], src[:, t, k * P:(k + 1) * P], ident[:, :])
                        last.then_inc(x_T, 1)
                        e += 1

            layer_input_T(0, xs)
            pe.wait_ge(h_act, 12)
            pe.wait_ge(h_dve, 12)
            pe.wait_ge(wlat_in, 16)
            pe.wait_ge(ckc_in, 16)
            for j in range(2):
                last = nc.tensor.transpose(bank[:, 6, j * P:(j + 1) * P], ckc[:, j * P:(j + 1) * P], ident[:, :])
            last.then_inc(l_T, 1)

            def lat_T(t):
                pe.wait_ge(l_lat, t + 1)
                if t >= 2:
                    pe.wait_ge(l_cp, t)
                for j in range(4):
                    last = nc.tensor.transpose(bank[:, 4 + t % 2, j * P:(j + 1) * P], lat[t % 2][:, j * P:(j + 1) * P], ident[:, :])
                last.then_inc(l_T, 1)

            for t in range(NT):
                if t >= 2:
                    pe.wait_ge(l_lat, t - 1)
                for j, (a, b) in enumerate(((0, RANK), (RANK, LAT))):
                    last = product(bank[:, 2 * (t % 2) + j, 0:b - a],
                                   [(hT[:, k, t * P:(t + 1) * P], w_lat[:, k, a:b]) for k in range(KT)])
                last.then_inc(l_mm, 1)
                if t:
                    lat_T(t - 1)
            lat_T(NT - 1)
            pe.wait_ge(kr_rot, 1)
            for t in range(10):
                last = nc.tensor.transpose(bank[0:ROPE, t // 4, (t % 4) * P:(t % 4 + 1) * P], krr[:, t, :], ident[:, :])
            last.then_inc(kr_T, 1)
            pe.wait_ge(l_cp, NT + 1)
            pe.wait_ge(kr_cp, 1)

            for s in (d_rel[3], d_rel[4], v_rel6, v_rel7):
                pe.sem_inc(s, 1)
            with pe.Fori(0, CA) as c:
                for j in range(5):
                    pe.wait_ge(wr_in[j], c * 16 + 16)
                    if j < 2:
                        pe.wait_ge(d_rel[4 - j], c + 1)
                    else:
                        pe.wait_ge(d_rel[j - 2], c + 1)
                    for n, (a, w) in enumerate(CHUNKS):
                        last = product(bank[:, 3 * (j % 2) + n, 0:w], [(wr[j][:, k, :], hT[:, k, a:a + w]) for k in range(KT)])
                    last.then_inc(d_mm[j], 1)
                    if j == 2:
                        pe.wait_ge(v_ready, c + 1)
                        for odd in range(2):
                            pe.wait_ge((v_rel6, v_rel7)[odd], c * (2 - odd) + 1)
                            for n in range(NK):
                                last = nc.tensor.transpose(bank[:, 6 + odd, n * P:(n + 1) * P], vt[:, 2 * P * n + odd:2 * P * (n + 1):2], ident[:, :])
                            last.then_inc((v_T6, v_T7)[odd], 1)
                        pe.wait_ge(v_rel6, c * 2 + 2)
                        nc.tensor.transpose(bank[:, 6, 0:P], vt[:, LS:TOK], ident[:, :]).then_inc(v_T6, 1)

            pe.wait_ge(d_rel[4], CA + 1)
            pe.wait_ge(d_rel[3], CA + 1)
            pe.wait_ge(f_in, 16 * 7)
            for n, (a, w) in enumerate(CHUNKS):
                last = nc.tensor.matmul(bank[0:FO, n, 0:w], fw1[0:EMB, :], f_z[0:EMB, a:a + w], start=True, stop=True)
            last.then_inc(f_mm, 1)
            pe.wait_ge(f_sin, 1)
            for n, (a, w) in enumerate(CHUNKS):
                last = nc.tensor.matmul(bank[0:FO, n, 0:w], fw2[0:FO, :], f_z[0:FO, a:a + w], start=True, stop=True)
            last.then_inc(f_mm, 1)
            pe.wait_ge(f_sin, 2)
            for t in range(NT):
                if t >= 3:
                    pe.wait_ge(fh_made, t - 2)
                for j in range(2):
                    last = nc.tensor.matmul(bank[:, 2 * (t % 3) + j, :], f_z[0:FO, t * P:(t + 1) * P], fw3[0:FO, j * DA:(j + 1) * DA], start=True, stop=True)
                last.then_inc(fh_mm, 1)
            pe.wait_ge(fh_abs, NT)
            pe.wait_ge(v_rel6, 2 * CA + 1)
            for w in range(2):
                for c in range(CA):
                    last = nc.tensor.matmul(bank[:, 6, w * CA + c:w * CA + c + 1], f_abs[:, w, c * P:(c + 1) * P], ones[:, 0:1], start=True, stop=True)
            last.then_inc(nrm_mm, 1)

            pe.wait_ge(sd_made, NT)
            pe.wait_ge(nrm_made, 1)
            pe.wait_ge(v_rel7, CA + 1)
            for kt in range(NK):
                s = kt % 2
                pe.wait_ge(tf_in[s], 16 * (kt // 2 + 1))
                if kt:
                    pe.wait_ge(k_cp, kt)
                for q in range(4):
                    last = product(bank[:, q, :], [(tf[s][:, q, n, :], sd[:, n + NK * (q // 2), q % 2, :]) for n in range(NK)])
                last.then_inc(k_mm, 1)
                if kt:
                    pe.wait_ge(v_cp, kt)
                for q in range(4):
                    last = product(bank[:, 4 + q, :], [(tf[s][:, q, n, :], vtm[:, n + NK * (q // 2), :]) for n in range(NK)])
                last.then_inc(v_mm, 1)
            pe.wait_ge(k_cp, NK)
            for q in range(2):
                nc.tensor.matmul(bank[:, q, :], tp[:, q, :], sd[:, PROMPT, q, :], start=True, stop=True)
            for q in range(2):
                last = nc.tensor.matmul(bank[:, 2 + q, :], tp[:, q, :], vtm[:, PROMPT, :], start=True, stop=True)
            last.then_inc(k_mm, 1)

            pe.wait_ge(z_made, NK + 1)
            pe.wait_ge(ti_in, 16)
            for c in range(CA):
                if c >= 2:
                    pe.wait_ge(i_done, c - 1)
                b0 = 3 * (c % 2)
                for odd in range(2):
                    product(bank[:, b0 + odd, :], [(zz[:, kt, 2 * odd + q, c * P:(c + 1) * P], ti[:, kt, 2 * odd + q, :])
                                                   for kt in range(NK) for q in range(2)])
                product(bank[:, b0 + 2, 0:P], [(yp[:, q, c * P:(c + 1) * P], tpi[:, q, :]) for q in range(2)]).then_inc(i_mm, 1)

            pe.wait_ge(i_done, CA)
            pe.wait_ge(wv_in, 16)
            for t in range(10):
                if t >= 2:
                    pe.wait_ge(v_all_cp, t - 1)
                product(bank[:, 6 + t % 2, :], [(keysT[:, k, t * P:(t + 1) * P], w_v[:, k, :]) for k in range(2)]).then_inc(v_all_mm, 1)
            pe.wait_ge(v_all_cp, 10)

            def gate_rows(l):
                for n in range(4):
                    pe.wait_ge(dg_made, 4 * l + n + 1)
                    nc.tensor.matmul(bank[:, 6, :], ones[:, :], diag.rearrange("p a b -> p (a b)"), start=True, stop=True).then_inc(dg_mm, 1)
                pe.wait_ge(gb_cp, 4 * l + 4)

            gate_rows(0)

            with pe.Fori(0, HEADS // 2) as i:
                for s in range(2):
                    pe.wait_ge(wq_in[s], i * 32 + 32)
                    steps = [(w_q[s], cqT, a, w, P) for a, w in CHUNKS] + [(w_k[s], keysT, a, w, NOPE) for a, w in ((0, 512), (512, 512), (1024, 256))]
                    for n, (wt, src, a, w, m) in enumerate(steps):
                        if n >= 2:
                            pe.wait_ge(pj_q if n < 5 else pj_k, i * 6 + (3 * s + (n - 1 if n < 5 else 1)))
                        last = product(bank[0:m, 6 + n % 2, 0:w], [(wt[:, k, 0:m], src[:, k, a:a + w]) for k in range(2)])
                        last.then_inc(pj_mm, 1)
                    pe.wait_ge(pj_k, i * 6 + 3 * (s + 1))
                    if s:
                        pe.wait_ge(o_cp, i * 18 + 9)

                    def scores(t):
                        if t >= 2:
                            pe.wait_ge(o_cp, i * 18 + (9 * s + t - 1))
                        b0 = 3 * (t % 2)
                        q = qT[s][0:QK, t * P:(t + 1) * P]
                        if t < PROMPT:
                            for n in range(3):
                                last = nc.tensor.matmul(bank[:, b0 + n, 0:KS3], q, kT[s][0:QK, n * KS3:(n + 1) * KS3], start=True, stop=True)
                        else:
                            last = nc.tensor.matmul(bank[:, b0, 0:P], q, kT[s][0:QK, KEYS:ALLKEYS], start=True, stop=True)
                        last.then_inc(s_mm, 1)

                    scores(0)
                    for t in range(NT):
                        if t + 1 < NT:
                            scores(t + 1)
                        pe.wait_ge(s_exp, i * 18 + (9 * s + t + 1))
                        parts = ((0, 4), (4, 4), (8, 1)) if t < PROMPT else ((0, 1),)
                        for n, (a, m) in enumerate(parts):
                            u = 8 * s + t
                            if n == 2:
                                pe.wait_ge(pt_cp[0], i * 18 + (9 * s + t + 1))
                            elif t > 0:
                                pe.wait_ge(pt_cp[(2, 1)[n]], i * 16 + u)
                            for m_ in range(m):
                                last = nc.tensor.transpose(bank[:, 6 + n % 2, m_ * P:(m_ + 1) * P], px[t % 2][:, (a + m_) * P:(a + m_ + 1) * P], ident[:, :])
                            last.then_inc(pt_mm[n], 1)
                        pe.wait_ge(pt_cp[0], i * 18 + (9 * s + t + 1))
                        o = bank[:, 3 * (t % 2) + 2, KS3:KS3 + VD]
                        v0 = i * (2 * VD) + s * VD
                        if t < PROMPT:
                            for kt in range(9):
                                if kt == 4:
                                    pe.wait_ge(pt_cp[1], i * 16 + (u + 1))
                                if kt == 8:
                                    pe.wait_ge(pt_cp[2], i * 16 + (u + 1))
                                last = nc.tensor.matmul(o, pT[t % 2][:, kt, :], vall[:, kt, bass.ds(v0, VD)], start=(kt == 0), stop=(kt == 8))
                        else:
                            last = nc.tensor.matmul(o, pT[t % 2][:, 0, :], vall[:, 9, bass.ds(v0, VD)], start=True, stop=True)
                        last.then_inc(o_mm, 1)
                pe.wait_ge(o_cp, i * 18 + 18)
                for n, (a, w) in enumerate(CHUNKS):
                    if n == 2:
                        pe.wait_ge(ot_cp, i * 3 + 1)
                    for m_ in range(w // P):
                        last = nc.tensor.transpose(bank[:, 6 + n % 2, m_ * P:(m_ + 1) * P], opair[:, 4 * n + m_, :], ident[:, :])
                    last.then_inc(ot_mm, 1)
                pe.wait_ge(ot_cp, i * 3 + 3)

            def out_product(l, act_T, w_o, w_sem):
                pe.wait_ge(w_sem, 16)
                for t in range(NT):
                    if t >= 2:
                        pe.wait_ge(g_add, NT * l + t - 1)
                    for j in range(2):
                        last = product(bank[:, 2 * (t % 2) + j, :], [(act_T[:, k, t * P:(t + 1) * P], w_o[:, k, j * 512:(j + 1) * 512]) for k in range(KT)])
                    last.then_inc(g_mm, 1)

            out_product(0, yT, w_oe, woe_in)
            pe.wait_ge(g_add, NT)
            gate_rows(1)
            layer_input_T(1, xnH)
            pe.wait_ge(h_act, 24)
            pe.wait_ge(h_dve, 24)

            pe.wait_ge(tl_in, 48)
            pe.sem_inc(gt_cp, 1)
            pe.sem_inc(y_done, 1)
            with pe.Fori(0, GROUPS) as g:
                pe.wait_ge(fw_in, g * 16 + 16)
                pe.wait_ge(y_done, g + 1)
                for q in range(2):
                    last = nc.tensor.matmul(bank[:, 7, q * P:(q + 1) * P], cg[:, q * P:(q + 1) * P], fw[:, :], start=True, stop=True)
                last.then_inc(csw_mm, 1)
                pe.wait_ge(ow_in[0], g * 16 + 16)
                for n, (a, w) in enumerate(CHUNKS):
                    last = product(bank[:, n, 0:w], [(wr[0][:, k, :], hT[:, k, a:a + w]) for k in range(KT)])
                last.then_inc(u_mm, 1)
                pe.wait_ge(ow_in[1], g * 16 + 16)
                pe.wait_ge(gt_cp, g + 1)
                for n, (a, w) in enumerate(CHUNKS):
                    last = product(bank[:, 3 + n, 0:w], [(wr[1][:, k, :], hT[:, k, a:a + w]) for k in range(KT)])
                last.then_inc(gt_mm, 1)
                pe.wait_ge(u_cp, g + 1)
                pe.wait_ge(csw_cp, g + 1)
                for n in range(5):
                    if n >= 2:
                        pe.wait_ge(*((ab_e, g * 3 + n // 2) if n % 2 == 0 else (ab_o, g * 2 + 1)))
                    for m_ in range(2 if n < 4 else 1):
                        t = 2 * n + m_
                        if t < PROMPT:
                            odd, q = divmod(t, NK)
                            lhs = uT[:, 2 * P * q + odd:2 * P * (q + 1):2]
                        else:
                            lhs = uT[:, LS:TOK]
                        last = nc.tensor.matmul(bank[:, 6 + n % 2, m_ * 256:(m_ + 1) * 256], lhs, csw[:, :], start=True, stop=True)
                    last.then_inc(ab_mm, 1)
                pe.wait_ge(ab_e, g * 3 + 3)
                pe.wait_ge(ab_o, g * 2 + 2)
                for q in range(4):
                    product(bank[:, (0, 1, 2, 6)[q], 0:FQ], [(ab[:, n + NK * (q // 2), (q % 2) * P:(q % 2 + 1) * P], tl[:, n, q, :]) for n in range(NK)])
                product(bank[:, 7, 0:P], [(ab[:, PROMPT, q * P:(q + 1) * P], tlp[:, q, :]) for q in range(2)]).then_inc(y_mm, 1)

            pe.wait_ge(y_done, GROUPS + 1)
            out_product(1, y1T, w_oo, woo_in)

        @block.scalar
        def _(act):
            act.wait_ge(vec_T, 1)
            nc.scalar.activation(cond.rearrange("p k g -> p g k"), split(bank[:, 7, P:P + 16], 2), ACT.Silu).then_inc(cond_made, 1)

            def squares(l, src, ready):
                for t in range(NT):
                    ready(t)
                    if t >= 2:
                        act.wait_ge(x_sq, NT * l + t - 1)
                    nc.scalar.activation(junk[t % 2], src[:, t, :], ACT.Square, accum_out=ssq[:, NT * l + t:NT * l + t + 1]).then_inc(x_sq, 1)

            def layer_input(l):
                for e in range(0, 24, 2):
                    ch, k = divmod(e, KT)
                    a, w = CHUNKS[ch]
                    grp = ch // 2
                    act.wait_ge(x_T, 24 * l + e + 1)
                    nc.scalar.activation(hT[:, k, a:a + w], bank[:, 1 + e % 6, 0:w], ACT.Identity, scale=gsc[:, 8 * l + k, grp:grp + 1],
                                         bias=modc[:, 24 * l + k, grp:grp + 1]).then_inc(h_act, 1)

            squares(0, xs, lambda t: act.wait_ge(x_in[t], 16))
            act.wait_ge(mod_made, 2)
            layer_input(0)
            act.wait_ge(l_T, 1)
            nc.scalar.copy(keysT[:, :, 0:P], split(bank[:, 6, 0:2 * P], 2)).then_inc(l_cp, 1)
            for t in range(NT + 1):
                if t < NT:
                    act.wait_ge(l_mm, t + 1)
                    if t:
                        act.wait_ge(l_sq, t)
                    for j in range(2):
                        last = nc.scalar.activation(junk[j][:, 0:RANK], bank[:, 2 * (t % 2) + j, 0:RANK], ACT.Square,
                                                    accum_out=ssq2[:, 2 * t + j:2 * t + j + 1])
                    last.then_inc(l_sq, 1)
                if t:
                    act.wait_ge(l_T, t + 1)
                    src = bank[:, 4 + (t - 1) % 2, :].rearrange("p (a k n) -> p a k n", a=2, k=2)
                    nc.scalar.copy(cqT[:, :, (t - 1) * P:t * P], src[:, 0])
                    nc.scalar.copy(keysT[:, :, t * P:(t + 1) * P], src[:, 1]).then_inc(l_cp, 1)
            act.wait_ge(kr_T, 1)
            nc.scalar.copy(kT[0][64:96, :], bank[0:ROPE, 0:3, :].rearrange("p a n -> p (a n)")[:, 0:ALLKEYS])
            nc.scalar.copy(kT[1][64:96, :], bank[0:ROPE, 0:3, :].rearrange("p a n -> p (a n)")[:, 0:ALLKEYS]).then_inc(kr_cp, 1)

            def spill(c, ready, n, buf, dst, s):
                act.wait_ge(ready, c + n)
                act.dma_start(T[dst][bass.ds(c, 1)].rearrange("a p n -> p a n"), buf.unsqueeze(1)).then_inc(s, 16)

            for s in (sp_v, sp_x, sp_g):
                act.sem_inc(s, 16)
            with act.Fori(0, CA) as c:
                for j, (dst, m0) in enumerate(((u1, 4), (vt, 8), (x0, 0))):
                    act.wait_ge(d_mm[j], c + 1)
                    if j == 1:
                        act.wait_ge(sp_v, c * 16 + 16)
                    if j == 2:
                        act.wait_ge(sp_x, c * 16 + 16)
                    nc.scalar.activation(dst, banks(3 * (j % 2), 3, 0, TOK), ACT.Identity, scale=col[:, bass.ds(c + (R_CW + 12 + m0), 1)],
                                         bias=col[:, bass.ds(c + (R_CB + m0), 1)]).then_inc(d_mid[j], 1)
                for odd in range(2):
                    act.wait_ge((v_T6, v_T7)[odd], c * (2 - odd) + 1)
                    nc.scalar.copy(vtm[:, NK * odd:NK * (odd + 1), bass.ds(c * P, P)], split(bank[:, 6 + odd, :], NK)).then_inc((v_rel6, v_rel7)[odd], 1)
                act.wait_ge(v_T6, c * 2 + 2)
                nc.scalar.copy(vtm[:, PROMPT, bass.ds(c * P, P)], bank[:, 6, 0:P]).then_inc(v_rel6, 1)
                spill(c, v_ready, 1, vt, "sp_v", sp_v)
                act.wait_ge(d_mm[3], c + 1)
                nc.scalar.activation(ga, banks(3, 3, 0, TOK), ACT.Silu).then_inc(d_rel[3], 1)
                act.wait_ge(d_mm[4], c + 1)
                act.wait_ge(sp_g, c * 16 + 16)
                nc.scalar.activation(gb, banks(0, 3, 0, TOK), ACT.Silu).then_inc(d_rel[4], 1)
                spill(c, xg_ready, 1, x0, "sp_x", sp_x)
                spill(c, d_rel[4], 2, gb, "sp_g", sp_g)

            for n in range(2):
                act.wait_ge(f_red, n + 1)
                nc.scalar.activation(f_z[0:FO, :], f_x[0:FO, :], ACT.Sin).then_inc(f_sin, 1)
            act.wait_ge(sp_x, 16 * (CA + 1))
            act.wait_ge(sp_g, 16 * (CA + 1))
            for t in range(NT):
                act.wait_ge(fh_made, t + 1)
                if t >= 2:
                    act.wait_ge(fh_abs, t - 1)
                nc.scalar.activation(f_mag[t % 2], f_h[t % 2], ACT.Abs).then_inc(fh_mag, 1)
            for kt in range(NK):
                act.wait_ge(k_mm, kt + 1)
                if kt:
                    act.wait_ge(z_made, kt)
                else:
                    act.wait_ge(sd_made, NT)
                nc.scalar.copy(ks, bank[:, 0:4, :]).then_inc(k_cp, 1)
                act.wait_ge(v_mm, kt + 1)
                nc.scalar.copy(vs, bank[:, 4:8, :]).then_inc(v_cp, 1)
            act.wait_ge(k_mm, NK + 1)
            act.wait_ge(z_made, NK)
            nc.scalar.copy(ks[:, 0:2, :], bank[:, 0:2, :])
            nc.scalar.copy(vs[:, 0:2, :], bank[:, 2:4, :]).then_inc(k_cp, 1)

            for t in range(10):
                act.wait_ge(v_all_mm, t + 1)
                nc.scalar.copy(vall[:, t, :], bank[:, 6 + t % 2, :]).then_inc(v_all_cp, 1)
            with act.Fori(0, HEADS // 2) as i:
                for s in range(2):
                    for n, (a, w) in enumerate(((0, 512), (512, 512), (1024, 256))):
                        act.wait_ge(pj_mm, i * 12 + (6 * s + 4 + n))
                        nc.scalar.copy(kT[s][0:NOPE, a:a + w], bank[0:NOPE, 6 + (n + 1) % 2, 0:w]).then_inc(pj_k, 1)

                    def exps(t):
                        act.wait_ge(s_max, i * 18 + (9 * s + t + 1))
                        b0 = 3 * (t % 2)
                        src, dst = (bank[:, b0:b0 + 3, 0:KS3], split(px[t % 2], 3)) if t < PROMPT else (bank[:, b0, 0:P], px[t % 2][:, 0:P])
                        nc.scalar.activation(dst, src, ACT.Exp, scale=SCALE, bias=nmax[:, t % 2:t % 2 + 1],
                                             accum_out=rsum[:, t % 2:t % 2 + 1]).then_inc(s_exp, 1)

                    exps(0)
                    for t in range(NT):
                        act.wait_ge(pt_mm[0], i * 18 + (9 * s + t + 1))
                        nt = 4 if t < PROMPT else 1
                        nc.scalar.copy(pT[t % 2][:, 0:nt, :], split(bank[:, 6, 0:nt * P], nt)).then_inc(pt_cp[0], 1)
                        if t < PROMPT:
                            act.wait_ge(pt_mm[2], i * 16 + (8 * s + t + 1))
                            nc.scalar.copy(pT[t % 2][:, 8, :], bank[:, 6, 0:P]).then_inc(pt_cp[2], 1)
                        if t + 1 < NT:
                            exps(t + 1)

            squares(1, xs, lambda t: act.wait_ge(g_add, t + 1))
            layer_input(1)
            with act.Fori(0, GROUPS) as g:
                act.wait_ge(csw_mm, g + 1)
                nc.scalar.copy(csw[:, :], bank[:, 7, 0:256]).then_inc(csw_cp, 1)
                act.wait_ge(u_mm, g + 1)
                nc.scalar.copy(uT, banks(0, 3, 0, TOK)).then_inc(u_cp, 1)
                act.wait_ge(gt_mm, g + 1)
                nc.scalar.activation(sg, banks(3, 3, 0, TOK), ACT.Silu).then_inc(gt_cp, 1)
                for n in (1, 3):
                    act.wait_ge(ab_mm, g * 5 + (n + 1))
                    nc.scalar.copy(ab[:, 2 * n:2 * n + 2, :], split(bank[:, 7, :], 2)).then_inc(ab_o, 1)
                act.wait_ge(y_mm, g + 1)
                nc.scalar.copy(cd[:, 0, :], bank[:, 2, 0:FQ])
                nc.scalar.copy(cd[:, 1, :], bank[:, 6, 0:FQ]).then_inc(cd_cp, 1)

            squares(2, xs, lambda t: act.wait_ge(g_add, NT + t + 1))

        @block.vector
        def _(dve):
            link = Chain(dve, dve_done)
            tscal, stt, tt_ = nc.vector.tensor_scalar, nc.vector.scalar_tensor_tensor, nc.vector.tensor_tensor
            dve.wait_ge(vec_T, 1)
            dve.wait_ge(cond_made, 1)
            link(nc.vector.tensor_copy(col[:, :], bank[:, 7, 0:R_ALL]))
            dve.wait_ge(wm_used[1], 6)
            nc.vector.tensor_tensor(modc, split(bank[:, 0, 0:96], 48), col[:, R_BMOD:R_BMOD + 48].unsqueeze(2).broadcast_to([P, 48, 2]),
                                    ALU.add).then_inc(mod_made, 1)
            dve.wait_ge(mod_made, 1)
            for l in range(2):
                last = stt(gsc[:, 8 * l:8 * l + 8, :], modc[:, 24 * l + 8:24 * l + 16, :], 1.0,
                           col[:, R_NG + 8 * l:R_NG + 8 * l + 8].unsqueeze(2).broadcast_to([P, KT, 2]), ALU.add, ALU.mult)
            last.then_inc(mod_made, 1)

            def normalise(l, dst, src):
                for t in range(NT):
                    dve.wait_ge(x_rs, NT * l + t + 1)
                    tscal(dst[:, t, :], src[:, t, :], rstd[:, NT * l + t:NT * l + t + 1], None, ALU.mult).then_inc(x_n, 1)

            def layer_input(l):
                for e in range(1, 24, 2):
                    ch, k = divmod(e, KT)
                    a, w = CHUNKS[ch]
                    grp = ch // 2
                    dve.wait_ge(x_T, 24 * l + e + 1)
                    tscal(hT[:, k, a:a + w], bank[:, 1 + e % 6, 0:w], gsc[:, 8 * l + k, grp:grp + 1], modc[:, 24 * l + k, grp:grp + 1],
                          ALU.mult, ALU.add).then_inc(h_dve, 1)

            normalise(0, xs, xs)
            dve.wait_ge(mod_made, 2)
            layer_input(0)
            dve.wait_ge(small_in, 16 * 5)
            for t in range(NT):
                dve.wait_ge(l_rs, t + 1)
                if t >= 2:
                    dve.wait_ge(l_T, t)
                b = 2 * (t % 2)
                nc.vector.tensor_copy(kro[:, 1 + t, :], bank[:, b + 1, RANK:RANK + ROPE])
                for j in range(2):
                    last = stt(lat[t % 2][:, j * RANK:(j + 1) * RANK], bank[:, b + j, 0:RANK], rstd2[:, 2 * t + j:2 * t + j + 1],
                               lat_g[:, j * RANK:(j + 1) * RANK], ALU.mult, ALU.mult)
                last.then_inc(l_lat, 1)
            dve.wait_ge(l_lat, NT)
            swap = lambda a: a.rearrange("p t (x h f) -> p (t x) h f", x=2, h=2)
            for h in range(2):
                last = nc.vector.tensor_copy(swap(krs)[:, :, h, :], swap(kro[:, 1:9, :])[:, :, 1 - h, :])
            link(last)
            rt = lambda n: rope_t[:, n, :].rearrange("p (t f) -> p t f", t=8)
            nc.vector.tensor_copy(krr[:, 0, :], kro[:, 0, :])
            nc.vector.tensor_copy(krr[:, 9, :], kro[:, 9, :])
            tt_(krr[:, 1:9, :], kro[:, 1:9, :], rt(0), ALU.mult)
            link(tt_(krs, krs, rt(1), ALU.mult))
            tt_(krr[:, 1:9, :], krr[:, 1:9, :], krs, ALU.add).then_inc(kr_rot, 1)

            with dve.Fori(0, CA) as c:
                link.loop(c, 3)
                for j, (dst, m0) in enumerate(((u1, 4), (vt, 8), (x0, 0))):
                    dve.wait_ge(d_mid[j], c + 1)
                    ps = banks(3 * (j % 2), 3, 0, TOK)
                    for n, (a, b) in enumerate(((0, LS), (LS, TOK))):
                        last = stt(dst[:, a + 1:b], ps[:, a:b - 1], col[:, bass.ds(c + (R_CW + m0), 1)], dst[:, a + 1:b], ALU.mult, ALU.add)
                    link(last)
                    for n, (a, b) in enumerate(((0, LS), (LS, TOK))):
                        last = stt(dst[:, a:b - 1], ps[:, a + 1:b], col[:, bass.ds(c + (R_CW + 24 + m0), 1)], dst[:, a:b - 1], ALU.mult, ALU.add)
                    last.then_inc(d_rel[j], 1)
                    if j == 1:
                        dve.wait_ge(d_rel[1], c + 1)
                        tt_(vt, vt, u1, ALU.mult).then_inc(v_ready, 1)
                dve.wait_ge(d_rel[2], c + 1)
                dve.wait_ge(d_rel[3], c + 2)
                tt_(x0, x0, ga, ALU.mult).then_inc(xg_ready, 1)
            link.end(CA)

            for n in range(2):
                dve.wait_ge(f_mm, n + 1)
                link(tscal(f_x[0:FO, :], bank[0:FO, 0:3, :].rearrange("p a n -> p (a n)")[:, 0:TOK], fb[0:FO, n:n + 1], None, ALU.add))
                link(tscal(f_r[0:FO, :], f_x[0:FO, :], 1.0 / (2 * math.pi), MAGIC, ALU.mult, ALU.add))
                link(tscal(f_r[0:FO, :], f_r[0:FO, :], MAGIC, None, ALU.subtract))
                link(stt(f_x[0:FO, :], f_r[0:FO, :], -TWO_PI_HI, f_x[0:FO, :], ALU.mult, ALU.add))
                link(stt(f_x[0:FO, :], f_r[0:FO, :], -TWO_PI_LO, f_x[0:FO, :], ALU.mult, ALU.add))
                tscal(f_x[0:FO, :], f_x[0:FO, :], PI_IN, -PI_IN, ALU.min, ALU.max).then_inc(f_red, 1)
            dve.wait_ge(sp_v, 16 * (CA + 1))
            dve.wait_ge(sp_x, 16 * (CA + 1))
            link(nc.vector.memset(f_abs, 0.0))
            dve.wait_ge(dec_in, 16)
            for t in range(NT):
                w = int(t == PROMPT)
                dve.wait_ge(fh_mm, t + 1)
                if t >= 2:
                    dve.wait_ge(sd_made, t - 1)
                b = 2 * (t % 3)
                tt_(f_h[t % 2][:, 0, :], bank[:, b, :], decay[:, t, :], ALU.mult)
                link_made = tt_(f_h[t % 2][:, 1, :], bank[:, b + 1, :], decay[:, t, :], ALU.mult)
                link_made.then_inc(fh_made, 1)
                dve.wait_ge(fh_mag, t + 1)
                link(tt_(f_abs[:, w, :], f_mag[t % 2][:, 0, :], f_abs[:, w, :], ALU.add))
                last = tt_(f_abs[:, w, :], f_mag[t % 2][:, 1, :], f_abs[:, w, :], ALU.add)
                if t in (0, PROMPT):
                    link(last)
                    last = nc.vector.memset(f_h[t % 2][0:1, 1, :], 0.0)
                last.then_inc(fh_abs, 1)
                dve.wait_ge(fh_abs, t + 1)
            dve.wait_ge(nrm_mm, 1)
            nc.vector.reciprocal(rnorm[:, :], bank[:, 6, 0:2 * CA]).then_inc(nrm_made, 1)

            for kt in range(NK):
                dve.wait_ge(v_cp, kt + 1)
                tt_(vp[:, 0:2, :], vs[:, 0:2, :], vs[:, 2:4, :], ALU.add)
                link(tt_(vp[:, 2:4, :], vs[:, 0:2, :], vs[:, 2:4, :], ALU.subtract))
                dve.wait_ge(kp_made, kt + 1)
                four = lambda a: a.rearrange("p (s r) n -> p s r n", s=2)
                tt_(ks, vp, kp, ALU.mult)
                link(tt_(four(vs), four(vp), four(kp)[:, :, ::-1, :], ALU.mult))
                tt_(kp[:, 0:2, :], four(ks)[:, :, 0, :], four(ks)[:, :, 1, :], ALU.subtract)
                link(tt_(kp[:, 2:4, :], four(vs)[:, :, 0, :], four(vs)[:, :, 1, :], ALU.add))
                tt_(zz[:, kt, 0:2, :], kp[:, 0::2, :], kp[:, 1::2, :], ALU.add)
                tt_(zz[:, kt, 2:4, :], kp[:, 0::2, :], kp[:, 1::2, :], ALU.subtract).then_inc(z_made, 1)
            dve.wait_ge(k_cp, NK + 1)
            dve.wait_ge(z_made, NK)
            tt_(kp[:, 0:2, :], vs[:, 0:2, :], ks[:, 0:2, :], ALU.mult)
            link(tt_(kp[:, 2:4, :], vs[:, 0:2, :], ks[:, 1::-1, :], ALU.mult))
            tt_(yp[:, 0, :], kp[:, 0, :], kp[:, 1, :], ALU.subtract)
            tt_(yp[:, 1, :], kp[:, 2, :], kp[:, 3, :], ALU.add).then_inc(z_made, 1)

            for c in range(CA):
                s = c % 2
                vf = vf_in[s]
                dve.wait_ge(vf_in_s[s], 16 * (c // 2 + 1))
                dve.wait_ge(xg_in_s[s], 16 * (c // 2 + 1))
                link(tscal(vf, vf, col[:, R_SKIP + c:R_SKIP + c + 1], None, ALU.mult))
                dve.wait_ge(i_mm, c + 1)
                for odd in range(2):
                    stt(vf[:, odd:LS:2], bank[:, 3 * s + odd, :], rnorm[:, c:c + 1], vf[:, odd:LS:2], ALU.mult, ALU.add)
                link(stt(vf[:, LS:TOK], bank[:, 3 * s + 2, 0:P], rnorm[:, CA + c:CA + c + 1], vf[:, LS:TOK], ALU.mult, ALU.add))
                tt_(yT[:, c, :], vf, xg_in[s], ALU.mult).then_inc(i_done, 1)

            def gate_rows(l):
                for n in range(4):
                    grp, h = divmod(n, 2)
                    if n:
                        dve.wait_ge(dg_mm, 4 * l + n)
                    for a in range(4):
                        last = tscal(diag[:, a, :], ident[:, :], modc[:, 24 * l + 16 + 4 * h + a, grp:grp + 1], None, ALU.mult)
                    last.then_inc(dg_made, 1)
                    dve.wait_ge(dg_mm, 4 * l + n + 1)
                    nc.vector.tensor_copy(gateb[:, grp, h * 512:(h + 1) * 512], bank[:, 6, :]).then_inc(gb_cp, 1)

            dve.wait_ge(i_done, CA)
            gate_rows(0)

            with dve.Fori(0, HEADS // 2) as i:
                link.loop(i, 4 + 2 * NT * 2)
                for s in range(2):
                    for n, (a, w) in enumerate(CHUNKS):
                        dve.wait_ge(pj_mm, i * 12 + (6 * s + 1 + n))
                        b = 6 + n % 2
                        if n < 2:
                            if n:
                                dve.wait_ge(pj_q, i * 6 + (3 * s + 1))
                            nc.vector.tensor_copy(qT[s][0:NOPE, a:a + w], bank[0:NOPE, b, 0:w])
                            tt_(qT[s][64:96, a:a + w], bank[64:96, b, 0:w], rope_q[64:96, a:a + w], ALU.mult)
                            link(tt_(rtmp[64:96, 0:w], bank[96:128, b, 0:w], rope_q[96:128, a:a + w], ALU.mult))
                            tt_(qT[s][64:96, a:a + w], qT[s][64:96, a:a + w], rtmp[64:96, 0:w], ALU.add).then_inc(pj_q, 1)
                        else:
                            nc.vector.tensor_copy(qT[s][0:QK, a:a + w], bank[0:QK, b, 0:w]).then_inc(pj_q, 1)

                    def maxima(t):
                        dve.wait_ge(s_mm, i * 18 + (9 * s + t + 1))
                        b0, m = 3 * (t % 2), t % 2
                        src = bank[:, b0:b0 + 3, 0:KS3] if t < PROMPT else bank[:, b0, 0:P]
                        link(nc.vector.tensor_reduce(amax[:, m:m + 1], src, mybir.AxisListType.XY if t < PROMPT else mybir.AxisListType.X, ALU.max))
                        tscal(nmax[:, m:m + 1], amax[:, m:m + 1], -SCALE, None, ALU.mult).then_inc(s_max, 1)

                    maxima(0)
                    for t in range(NT):
                        if t < PROMPT:
                            dve.wait_ge(pt_mm[1], i * 16 + (8 * s + t + 1))
                            nc.vector.tensor_copy(pT[t % 2][:, 4:8, :], split(bank[:, 7, :], 4)).then_inc(pt_cp[1], 1)
                        if t + 1 < NT:
                            maxima(t + 1)
                        m = t % 2
                        dve.wait_ge(s_exp, i * 18 + (9 * s + t + 1))
                        link(nc.vector.reciprocal(rinv[:, m:m + 1], rsum[:, m:m + 1]))
                        dve.wait_ge(o_mm, i * 18 + (9 * s + t + 1))
                        tscal(opair[:, t, s * VD:(s + 1) * VD], bank[:, 3 * m + 2, KS3:KS3 + VD], rinv[:, m:m + 1], None, ALU.mult).then_inc(o_cp, 1)
                dve.wait_ge(sg_in, i * 16 + 16)
                for n, (a, w) in enumerate(CHUNKS):
                    dve.wait_ge(ot_mm, i * 3 + (n + 1))
                    tt_(yT[:, bass.ds(i + CA, 1), a:a + w].rearrange("p a n -> p (a n)"), bank[:, 6 + n % 2, 0:w], sgate[:, a:a + w], ALU.mult).then_inc(ot_cp, 1)
            link.end(HEADS // 2)

            def residual(l):
                for t in range(NT):
                    grp = int(t == PROMPT)
                    if l == 0:
                        dve.wait_ge(x_in[t], 32)
                    dve.wait_ge(g_mm, NT * l + t + 1)
                    b = 2 * (t % 2)
                    gy = resid_tmp(t)
                    link(tt_(split(gy, 2), bank[:, b:b + 2, :], split(gateb[:, grp, :], 2), ALU.mult))
                    tt_(xs[:, t, :], xs[:, t, :], gy, ALU.add).then_inc(g_add, 1)

            resid_tmp = lambda t: VR[:, 2048 + 1024 * (t % 2):3072 + 1024 * (t % 2)]
            residual(0)
            dve.wait_ge(g_add, NT)
            gate_rows(1)
            normalise(1, xnH, xs)
            layer_input(1)

            with dve.Fori(0, GROUPS) as g:
                link.loop(g, 2)
                for n in (0, 2, 4):
                    dve.wait_ge(ab_mm, g * 5 + (n + 1))
                    w = 2 if n < 4 else 1
                    nc.vector.tensor_copy(ab[:, 2 * n:2 * n + w, :], split(bank[:, 6, 0:256 * w], w)).then_inc(ab_e, 1)
                dve.wait_ge(cd_cp, g + 1)
                for q in range(2):
                    tt_(tt[:, 2 * q, :], bank[:, q, 0:FQ], cd[:, q, :], ALU.add)
                    last = tt_(tt[:, 2 * q + 1, :], bank[:, q, 0:FQ], cd[:, q, :], ALU.subtract)
                link(last)
                n = HALF // 2
                tt_(yt[:, 0:n + 1], tt[:, 0, 0:n + 1], tt[:, 2, 0:n + 1], ALU.add)
                tt_(yt[:, 2 * n:n:-1], tt[:, 1, 0:n], tt[:, 3, 0:n], ALU.subtract)
                tt_(yt[:, 2 * n + 1:3 * n + 1], tt[:, 1, 1:n + 1], tt[:, 3, 1:n + 1], ALU.add)
                link(tt_(yt[:, 4 * n - 1:3 * n:-1], tt[:, 0, 1:n], tt[:, 2, 1:n], ALU.subtract))
                tt_(y1T[:, bass.ds(g, 1), 0:LS].rearrange("p a n -> p (a n)"), yt[:, 0:LS], sg[:, 0:LS], ALU.mult)
                tt_(y1T[:, bass.ds(g, 1), LS:TOK].rearrange("p a n -> p (a n)"), bank[:, 7, 0:P], sg[:, LS:TOK], ALU.mult).then_inc(y_done, 1)
            link.end(GROUPS)

            residual(1)
            dve.wait_ge(fg_in, 16)
            for t in range(NT):
                dve.wait_ge(x_rs, 2 * NT + t + 1)
                stt(xs[:, t, :], xs[:, t, :], rstd[:, 2 * NT + t:2 * NT + t + 1], fgb, ALU.mult, ALU.mult).then_inc(out_ready, 1)

        @block.gpsimd
        def _(pool):
            link = Chain(pool, pool_done)
            link(nc.gpsimd.memset(ident[:, :], 0.0))
            nc.gpsimd.affine_select(out=ident[:, :], in_=ident[:, :], compare_op=ALU.not_equal, fill=1.0, base=0,
                                    pattern=[[-1, P]], channel_multiplier=1).then_inc(consts_made, 1)
            nc.gpsimd.memset(ones[:, :], 1.0).then_inc(consts_made, 1)
            nc.gpsimd.memset(half_neg[:, :], -0.5).then_inc(consts_made, 1)
            pool.wait_ge(consts_made, 3)

            def inverse_root(dst, src, n, width):
                link(nc.gpsimd.tensor_scalar(src, src, 1.0 / n, EPS, ALU.mult, ALU.add))
                return nc.gpsimd.tensor_tensor(dst, src, half_neg[:, 0:width], ALU.pow)

            def row_norms(l):
                for t in range(NT):
                    a = NT * l + t
                    pool.wait_ge(x_sq, a + 1)
                    inverse_root(rstd[:, a:a + 1], ssq[:, a:a + 1], D, 1).then_inc(x_rs, 1)

            row_norms(0)
            for t in range(NT):
                pool.wait_ge(l_sq, t + 1)
                inverse_root(rstd2[:, 2 * t:2 * t + 2], ssq2[:, 2 * t:2 * t + 2], RANK, 2).then_inc(l_rs, 1)
            for t in range(NT):
                pool.wait_ge(fh_abs, t + 1)
                nc.gpsimd.tensor_tensor(sd[:, t, 0, :], f_h[t % 2][:, 0, :], f_h[t % 2][:, 1, :], ALU.add)
                nc.gpsimd.tensor_tensor(sd[:, t, 1, :], f_h[t % 2][:, 0, :], f_h[t % 2][:, 1, :], ALU.subtract).then_inc(sd_made, 1)
            pool.wait_ge(sp_g, 16 * (CA + 1))
            for kt in range(NK):
                pool.wait_ge(k_cp, kt + 1)
                nc.gpsimd.tensor_tensor(kp[:, 0:2, :], ks[:, 0:2, :], ks[:, 2:4, :], ALU.add)
                nc.gpsimd.tensor_tensor(kp[:, 2:4, :], ks[:, 0:2, :], ks[:, 2:4, :], ALU.subtract).then_inc(kp_made, 1)
            row_norms(1)
            row_norms(2)


def tables():
    f = np.float32
    out = {}

    def positions(L):
        n = np.arange(L)
        t = np.linspace(0.0, 1.0, L)[:, None]
        w = 2 * math.pi * n[:, None] / L
        fr = np.linspace(1e-4, BANDS - 1, BANDS)[None, :]
        z = np.concatenate([t, np.cos(fr * w), -np.sin(fr * w)], axis=-1)
        lo, hi = math.log(1e-2) / 1.5, math.log(1e-2) / 0.3
        return z, np.exp(-t * np.abs(np.linspace(lo, hi, DA)))

    zs, ds = positions(LS)
    zp, dp = positions(LP)
    z = np.concatenate([zs[0::2], zs[1::2], zp])
    dec = np.concatenate([ds[0::2], ds[1::2], dp])
    out["zT"] = z.T.astype(f)
    out["decay"] = dec.reshape(NT, P, DA).transpose(1, 0, 2).astype(f)
    k = np.arange(HALF)
    par = [np.arange(0, LS, 2), np.arange(1, LS, 2)]
    ang = [np.outer(n, math.pi * (2 * k + 1) / (2 * LS)) for n in par]
    quad = np.stack([np.cos(ang[0]), -np.sin(ang[0]), np.cos(ang[1]), -np.sin(ang[1])])
    out["tf"] = quad.reshape(4, NK, P, NK, P).transpose(3, 2, 0, 1, 4).astype(f)
    out["ti"] = (quad / LS).transpose(2, 0, 1).reshape(NK, P, 4, HALF).transpose(1, 0, 2, 3).astype(f)
    n = np.arange(LP)
    a = np.outer(n, math.pi * (2 * n + 1) / (2 * LP))
    pair = np.stack([np.cos(a), -np.sin(a)])
    out["tp"] = pair.transpose(1, 0, 2).astype(f)
    out["tpi"] = (pair / LP).transpose(2, 0, 1).astype(f)
    t = np.arange(LS)
    inv = 10000.0 ** (-np.arange(0, ROPE // 2, 2) / (ROPE // 2))
    an = np.stack([(t // GRID_W)[:, None] * inv, (t % GRID_W)[:, None] * inv], axis=1)
    cos = np.repeat(np.cos(an)[:, :, None, :], 2, axis=2).reshape(LS, ROPE)
    sin = np.stack([-np.sin(an), np.sin(an)], axis=2).reshape(LS, ROPE)
    both = np.stack([cos, sin])
    out["rope_t"] = both.reshape(2, LS // P, P, ROPE).transpose(2, 0, 1, 3).reshape(P, 2, 256).astype(f)
    out["rope_q"] = both.transpose(0, 2, 1).reshape(2 * ROPE, LS).astype(f)
    kk = np.arange(FQ)
    quad = []
    for nn in par:
        x = 2 * math.pi * np.outer(nn, kk) / LS
        quad += [np.cos(x), -np.sin(x)]
    quad = np.stack(quad) / math.sqrt(LS * P)
    out["tl"] = quad.reshape(4, NK, P, FQ).transpose(2, 1, 0, 3).astype(f)
    x = 2 * math.pi * np.outer(n, n) / P
    out["cg"] = np.concatenate([np.cos(x), np.sin(x)], axis=1).astype(f)
    out["tlp"] = (np.stack([np.cos(x), -np.sin(x)]) / math.sqrt(LP * P)).transpose(1, 0, 2).astype(f)
    return {name: np.ascontiguousarray(v) for name, v in out.items()}


def layout(inputs):
    i = {k: np.asarray(v) for k, v in inputs.items()}
    out = {}
    out["x_sample"], out["x_prompt"] = i["x_sample"][0], i["x_prompt"][0]
    out["vecs"] = np.concatenate([i["b_mod"].reshape(48, P), i["norm_g"].reshape(16, P), i["conv_w"].reshape(36, P),
                                  i["conv_b"].reshape(12, P), i["hyena_skip"].reshape(4, P)])
    out["cond"] = np.concatenate([i["c"].reshape(8, P), i["c_ctx"].reshape(8, P)])
    out["w_mod"] = i["w_mod"].reshape(2, KT, P, 6, 512).transpose(0, 3, 2, 1, 4).reshape(12, P, KT, 512)
    w = i["w_in_e"][0].reshape(KT, P, -1).transpose(1, 0, 2)
    tile = lambda a, n: w[:, :, a:a + n * P].reshape(P, KT, n, P).transpose(2, 0, 1, 3)
    out["w_in"] = np.stack([tile(DA, CA), tile(2 * DA, CA), tile(0, CA), tile(3 * DA, CA), tile(4 * DA + LAT, CA)])
    out["w_lat"] = w[:, :, 4 * DA:4 * DA + LAT]
    out["qg"], out["kvg"], out["final_g"] = i["q_norm_g"][0], i["kv_norm_g"][0], i["final_g"]
    out["cache_ckv"], out["cache_krope"] = i["cache_ckv"][0, 0], i["cache_krope"][0, 0]
    out["f_w1"], out["f_w2"], out["f_w3"] = i["filt_w1"][0], i["filt_w2"][0], i["filt_w3"][0]
    out["f_b"] = np.stack([i["filt_b1"][0], i["filt_b2"][0]], axis=1)
    q = i["w_uq"][0].reshape(RANK, HEADS, QK)
    rope = q[:, :, NOPE:].reshape(RANK, HEADS, 2, 2, 8)[:, :, :, ::-1, :].reshape(RANK, HEADS, ROPE)
    q = np.concatenate([q, rope], axis=2)
    out["w_q"] = q.reshape(2, P, HEADS, P).transpose(2, 1, 0, 3)
    kv = i["w_ukv"][0].reshape(2, P, HEADS, NOPE + VD)
    out["w_k"] = kv[..., 0:NOPE].transpose(2, 1, 0, 3)
    out["w_v"] = kv[..., NOPE:].transpose(1, 0, 2, 3).reshape(P, 2, HEADS * VD)
    out["w_oe"] = i["w_out_e"][0].reshape(KT, P, D).transpose(1, 0, 2)
    out["w_io"] = i["w_in_o"][0].reshape(KT, P, 2, GROUPS, P).transpose(2, 3, 1, 0, 4)
    out["fnet_w"] = i["fnet_w"][0]
    out["w_oo"] = i["w_out_o"][0].reshape(KT, P, D).transpose(1, 0, 2)
    return {name: np.ascontiguousarray(v) for name, v in out.items()}


OUTS = {"y_prompt": (LP, D), "y_sample": (LS, D), "state_ckv": (LP, RANK), "state_krope": (LP, ROPE)}
SPILLS = ("sp_v", "sp_x", "sp_g")


def kernel(**inputs):
    import concourse.bacc as bacc
    from concourse.bass_utils import run_bass_kernel_spmd

    nc = bacc.Bacc("TRN2", target_bir_lowering=False, num_devices=1)
    arrays = {**layout(inputs), **tables()}
    T = {n: nc.dram_tensor(f"{n}_in", a.shape, F32, kind="ExternalInput").ap() for n, a in arrays.items()}
    for n, shape in OUTS.items():
        T[n] = nc.dram_tensor(f"{n}_out", shape, F32, kind="ExternalOutput").ap()
    for n in SPILLS:
        T[n] = nc.dram_tensor(f"{n}_rows", (CA, P, TOK), F32, kind="Internal").ap()
    build(nc, T)
    r = run_bass_kernel_spmd(nc, [{f"{n}_in": a for n, a in arrays.items()}], core_ids=[0]).results[0]
    return (r["y_prompt_out"].reshape(1, LP, D), r["y_sample_out"].reshape(1, LS, D),
            r["state_ckv_out"].reshape(1, 1, LP, RANK), r["state_krope_out"].reshape(1, 1, LP, ROPE))
```

```python
import math
from contextlib import ExitStack

import numpy as np

import concourse.bass as bass
from concourse import mybir

F32 = mybir.dt.float32
F32R = mybir.dt.float32r
ALU = mybir.AluOpType
ACT = mybir.ActivationFunctionType

P = 128
D = 1024
KT = D // P
LS, LP = 1024, 128
TOK = LS + LP
NT = TOK // P
PROMPT = NT - 1
CHUNKS = [(0, 512), (512, 512), (1024, 128)]
T3 = TOK // 3
EPS = 1e-6
DA = 512
CA = DA // P
BANDS = 16
EMB = 2 * BANDS + 1
FO = 64
HEADS, NOPE, ROPE, VD, RANK = 8, 64, 32, 64, 256
QK = NOPE + ROPE
SCALE = 1.0 / math.sqrt(QK)
PAST = 128
KEYS = PAST + LS
ALLKEYS = KEYS + LP
KS3 = KEYS // 3
GRID_W = 64
HALF = LS // 2
NK = HALF // P
GROUPS = 8
FQ = HALF // 2 + 2
LAT = 2 * RANK + ROPE
R_BMOD, R_NG, R_CW, R_CB, R_SKIP, R_ALL = 0, 48, 64, 100, 112, 116
MAGIC = 1.5 * 2.0 ** 23
TWO_PI_HI = 6.28125
TWO_PI_LO = float(np.float32(2 * math.pi - 6.28125))
PI_IN = 3.1415925


def build(nc, T):
    ctx = ExitStack()
    with ctx:
        place = [0]

        def sb(name, width, also_rounded=False):
            base = (nc.sbuf_base + 63) // 64 * 64 + 4 * place[0]
            place[0] += (width + 7) // 8 * 8
            plain = nc.alloc_sbuf_tensor_at(name, [P, width], F32, offset=base)
            return (plain, nc.alloc_sbuf_tensor_at(name + "_r", [P, width], F32R, offset=base)) if also_rounded else plain

        def sem(name):
            return ctx.enter_context(nc.semaphore(name))

        def sems(name, n):
            return [sem(f"{name}{i}") for i in range(n)]

        def split(ap, a):
            return ap.rearrange("p (a b) -> p a b", a=a)

        H, H_r = sb("H", 18432, True)
        H2 = 9216
        SCR, SCR_r = sb("SCR", 9600, True)
        WR, WR_r = sb("WR", 5120, True)
        KV, KV_r = sb("KV", 12544, True)
        WX, WX_r = sb("WX", 1024, True)
        KR_, VR = KV[:, 0:7424], KV[:, 7424:12544]
        bank = ctx.enter_context(nc.psum_tensor("bank", [P, 8, 512], F32))

        def banks(b, n, lo, hi):
            return bank[:, b:b + n, :].rearrange("p a n -> p (a n)")[:, lo:hi]

        ident = sb("ident", P)
        ones = sb("ones", P)
        half_neg = sb("half_neg", 2)
        vec_rows, cond_rows = WX[:, 0:P], WX[:, P:2 * P]
        col = sb("col", R_ALL)
        cond = split(sb("cond", 16)[:, :], KT)
        modc = split(sb("modc", 96)[:, :], 48)
        gsc = split(sb("gsc", 32)[:, :], 16)
        LATS = sb("LATS", 2048)
        lat_g = LATS[:, 0:512]
        lat = [LATS[:, 512 * i:512 * (i + 1)] for i in (1, 2)]
        rope_t = split(LATS[:, 1536:2048], 2)
        rope_q = sb("rope_q", LS)
        kro = split(sb("kro", 10 * ROPE)[:, :], 10)
        krs = split(sb("krs", 8 * ROPE)[:, :], 8)
        krr = split(sb("krr", 10 * ROPE)[:, :], 10)
        fw1 = sb("fw1", FO)
        fw2 = sb("fw2", FO)
        fb = sb("fb", 2)
        fw3 = sb("fw3", 2 * DA)
        tp = split(sb("tp", 2 * P)[:, :], 2)
        tpi = split(sb("tpi", 2 * P)[:, :], 2)
        ssq = sb("ssq", 3 * NT)
        rstd = sb("rstd", 3 * NT)
        ssq2 = sb("ssq2", 2 * NT)
        rstd2 = sb("rstd2", 2 * NT)
        rnorm = sb("rnorm", 2 * CA)
        amax = sb("amax", 2)
        nmax = sb("nmax", 2)
        rsum = sb("rsum", 2)
        rinv = sb("rinv", 2)

        wm = [split(H[:, 4096 * i:4096 * (i + 1)], KT) for i in range(4)]
        mod_rows = KR_[0:2, 0:6 * D]
        hT = [split(H_r[:, a:a + KT * TOK], KT) for a in (0, H2)]
        h_tmp = [KR_[:, 4132 + 512 * i:4644 + 512 * i] for i in range(4)]
        w_lat_raw = split(VR[:, 0:KT * LAT], KT)
        w_lat = [split(WR_r[:, 768:5120], KT), split(KV_r[:, 7424:7424 + KT * LAT], KT)]
        sd = H[:, 0:NT * 2 * DA].rearrange("p (t s n) -> p t s n", t=NT, s=2)
        zz = H[:, H2:H2 + NK * 4 * DA].rearrange("p (k q n) -> p k q n", k=NK, q=4)
        yT = split(H[:, 0:KT * TOK], KT)
        y1T = split(SCR[:, 0:KT * TOK], KT)
        wo_raw = [split(H[:, a:a + KT * D], KT) for a in (H2, 0)]
        wo = [[split(KV_r[:, 0:KT * D], KT), split(H_r[:, H2:H2 + KT * D], KT)],
              [split(H_r[:, KT * D:2 * KT * D], KT), split(H_r[:, 0:KT * D], KT)]]
        y_in = [yT, y1T]
        y_sl = [[[split(m[:, a + 2048 * i + 1024 * j:a + 2048 * i + 1024 * (j + 1)], KT) for j in range(2)] for i in range(2)]
                for m, a in ((KV_r, KT * D), (WR_r, 0))]

        xs = split(SCR[:, 0:NT * D], NT)
        u1 = SCR[:, 0:TOK]
        vt = SCR[:, TOK:2 * TOK]
        x0 = SCR[:, 2 * TOK:3 * TOK]
        ga = SCR[:, 3 * TOK:4 * TOK]
        gb = SCR[:, 4 * TOK:5 * TOK]
        f_z = KR_[:, 4864:4864 + TOK]
        f_x = KR_[:, 6144:6144 + TOK]
        f_r = SCR[:, 7 * TOK:8 * TOK]
        f_h = [split(SCR[:, 1024 * i:1024 * (i + 1)], 2) for i in range(2)]
        f_abs = split(SCR[:, 2048:3072], 2)
        f_mag = [split(SCR[:, 3072 + 1024 * i:4096 + 1024 * i], 2) for i in range(2)]
        ks = split(SCR[:, 0:2048], 4)
        vs = split(SCR[:, 2048:4096], 4)
        kp = split(SCR[:, 4096:6144], 4)
        vp = split(SCR[:, 6144:8192], 4)
        yp = split(SCR[:, 8192:9216], 2)
        ti = SCR[:, 0:8192].rearrange("p (k q n) -> p k q n", k=NK, q=4)
        qT = [SCR[:, TOK * i:TOK * (i + 1)] for i in range(2)]
        px = [SCR[:, TOK * (2 + i):TOK * (3 + i)] for i in range(2)]
        pT = [split(SCR[:, TOK * (4 + i):TOK * (5 + i)], NT) for i in range(2)]
        sgate = SCR[:, TOK * 6:TOK * 7]
        vpair = split(SCR[:, TOK * 7:TOK * 7 + 10 * P], 10)

        w_raw = [split(SCR[:, 5 * TOK + 1024 * i:5 * TOK + 1024 * (i + 1)], KT) for i in range(3)]
        w_lo = [split(SCR_r[:, 5 * TOK + 1024 * i:5 * TOK + 1024 * (i + 1)], KT) for i in range(3)]
        w_hi = [split(m, KT) for m in (WX_r[:, :], WR_r[:, 0:1024], WR_r[:, 1024:2048])]
        o_raw = [split(WR[:, 1024 * i:1024 * (i + 1)], KT) for i in range(2)]
        o_lo = [split(WR_r[:, 1024 * i:1024 * (i + 1)], KT) for i in range(2)]
        o_hi = [split(WR_r[:, 1024 * i:1024 * (i + 1)], KT) for i in (2, 3)]
        decay = split(WR[:, 0:NT * DA], NT)
        tf = [WR[:, 2048 * i:2048 * (i + 1)].rearrange("p (q n k) -> p q n k", q=4, n=NK) for i in range(2)]
        vf_in = [WR[:, TOK * i:TOK * (i + 1)] for i in range(2)]
        xg_in = [WR[:, TOK * (2 + i):TOK * (3 + i)] for i in range(2)]
        w_v = split(WR[:, 0:1024], 2)
        w_q = [split(WR[:, 1024 + 256 * i:1280 + 256 * i], 2) for i in range(2)]
        w_k = [split(WR[:, 1536 + 128 * i:1664 + 128 * i], 2) for i in range(2)]
        rtmp = WR[:, 1792:2176]
        fw = WR[:, 4096:4224]
        csw = WR[:, 4224:4480]
        gateb = split(LATS[:, :], 2)
        diag = split(WR[:, 4608:5120], 4)

        junk = [[m[:, a + 1024 * i:a + 1024 * (i + 1)] for i in range(2)] for m, a in ((H, 16384), (WR, 2048), (H, 16384))]
        junk_l = [SCR[:, 256 * i:256 * (i + 1)] for i in range(2)]
        ckc = VR[:, 4352:4608]
        vtm = split(VR[:, 0:NT * DA], NT)
        vall = split(VR[:, :], 10)
        uT = VR[:, 0:TOK]
        sg = VR[:, TOK:2 * TOK]
        ab = split(VR[:, 2304:4608], NT)
        xo = split(KV[:, 0:NT * D], NT)
        fgb = KV[:, 9216:10240]
        x_res = [xs, xo]
        gy = [[m[:, a + 1024 * i:a + 1024 * (i + 1)] for i in range(2)] for m, a in ((WR, 0), (KV, 10240))]

        cqT = split(KR_[:, 0:2304], 2)
        keysT = split(KR_[:, 2304:4864], 2)
        kT = [KR_[:, 4864 + 1280 * i:6144 + 1280 * i] for i in range(2)]
        tl = KR_[:, 0:16 * FQ].rearrange("p (n q k) -> p n q k", n=NK, q=4)
        cd = split(KR_[:, 4128:4644], 2)
        tt = split(KR_[:, 4644:5676], 4)
        yt = KR_[:, 5676:6828]
        cg = KR_[:, 6828:7084]
        tlp = split(KR_[:, 7084:7340], 2)

        consts_made = sem("consts_made")
        vec_in, small_in, wlat_in, ckc_in = sem("vec_in"), sem("small_in"), sem("wlat_in"), sem("ckc_in")
        vec_T, cols_made, cond_made = sem("vec_T"), sem("cols_made"), sem("cond_made")
        wm_in, wm_used, mod_made = sems("wm_in", 4), sem("wm_used"), sem("mod_made")
        mr_cp, mod_T = sem("mr_cp"), sem("mod_T")
        x_in = sems("x_in", NT)
        x_sq, x_rs, x_n = sem("x_sq"), sem("x_rs"), sem("x_n")
        x_T, h_full, h_hi, h_lo = sem("x_T"), sem("h_full"), sem("h_hi"), sem("h_lo")
        wl_hi, wl_lo = sem("wl_hi"), sem("wl_lo")
        l_mm, l_sq, l_rs, l_lat, l_T, l_cp = (sem(n) for n in ("l_mm", "l_sq", "l_rs", "l_lat", "l_T", "l_cp"))
        kr_in, kr_rot, kr_T, kr_cp = sem("kr_in"), sem("kr_rot"), sem("kr_T"), sem("kr_cp")
        st_ckv, st_kro = sem("st_ckv"), sem("st_kro")
        wr_in, d_mm, d_mid, d_rel = sems("wr_in", 5), sem("d_mm"), sems("d_mid", 3), sems("d_rel", 5)
        v_ready, v_T6, v_T7, v_rel6, v_rel7 = (sem(n) for n in ("v_ready", "v_T6", "v_T7", "v_rel6", "v_rel7"))
        xg_ready = sem("xg_ready")
        w_his, w_los = sem("w_his"), sem("w_los")
        sp_v, sp_x, sp_g = sem("sp_v"), sem("sp_x"), sem("sp_g")
        f_in, f_mm, f_red, f_sin = sem("f_in"), sem("f_mm"), sem("f_red"), sem("f_sin")
        dec_in, fh_mm, fh_made, fh_abs, sd_made = (sem(n) for n in ("dec_in", "fh_mm", "fh_made", "fh_abs", "sd_made"))
        nrm_mm, nrm_made = sem("nrm_mm"), sem("nrm_made")
        tf_in = sems("tf_in", 2)
        k_mm, k_cp, v_mm, v_cp, kp_made, z_made = (sem(n) for n in ("k_mm", "k_cp", "v_mm", "v_cp", "kp_made", "z_made"))
        fh_mag = sem("fh_mag")
        ti_in, vf_in_s, xg_in_s, i_mm, i_done = sem("ti_in"), sems("vfr", 2), sems("xgr", 2), sem("i_mm"), sem("i_done")
        wv_in, wq_in, v_all_mm, v_all_cp = sem("wv_in"), sems("wq_in", 2), sem("v_all_mm"), sem("v_all_cp")
        dg_made, dg_mm, gb_cp = sem("dg_made"), sem("dg_mm"), sem("gb_cp")
        pj_mm, pj_q, pj_k = sem("pj_mm"), sem("pj_q"), sem("pj_k")
        v_pair, pads_made = sem("v_pair"), sem("pads_made")
        s_mm, s_max, s_exp, p_norm = sem("s_mm"), sem("s_max"), sem("s_exp"), sem("p_norm")
        pt_mm_a, pt_mm_d, pt_cp_a, pt_cp_d = sem("pt_mm_a"), sem("pt_mm_d"), sem("pt_cp_a"), sem("pt_cp_d")
        o_mm, o_cp, sg_in = sem("o_mm"), sem("o_cp"), sem("sg_in")
        wo_in, wo_his, wo_los = sems("wo_in", 2), sem("wo_his"), sem("wo_los")
        y_his, y_los = sem("y_his"), sem("y_los")
        uw_his, uw_los, gw_his, gw_los = sem("uw_his"), sem("uw_los"), sem("gw_his"), sem("gw_los")
        g_mm, g_add = sem("g_mm"), sem("g_add")
        tl_in = sem("tl_in")
        ow_in, fw_in = sems("ow_in", 2), sem("fw_in")
        csw_mm, csw_cp, u_mm, u_cp, gt_mm, gt_cp = (sem(n) for n in ("csw_mm", "csw_cp", "u_mm", "u_cp", "gt_mm", "gt_cp"))
        ab_mm, ab_e, ab_o = sem("ab_mm"), sem("ab_e"), sem("ab_o")
        y_mm, cd_cp, y_rel, y_done = sem("y_mm"), sem("cd_cp"), sem("y_rel"), sem("y_done")
        fg_in = sem("fg_in")
        out_ready, st_out = sem("out_ready"), sem("st_out")
        dve_done, pool_done = sem("dve_done"), sem("pool_done")

        block = ctx.enter_context(nc.Block())

        class Chain:
            def __init__(self, eng, s):
                self.eng, self.s, self.n, self.i, self.per, self.k = eng, s, 0, None, 0, 0

            def loop(self, i, per):
                self.i, self.per, self.k = i, per, 0

            def end(self, trips):
                assert self.k == self.per, self.k
                self.n += trips * self.per
                self.i = None

            def __call__(self, ins):
                ins.then_inc(self.s, 1)
                if self.i is None:
                    self.n += 1
                    self.eng.wait_ge(self.s, self.n)
                else:
                    self.k += 1
                    self.eng.wait_ge(self.s, self.i * self.per + self.n + self.k)

        @block.sync
        def _(sp):
            sp.dma_start(vec_rows[0:R_ALL, :], T["vecs"]).then_inc(vec_in, 16)
            sp.dma_start(cond_rows[0:16, :], T["cond"]).then_inc(vec_in, 16)
            for i in range(4):
                sp.dma_start(wm[i], T["w_mod"][i]).then_inc(wm_in[i], 16)
            for t in range(NT):
                src = T["x_prompt"] if t == PROMPT else T["x_sample"][t * P:(t + 1) * P, :]
                sp.dma_start(xs[:, t, :], src).then_inc(x_in[t], 16)
            sp.dma_start(w_lat_raw, T["w_lat"]).then_inc(wlat_in, 16)
            sp.dma_start(ckc, T["cache_ckv"]).then_inc(ckc_in, 16)
            with sp.Fori(1, 3) as i:
                for s in range(4):
                    src = T["w_mod"][bass.ds(i * 4 + s, 1)].rearrange("a p k n -> p a k n")
                    sp.wait_ge(wm_used, i * 4 + (s - 3))
                    sp.dma_start(wm[s].unsqueeze(1), src).then_inc(wm_in[s], 16)
            smalls = [
                (lat_g[:, 0:RANK], T["qg"].partition_broadcast(P)), (lat_g[:, RANK:], T["kvg"].partition_broadcast(P)),
                (rope_t, T["rope_t"]), (rope_q[64:128, :], T["rope_q"]), (kro[:, 0, :], T["cache_krope"]),
            ]
            for d, s in smalls:
                sp.dma_start(d, s).then_inc(small_in, 16)
            sp.wait_ge(x_T, 24)
            for j in range(3):
                sp.dma_start(w_raw[j], T["w_in"][j, 0]).then_inc(wr_in[j], 16)
            fsm = [(fw1[0:EMB, :], T["f_w1"]), (fw2[0:FO, :], T["f_w2"]), (fb[0:FO, :], T["f_b"]),
                   (fw3[0:FO, :], T["f_w3"]), (tp, T["tp"]), (tpi, T["tpi"])]
            for d, s in fsm:
                sp.dma_start(d, s).then_inc(f_in, 16)
            sp.wait_ge(h_lo, 24)
            sp.dma_start(f_z[0:EMB, :], T["zT"]).then_inc(f_in, 16)
            sp.wait_ge(l_lat, NT)
            sp.dma_start(T["state_ckv"], lat[PROMPT % 2][:, RANK:]).then_inc(st_ckv, 16)
            sp.dma_start(T["state_krope"], kro[:, 9, :]).then_inc(st_kro, 16)
            def w_load(j, ahead, used, c):
                src = T["w_in"][j, ahead:CA][bass.ds(c, 1)].rearrange("a p k n -> p a k n")
                sp.wait_ge(d_mm, c * 5 + (used + 1))
                sp.dma_start(w_raw[j % 3].unsqueeze(1), src).then_inc(wr_in[j], 16)

            with sp.Fori(0, CA - 1) as i:
                for j, ahead, used in ((3, 0, 0), (4, 0, 1), (2, 1, 2), (0, 1, 3), (1, 1, 4)):
                    w_load(j, ahead, used, i)
            for j, ahead, used in ((3, 0, 0), (4, 0, 1)):
                w_load(j, ahead, used, CA - 1)
            sp.wait_ge(d_mm, 5 * CA)
            sp.dma_start(decay, T["decay"]).then_inc(dec_in, 16)
            sp.wait_ge(fh_abs, NT)
            for s in range(2):
                sp.dma_start(tf[s], T["tf"][s]).then_inc(tf_in[s], 16)
            for s in range(2):
                sp.wait_ge(v_mm, s + 1)
                sp.dma_start(tf[s], T["tf"][2 + s]).then_inc(tf_in[s], 16)
            sp.wait_ge(v_mm, NK)
            sp.wait_ge(sp_v, 16 * (CA + 1))
            sp.wait_ge(sp_x, 16 * (CA + 1))
            sp.wait_ge(sp_g, 16 * (CA + 1))
            for c in range(2):
                sp.dma_start(vf_in[c], T["sp_v"][c]).then_inc(vf_in_s[c], 16)
                sp.dma_start(xg_in[c], T["sp_x"][c]).then_inc(xg_in_s[c], 16)
            sp.wait_ge(z_made, NK + 1)
            sp.dma_start(ti, T["ti"]).then_inc(ti_in, 16)
            for c in range(2, CA):
                sp.wait_ge(i_done, c - 1)
                sp.dma_start(vf_in[c % 2], T["sp_v"][c]).then_inc(vf_in_s[c % 2], 16)
                sp.dma_start(xg_in[c % 2], T["sp_x"][c]).then_inc(xg_in_s[c % 2], 16)
            sp.wait_ge(i_done, CA)
            sp.dma_start(w_v, T["w_v"]).then_inc(wv_in, 16)
            for s in range(2):
                sp.dma_start(w_q[s], T["w_q"][s]).then_inc(wq_in[s], 16)
                sp.dma_start(w_k[s], T["w_k"][s]).then_inc(wq_in[s], 16)
            sp.dma_start(sgate, T["sp_g"][0]).then_inc(sg_in, 16)
            for h in range(2):
                sp.dma_start(wo_raw[0][:, :, 512 * h:512 * (h + 1)], T["w_oe"][:, :, 512 * h:512 * (h + 1)]).then_inc(wo_in[h], 16)
            with sp.Fori(1, HEADS // 2) as i:
                for s in range(2):
                    sp.wait_ge(pj_mm, i * 14 + (7 * s - 7))
                    sp.dma_start(w_q[s].unsqueeze(1), T["w_q"][bass.ds(i * 2 + s, 1)].rearrange("a p k n -> p a k n")).then_inc(wq_in[s], 16)
                    sp.dma_start(w_k[s].unsqueeze(1), T["w_k"][bass.ds(i * 2 + s, 1)].rearrange("a p k n -> p a k n")).then_inc(wq_in[s], 16)
                sp.wait_ge(o_cp, i * 18 + 1)
                sp.dma_start(sgate.unsqueeze(1), T["sp_g"][bass.ds(i, 1)].rearrange("a p n -> p a n")).then_inc(sg_in, 16)
            sp.wait_ge(o_cp, NT * HEADS + 1)
            for t in range(NT):
                src = T["x_prompt"] if t == PROMPT else T["x_sample"][t * P:(t + 1) * P, :]
                sp.dma_start(xs[:, t, :], src).then_inc(x_in[t], 16)
            for t in range(NT):
                sp.wait_ge(g_add, t + 1)
                sp.dma_start(T["sp_1"][t], xs[:, t, :]).then_inc(x_in[t], 16)
            sp.wait_ge(g_mm, NT)
            for d, s in ((tl, T["tl"]), (cg, T["cg"]), (tlp, T["tlp"])):
                sp.dma_start(d, s).then_inc(tl_in, 16)
            sp.wait_ge(x_sq, 2 * NT)
            for j in range(2):
                sp.dma_start(o_raw[j], T["w_io"][j, 0]).then_inc(ow_in[j], 16)
            sp.dma_start(fw, T["fnet_w"][0]).then_inc(fw_in, 16)
            with sp.Fori(1, GROUPS) as i:
                for j in range(2):
                    sp.wait_ge((u_mm, gt_mm)[j], i)
                    sp.dma_start(o_raw[j].unsqueeze(1), T["w_io"][j, bass.ds(i, 1)].rearrange("a p k n -> p a k n")).then_inc(ow_in[j], 16)
                    if j == 0:
                        sp.wait_ge(csw_mm, i)
                        sp.dma_start(fw.unsqueeze(1), T["fnet_w"][bass.ds(i, 1)].rearrange("a p n -> p a n")).then_inc(fw_in, 16)
            sp.wait_ge(gt_mm, GROUPS)
            for h in range(2):
                sp.dma_start(wo_raw[1][:, :, 512 * h:512 * (h + 1)], T["w_oo"][:, :, 512 * h:512 * (h + 1)]).then_inc(wo_in[h], 16)
            sp.wait_ge(y_done, GROUPS)
            for t in range(NT):
                sp.dma_start(xo[:, t, :], T["sp_1"][t]).then_inc(x_in[t], 16)
            sp.dma_start(fgb, T["final_g"].partition_broadcast(P)).then_inc(fg_in, 16)
            for t in range(NT):
                sp.wait_ge(out_ready, t + 1)
                dst = T["y_prompt"] if t == PROMPT else T["y_sample"][t * P:(t + 1) * P, :]
                sp.dma_start(dst, xo[:, t, :]).then_inc(st_out, 16)
            sp.wait_ge(st_out, 16 * NT)
            sp.wait_ge(st_ckv, 16)
            sp.wait_ge(st_kro, 16)

        @block.tensor
        def _(pe):
            def product(out, pairs):
                for n, (l, r) in enumerate(pairs):
                    last = nc.tensor.matmul(out, l, r, start=(n == 0), stop=(n == len(pairs) - 1))
                return last

            def product3(out, pairs):
                return product(out, [(l[a], r[b]) for l, r in pairs for a, b in ((0, 0), (0, 1), (1, 0))])

            pe.wait_ge(consts_made, 3)
            pe.wait_ge(vec_in, 32)
            nc.tensor.transpose(bank[:, 7, 0:R_ALL], vec_rows[0:R_ALL, :], ident[0:R_ALL, 0:R_ALL])
            nc.tensor.transpose(bank[:, 7, P:P + 16], cond_rows[0:16, :], ident[0:16, 0:16]).then_inc(vec_T, 1)
            pe.wait_ge(cond_made, 1)
            pe.sem_inc(mr_cp, 4)
            with pe.Fori(0, 3) as i:
                for s in range(4):
                    pe.wait_ge(wm_in[s], i * 16 + 16)
                    pe.wait_ge(mr_cp, i * 4 + (s + 1))
                    product(bank[0:2, s, :], [(cond[:, k, :], wm[s][:, k, :]) for k in range(KT)]).then_inc(wm_used, 1)
            pe.wait_ge(mr_cp, 16)
            for n in range(48):
                last = nc.tensor.transpose(bank[:, 0, 2 * n:2 * n + 2], mod_rows[:, n * P:(n + 1) * P], ident[0:2, 0:2])
            last.then_inc(mod_T, 1)

            def layer_input_T(l, src):
                e = 0
                for ch, (_, width) in enumerate(CHUNKS):
                    tiles = range(4 * ch, 4 * ch + width // P)
                    pe.wait_ge(x_n, NT * l + tiles[-1] + 1)
                    for k in range(KT):
                        if e >= 6:
                            pe.wait_ge(h_full, 24 * l + e - 5)
                        for n, t in enumerate(tiles):
                            last = nc.tensor.transpose(bank[:, 1 + e % 6, n * P:(n + 1) * P], src[:, t, k * P:(k + 1) * P], ident[:, :])
                        last.then_inc(x_T, 1)
                        e += 1

            layer_input_T(0, xs)
            pe.wait_ge(h_lo, 24)
            pe.wait_ge(wl_lo, 1)
            pe.wait_ge(ckc_in, 16)
            for j in range(2):
                last = nc.tensor.transpose(bank[:, 6, j * P:(j + 1) * P], ckc[:, j * P:(j + 1) * P], ident[:, :])
            last.then_inc(l_T, 1)

            def lat_T(t):
                pe.wait_ge(l_lat, t + 1)
                if t >= 2:
                    pe.wait_ge(l_cp, t)
                for j in range(4):
                    last = nc.tensor.transpose(bank[:, 4 + t % 2, j * P:(j + 1) * P], lat[t % 2][:, j * P:(j + 1) * P], ident[:, :])
                last.then_inc(l_T, 1)

            for t in range(NT):
                if t >= 2:
                    pe.wait_ge(l_lat, t - 1)
                for j, (a, b) in enumerate(((0, RANK), (RANK, LAT))):
                    last = product3(bank[:, 2 * (t % 2) + j, 0:b - a],
                                    [([m[:, k, t * P:(t + 1) * P] for m in hT], [m[:, k, a:b] for m in w_lat]) for k in range(KT)])
                last.then_inc(l_mm, 1)
                if t:
                    lat_T(t - 1)
            lat_T(NT - 1)
            pe.wait_ge(kr_rot, 1)
            for t in range(10):
                last = nc.tensor.transpose(bank[0:ROPE, t // 4, (t % 4) * P:(t % 4 + 1) * P], krr[:, t, :], ident[:, :])
            last.then_inc(kr_T, 1)
            pe.wait_ge(l_cp, NT + 1)
            pe.wait_ge(kr_cp, 1)

            for s in (d_rel[3], d_rel[4], v_rel6, v_rel7):
                pe.sem_inc(s, 1)
            with pe.Fori(0, CA) as c:
                for j in range(5):
                    pe.wait_ge(w_los, c * 5 + (j + 1))
                    if j < 2:
                        pe.wait_ge(d_rel[4 - j], c + 1)
                    else:
                        pe.wait_ge(d_rel[j - 2], c + 1)
                    for n in range(3):
                        last = product3(bank[:, 3 * (j % 2) + n, 0:T3], [([m[j % 3][:, k, :] for m in (w_hi, w_lo)],
                                                                          [m[:, k, T3 * n:T3 * (n + 1)] for m in hT]) for k in range(KT)])
                    last.then_inc(d_mm, 1)
                    if j == 2:
                        pe.wait_ge(v_ready, c + 1)
                        for odd in range(2):
                            pe.wait_ge((v_rel6, v_rel7)[odd], c * (2 - odd) + 1)
                            for n in range(NK):
                                last = nc.tensor.transpose(bank[:, 6 + odd, n * P:(n + 1) * P], vt[:, 2 * P * n + odd:2 * P * (n + 1):2], ident[:, :])
                            last.then_inc((v_T6, v_T7)[odd], 1)
                        pe.wait_ge(v_rel6, c * 2 + 2)
                        nc.tensor.transpose(bank[:, 6, 0:P], vt[:, LS:TOK], ident[:, :]).then_inc(v_T6, 1)

            pe.wait_ge(d_rel[4], CA + 1)
            pe.wait_ge(d_rel[3], CA + 1)
            pe.wait_ge(f_in, 16 * 7)
            for n, (a, w) in enumerate(CHUNKS):
                last = nc.tensor.matmul(bank[0:FO, n, 0:w], fw1[0:EMB, :], f_z[0:EMB, a:a + w], start=True, stop=True)
            last.then_inc(f_mm, 1)
            pe.wait_ge(f_sin, 1)
            for n, (a, w) in enumerate(CHUNKS):
                last = nc.tensor.matmul(bank[0:FO, n, 0:w], fw2[0:FO, :], f_z[0:FO, a:a + w], start=True, stop=True)
            last.then_inc(f_mm, 1)
            pe.wait_ge(f_sin, 2)
            for t in range(NT):
                if t >= 3:
                    pe.wait_ge(fh_made, t - 2)
                for j in range(2):
                    last = nc.tensor.matmul(bank[:, 2 * (t % 3) + j, :], f_z[0:FO, t * P:(t + 1) * P], fw3[0:FO, j * DA:(j + 1) * DA], start=True, stop=True)
                last.then_inc(fh_mm, 1)
            pe.wait_ge(fh_abs, NT)
            pe.wait_ge(v_rel6, 2 * CA + 1)
            for w in range(2):
                for c in range(CA):
                    last = nc.tensor.matmul(bank[:, 6, w * CA + c:w * CA + c + 1], f_abs[:, w, c * P:(c + 1) * P], ones[:, 0:1], start=True, stop=True)
            last.then_inc(nrm_mm, 1)

            pe.wait_ge(sd_made, NT)
            pe.wait_ge(nrm_made, 1)
            pe.wait_ge(v_rel7, CA + 1)
            for kt in range(NK):
                s = kt % 2
                pe.wait_ge(tf_in[s], 16 * (kt // 2 + 1))
                if kt:
                    pe.wait_ge(k_cp, kt)
                for q in range(4):
                    last = product(bank[:, q, :], [(tf[s][:, q, n, :], sd[:, n + NK * (q // 2), q % 2, :]) for n in range(NK)])
                last.then_inc(k_mm, 1)
                if kt:
                    pe.wait_ge(v_cp, kt)
                for q in range(4):
                    last = product(bank[:, 4 + q, :], [(tf[s][:, q, n, :], vtm[:, n + NK * (q // 2), :]) for n in range(NK)])
                last.then_inc(v_mm, 1)
            pe.wait_ge(k_cp, NK)
            for q in range(2):
                nc.tensor.matmul(bank[:, q, :], tp[:, q, :], sd[:, PROMPT, q, :], start=True, stop=True)
            for q in range(2):
                last = nc.tensor.matmul(bank[:, 2 + q, :], tp[:, q, :], vtm[:, PROMPT, :], start=True, stop=True)
            last.then_inc(k_mm, 1)

            pe.wait_ge(z_made, NK + 1)
            pe.wait_ge(ti_in, 16)
            for c in range(CA):
                if c >= 2:
                    pe.wait_ge(i_done, c - 1)
                b0 = 3 * (c % 2)
                for odd in range(2):
                    product(bank[:, b0 + odd, :], [(zz[:, kt, 2 * odd + q, c * P:(c + 1) * P], ti[:, kt, 2 * odd + q, :])
                                                   for kt in range(NK) for q in range(2)])
                product(bank[:, b0 + 2, 0:P], [(yp[:, q, c * P:(c + 1) * P], tpi[:, q, :]) for q in range(2)]).then_inc(i_mm, 1)

            pe.wait_ge(i_done, CA)
            pe.wait_ge(wv_in, 16)
            for t in range(10):
                if t >= 2:
                    pe.wait_ge(v_all_cp, t - 1)
                product(bank[:, 6 + t % 2, :], [(keysT[:, k, t * P:(t + 1) * P], w_v[:, k, :]) for k in range(2)]).then_inc(v_all_mm, 1)
            pe.wait_ge(v_all_cp, 10)

            def gate_rows(l):
                for n in range(4):
                    pe.wait_ge(dg_made, 4 * l + n + 1)
                    nc.tensor.matmul(bank[:, 6, :], ones[:, :], diag.rearrange("p a b -> p (a b)"), start=True, stop=True).then_inc(dg_mm, 1)
                pe.wait_ge(gb_cp, 4 * l + 4)

            gate_rows(0)

            pe.wait_ge(pads_made, 1)
            for m in (pt_cp_a, o_cp, o_mm):
                pe.sem_inc(m, 1)
            with pe.Fori(0, HEADS // 2) as i:
                for s in range(2):
                    def project(s, steps):
                        for n in steps:
                            if n == 0:
                                pe.wait_ge(wq_in[s], i * 32 + 32)
                            if n == 2:
                                pe.wait_ge(o_cp, i * 18 + (7 * s + 1))
                            if n == 5 and s:
                                pe.wait_ge(o_cp, i * 18 + 9)
                            if n == 6:
                                pe.wait_ge(pj_q, i * 6 + (3 * s + 1))
                            wt, src, m = (w_q[s], cqT, P) if n < 3 else (w_k[s], keysT, NOPE)
                            a = KS3 * (n % 3) if n < 6 else KEYS
                            w = KS3 if n < 6 else P
                            product(bank[0:m, (3, 4, 5, 1, 0, 2, 3)[n], 0:w], [(wt[:, k, 0:m], src[:, k, a:a + w]) for k in range(2)]).then_inc(pj_mm, 1)

                    def scores(t):
                        if t >= 2:
                            pe.wait_ge(s_exp, i * 18 + (9 * s + t - 1))
                            pe.wait_ge(pt_cp_d, i * 16 + (8 * s + t - 1))
                        b0 = 3 * (t % 2)
                        q = qT[s][:, t * P:(t + 1) * P]
                        if t < PROMPT:
                            for n in range(3):
                                if n == 2 and t:
                                    pe.wait_ge(o_cp, i * 18 + (9 * s + (t - 1 if t > 2 else 1)))
                                last = nc.tensor.matmul(bank[:, b0 + n, 0:KS3], q, kT[s][:, n * KS3:(n + 1) * KS3], start=True, stop=True)
                        else:
                            last = nc.tensor.matmul(bank[:, b0, 0:P], q, kT[s][:, KEYS:ALLKEYS], start=True, stop=True)
                        last.then_inc(s_mm, 1)

                    def probs_T(t):
                        u = 9 * s + t
                        pe.wait_ge(p_norm, i * 18 + (u + 1))
                        pe.wait_ge(pt_cp_a, i * 18 + (u + 1))
                        for n in range(7 if t < PROMPT else 1):
                            last = nc.tensor.transpose(bank[:, 6 + n // 4, n % 4 * P:(n % 4 + 1) * P], px[t % 2][:, n * P:(n + 1) * P], ident[:, :])
                        last.then_inc(pt_mm_a, 1)
                        if t < PROMPT:
                            for n in range(7, 9):
                                last = nc.tensor.transpose(bank[:, 3 * (t % 2) + n - 7, KS3:KS3 + P], px[t % 2][:, n * P:(n + 1) * P], ident[:, :])
                            last.then_inc(pt_mm_d, 1)

                    def outputs(t):
                        u = 9 * s + t
                        pe.wait_ge(pt_cp_a, i * 18 + (u + 2))
                        if t >= 7:
                            pe.wait_ge(o_cp, i * 18 + u)
                        if s == 0 and t == PROMPT:
                            pe.wait_ge(pj_q, i * 6 + 6)
                        o = bank[:, 5 - 3 * (t % 2), KS3:KS3 + P]
                        if t < PROMPT:
                            pe.wait_ge(pt_cp_d, i * 16 + (8 * s + t + 1))
                            last = product(o, [(vpair[:, kt, :], pT[t % 2][:, kt, :]) for kt in range(9)])
                        else:
                            last = product(o, [(vpair[:, 9, :], pT[t % 2][:, 0, :])])
                        last.then_inc(o_mm, 1)

                    if s == 0:
                        project(0, range(7))
                        pe.wait_ge(v_pair, i + 1)
                    pe.wait_ge(pj_q, i * 6 + 3 * (s + 1))
                    pe.wait_ge(pj_k, i * 8 + 4 * (s + 1))
                    scores(0)
                    for t in range(NT):
                        if t + 1 < NT:
                            scores(t + 1)
                        if s == 0 and t == NT - 1:
                            pe.wait_ge(pt_cp_d, i * 16 + 8)
                            project(1, range(0, 3))
                        probs_T(t)
                        if t:
                            outputs(t - 1)
                    if s == 0:
                        project(1, range(3, 5))
                    outputs(NT - 1)
                    if s == 0:
                        project(1, range(5, 7))
            pe.wait_ge(o_cp, NT * HEADS + 1)

            def out_product(l):
                for t in range(NT):
                    if t >= 2:
                        pe.wait_ge(g_add, NT * l + t - 1)
                    pe.wait_ge(y_los, NT * l + t + 1)
                    for j in range(2):
                        for k in range(KT):
                            if t == 0 and k % 2 == 0:
                                pe.wait_ge(wo_los, 8 * l + 4 * j + k // 2 + 1)
                            for a, b in ((0, 0), (0, 1), (1, 0)):
                                last = nc.tensor.matmul(bank[:, 2 * (t % 2) + j, :], y_sl[l][t % 2][a][:, k, :], wo[l][b][:, k, j * 512:(j + 1) * 512],
                                                        start=(k == 0 and a == b), stop=(k == KT - 1 and a == 1))
                    last.then_inc(g_mm, 1)

            out_product(0)
            pe.wait_ge(g_add, NT)
            gate_rows(1)
            layer_input_T(1, xs)
            pe.wait_ge(h_lo, 48)

            pe.wait_ge(tl_in, 48)
            pe.sem_inc(gt_cp, 1)
            pe.sem_inc(y_rel, 1)
            with pe.Fori(0, GROUPS) as g:
                def third(j, n):
                    return product3(bank[:, 3 * j + n, 0:T3], [([m[j][:, k, :] for m in (o_hi, o_lo)],
                                                                [m[:, k, T3 * n:T3 * (n + 1)] for m in hT]) for k in range(KT)])

                pe.wait_ge(gw_los, g + 1)
                pe.wait_ge(gt_cp, g + 1)
                third(1, 0)
                pe.wait_ge(fw_in, g * 16 + 16)
                pe.wait_ge(y_rel, g + 1)
                for q in range(2):
                    last = nc.tensor.matmul(bank[:, 7, q * P:(q + 1) * P], cg[:, q * P:(q + 1) * P], fw[:, :], start=True, stop=True)
                last.then_inc(csw_mm, 1)
                pe.wait_ge(uw_los, g + 1)
                for n in range(3):
                    last = third(0, n)
                last.then_inc(u_mm, 1)
                for n in (1, 2):
                    last = third(1, n)
                last.then_inc(gt_mm, 1)
                pe.wait_ge(u_cp, g + 1)
                pe.wait_ge(csw_cp, g + 1)
                for n in range(5):
                    if n >= 2:
                        pe.wait_ge(*((ab_e, g * 3 + n // 2) if n % 2 == 0 else (ab_o, g * 2 + 1)))
                    for m_ in range(2 if n < 4 else 1):
                        t = 2 * n + m_
                        if t < PROMPT:
                            odd, q = divmod(t, NK)
                            lhs = uT[:, 2 * P * q + odd:2 * P * (q + 1):2]
                        else:
                            lhs = uT[:, LS:TOK]
                        last = nc.tensor.matmul(bank[:, 6 + n % 2, m_ * 256:(m_ + 1) * 256], lhs, csw[:, :], start=True, stop=True)
                    last.then_inc(ab_mm, 1)
                pe.wait_ge(ab_e, g * 3 + 3)
                pe.wait_ge(ab_o, g * 2 + 2)
                for q in range(4):
                    product(bank[:, (0, 1, 2, 6)[q], 0:FQ], [(ab[:, n + NK * (q // 2), (q % 2) * P:(q % 2 + 1) * P], tl[:, n, q, :]) for n in range(NK)])
                product(bank[:, 7, 0:P], [(ab[:, PROMPT, q * P:(q + 1) * P], tlp[:, q, :]) for q in range(2)]).then_inc(y_mm, 1)

            pe.wait_ge(y_rel, GROUPS + 1)
            out_product(1)

        @block.scalar
        def _(act):
            act.wait_ge(vec_T, 1)
            nc.scalar.activation(cond.rearrange("p k g -> p g k"), split(bank[:, 7, P:P + 16], 2), ACT.Silu).then_inc(cond_made, 1)

            def square(l, t, src):
                if t >= 2:
                    act.wait_ge(x_sq, NT * l + t - 1)
                nc.scalar.activation(junk[l][t % 2], src[:, t, :], ACT.Square, accum_out=ssq[:, NT * l + t:NT * l + t + 1]).then_inc(x_sq, 1)

            def layer_input(l):
                for e in range(24):
                    ch, k = divmod(e, KT)
                    a, w = CHUNKS[ch]
                    grp = ch // 2
                    act.wait_ge(x_T, 24 * l + e + 1)
                    if e >= 4:
                        act.wait_ge(h_lo, 24 * l + e - 3)
                    tmp = h_tmp[e % 4][:, 0:w]
                    nc.scalar.activation(tmp, bank[:, 1 + e % 6, 0:w], ACT.Identity, scale=gsc[:, 8 * l + k, grp:grp + 1],
                                         bias=modc[:, 24 * l + k, grp:grp + 1]).then_inc(h_full, 1)
                    if e % 2 == 0:
                        act.wait_ge(h_full, 24 * l + e + 1)
                        nc.scalar.copy(hT[0][:, k, a:a + w], tmp).then_inc(h_hi, 1)

            def out_his(l, squares_of):
                def y_hi(t):
                    if t >= 2:
                        act.wait_ge(g_mm, NT * l + t - 1)
                    nc.scalar.copy(y_sl[l][t % 2][0], y_in[l][:, :, t * P:(t + 1) * P]).then_inc(y_his, 1)

                y_hi(0)
                for h in range(2):
                    act.wait_ge(wo_in[h], 16 * l + 16)
                    for k in range(0, KT, 2):
                        nc.scalar.copy(wo[l][0][:, k:k + 2, 512 * h:512 * (h + 1)], wo_raw[l][:, k:k + 2, 512 * h:512 * (h + 1)]).then_inc(wo_his, 1)
                    if h == 0:
                        y_hi(1)
                for t in range(NT):
                    if t + 2 < NT:
                        y_hi(t + 2)
                    squares_of(t)

            for t in range(NT):
                act.wait_ge(x_in[t], 16)
                square(0, t, xs)
            act.wait_ge(wlat_in, 16)
            nc.scalar.copy(w_lat[0], w_lat_raw).then_inc(wl_hi, 1)
            with act.Fori(0, 3) as i:
                for s in range(4):
                    act.wait_ge(wm_used, i * 4 + (s + 1))
                    nc.scalar.copy(mod_rows[:, bass.ds(i * 2048 + s * 512, 512)], bank[0:2, s, :]).then_inc(mr_cp, 1)
            act.wait_ge(mod_made, 2)
            layer_input(0)
            def w_split_hi(j, c, used):
                act.wait_ge(wr_in[j], c * 16 + 16)
                if j >= 3 or used == 3:
                    act.wait_ge(d_mm, (c - (j < 3)) * 5 + (used + 1))
                nc.scalar.copy(w_hi[j % 3], w_raw[j % 3]).then_inc(w_his, 1)

            act.wait_ge(l_T, 1)
            nc.scalar.copy(keysT[:, :, 0:P], split(bank[:, 6, 0:2 * P], 2)).then_inc(l_cp, 1)
            for t in range(NT + 1):
                if t < NT:
                    act.wait_ge(l_mm, t + 1)
                    if t:
                        act.wait_ge(l_sq, t)
                    for j in range(2):
                        last = nc.scalar.activation(junk_l[j], bank[:, 2 * (t % 2) + j, 0:RANK], ACT.Square,
                                                    accum_out=ssq2[:, 2 * t + j:2 * t + j + 1])
                    last.then_inc(l_sq, 1)
                if t:
                    act.wait_ge(l_T, t + 1)
                    src = bank[:, 4 + (t - 1) % 2, :].rearrange("p (a k n) -> p a k n", a=2, k=2)
                    nc.scalar.copy(cqT[:, :, (t - 1) * P:t * P], src[:, 0])
                    nc.scalar.copy(keysT[:, :, t * P:(t + 1) * P], src[:, 1]).then_inc(l_cp, 1)
            w_split_hi(0, 0, None)
            act.wait_ge(kr_T, 1)
            nc.scalar.copy(kT[0][64:96, :], bank[0:ROPE, 0:3, :].rearrange("p a n -> p (a n)")[:, 0:ALLKEYS])
            nc.scalar.copy(kT[1][64:96, :], bank[0:ROPE, 0:3, :].rearrange("p a n -> p (a n)")[:, 0:ALLKEYS]).then_inc(kr_cp, 1)

            def spill(c, ready, n, buf, dst, s):
                act.wait_ge(ready, c + n)
                act.dma_start(T[dst][bass.ds(c, 1)].rearrange("a p n -> p a n"), buf.unsqueeze(1)).then_inc(s, 16)

            for s in (sp_v, sp_x, sp_g):
                act.sem_inc(s, 16)

            def hyena_input(c, last):
                for j, (dst, m0) in enumerate(((u1, 4), (vt, 8), (x0, 0))):
                    if j == 0:
                        w_split_hi(1, c, None)
                    elif j == 1:
                        w_split_hi(2, c, None)
                    else:
                        w_split_hi(3, c, 0)
                    act.wait_ge(d_mm, c * 5 + (j + 1))
                    if j == 1:
                        act.wait_ge(sp_v, c * 16 + 16)
                    if j == 2:
                        act.wait_ge(sp_x, c * 16 + 16)
                    nc.scalar.activation(split(dst, 3), bank[:, 3 * (j % 2):3 * (j % 2) + 3, 0:T3], ACT.Identity, scale=col[:, bass.ds(c + (R_CW + 12 + m0), 1)],
                                         bias=col[:, bass.ds(c + (R_CB + m0), 1)]).then_inc(d_mid[j], 1)
                for odd in range(2):
                    act.wait_ge((v_T6, v_T7)[odd], c * (2 - odd) + 1)
                    nc.scalar.copy(vtm[:, NK * odd:NK * (odd + 1), bass.ds(c * P, P)], split(bank[:, 6 + odd, :], NK)).then_inc((v_rel6, v_rel7)[odd], 1)
                act.wait_ge(v_T6, c * 2 + 2)
                nc.scalar.copy(vtm[:, PROMPT, bass.ds(c * P, P)], bank[:, 6, 0:P]).then_inc(v_rel6, 1)
                spill(c, v_ready, 1, vt, "sp_v", sp_v)
                w_split_hi(4, c, 1)
                act.wait_ge(d_mm, c * 5 + 4)
                nc.scalar.activation(split(ga, 3), bank[:, 3:6, 0:T3], ACT.Silu).then_inc(d_rel[3], 1)
                if not last:
                    w_split_hi(0, c + 1, 3)
                act.wait_ge(d_mm, c * 5 + 5)
                act.wait_ge(sp_g, c * 16 + 16)
                nc.scalar.activation(split(gb, 3), bank[:, 0:3, 0:T3], ACT.Silu).then_inc(d_rel[4], 1)
                spill(c, xg_ready, 1, x0, "sp_x", sp_x)
                spill(c, d_rel[4], 2, gb, "sp_g", sp_g)

            with act.Fori(0, CA - 1) as c:
                hyena_input(c, False)
            hyena_input(CA - 1, True)

            for n in range(2):
                act.wait_ge(f_red, n + 1)
                nc.scalar.activation(f_z[0:FO, :], f_x[0:FO, :], ACT.Sin).then_inc(f_sin, 1)
            act.wait_ge(sp_x, 16 * (CA + 1))
            act.wait_ge(sp_g, 16 * (CA + 1))
            for t in range(NT):
                act.wait_ge(fh_made, t + 1)
                if t >= 2:
                    act.wait_ge(fh_abs, t - 1)
                nc.scalar.activation(f_mag[t % 2], f_h[t % 2], ACT.Abs).then_inc(fh_mag, 1)
            for kt in range(NK):
                act.wait_ge(k_mm, kt + 1)
                if kt:
                    act.wait_ge(z_made, kt)
                else:
                    act.wait_ge(sd_made, NT)
                nc.scalar.copy(ks, bank[:, 0:4, :]).then_inc(k_cp, 1)
                act.wait_ge(v_mm, kt + 1)
                nc.scalar.copy(vs, bank[:, 4:8, :]).then_inc(v_cp, 1)
            act.wait_ge(k_mm, NK + 1)
            act.wait_ge(z_made, NK)
            nc.scalar.copy(ks[:, 0:2, :], bank[:, 0:2, :])
            nc.scalar.copy(vs[:, 0:2, :], bank[:, 2:4, :]).then_inc(k_cp, 1)

            for t in range(10):
                act.wait_ge(v_all_mm, t + 1)
                nc.scalar.copy(vall[:, t, :], bank[:, 6 + t % 2, :]).then_inc(v_all_cp, 1)
            with act.Fori(0, HEADS // 2) as i:
                def keys(s):
                    for n in range(4):
                        act.wait_ge(pj_mm, i * 14 + (7 * s + 4 + n))
                        a, w = KS3 * n, KS3 if n < 3 else P
                        nc.scalar.copy(kT[s][0:NOPE, a:a + w], bank[0:NOPE, (1, 0, 2, 3)[n], 0:w]).then_inc(pj_k, 1)

                keys(0)
                for s in range(2):
                    def exps(t):
                        act.wait_ge(s_max, i * 18 + (9 * s + t + 1))
                        b0 = 3 * (t % 2)
                        src, dst = (bank[:, b0:b0 + 3, 0:KS3], split(px[t % 2], 3)) if t < PROMPT else (bank[:, b0, 0:P], px[t % 2][:, 0:P])
                        nc.scalar.activation(dst, src, ACT.Exp, scale=SCALE, bias=nmax[:, t % 2:t % 2 + 1],
                                             accum_out=rsum[:, t % 2:t % 2 + 1]).then_inc(s_exp, 1)

                    exps(0)
                    for t in range(NT):
                        u = 9 * s + t
                        act.wait_ge(pt_mm_a, i * 18 + (u + 1))
                        act.wait_ge(o_mm, i * 18 + (u if t >= 2 else 9 * s + 1))
                        if t < PROMPT:
                            nc.scalar.copy(pT[t % 2][:, 0:7, :].rearrange("p a n -> p (a n)"), banks(6, 2, 0, 7 * P)).then_inc(pt_cp_a, 1)
                            exps(t + 1)
                        else:
                            nc.scalar.copy(pT[t % 2][:, 0, :], bank[:, 6, 0:P]).then_inc(pt_cp_a, 1)
                    if s == 0:
                        keys(1)

            act.wait_ge(o_cp, NT * HEADS + 1)
            def residual_square(l, src):
                def f(t):
                    act.wait_ge(g_add, NT * l + t + 1)
                    square(l + 1, t, src)
                return f

            out_his(0, residual_square(0, xs))
            layer_input(1)

            def o_split_hi(j, g):
                act.wait_ge(ow_in[j], g * 16 + 16)
                nc.scalar.copy(o_hi[j], o_raw[j]).then_inc((uw_his, gw_his)[j], 1)

            o_split_hi(1, 0)
            o_split_hi(0, 0)

            def fourier(g, last):
                act.wait_ge(csw_mm, g + 1)
                nc.scalar.copy(csw[:, :], bank[:, 7, 0:256]).then_inc(csw_cp, 1)
                act.wait_ge(u_mm, g + 1)
                nc.scalar.copy(split(uT, 3), bank[:, 0:3, 0:T3]).then_inc(u_cp, 1)
                act.wait_ge(gt_mm, g + 1)
                nc.scalar.activation(split(sg, 3), bank[:, 3:6, 0:T3], ACT.Silu).then_inc(gt_cp, 1)
                for n in (1, 3):
                    act.wait_ge(ab_mm, g * 5 + (n + 1))
                    nc.scalar.copy(ab[:, 2 * n:2 * n + 2, :], split(bank[:, 7, :], 2)).then_inc(ab_o, 1)
                if not last:
                    o_split_hi(1, g + 1)
                act.wait_ge(y_mm, g + 1)
                nc.scalar.copy(cd[:, 0, :], bank[:, 2, 0:FQ])
                nc.scalar.copy(cd[:, 1, :], bank[:, 6, 0:FQ]).then_inc(cd_cp, 1)
                if not last:
                    o_split_hi(0, g + 1)

            with act.Fori(0, GROUPS - 1) as g:
                fourier(g, False)
            fourier(GROUPS - 1, True)

            act.wait_ge(y_done, GROUPS)
            out_his(1, residual_square(1, xo))

        @block.vector
        def _(dve):
            link = Chain(dve, dve_done)
            tscal, stt, tt_ = nc.vector.tensor_scalar, nc.vector.scalar_tensor_tensor, nc.vector.tensor_tensor
            dve.wait_ge(vec_T, 1)
            dve.wait_ge(cond_made, 1)
            link(nc.vector.tensor_copy(col[:, :], bank[:, 7, 0:R_ALL]))
            def modulation():
                dve.wait_ge(mod_T, 1)
                nc.vector.tensor_tensor(modc, split(bank[:, 0, 0:96], 48), col[:, R_BMOD:R_BMOD + 48].unsqueeze(2).broadcast_to([P, 48, 2]),
                                        ALU.add).then_inc(mod_made, 1)
                dve.wait_ge(mod_made, 1)
                for l in range(2):
                    last = stt(gsc[:, 8 * l:8 * l + 8, :], modc[:, 24 * l + 8:24 * l + 16, :], 1.0,
                               col[:, R_NG + 8 * l:R_NG + 8 * l + 8].unsqueeze(2).broadcast_to([P, KT, 2]), ALU.add, ALU.mult)
                last.then_inc(mod_made, 1)

            def normalise(l, dst, src):
                for t in range(NT):
                    dve.wait_ge(x_rs, NT * l + t + 1)
                    tscal(dst[:, t, :], src[:, t, :], rstd[:, NT * l + t:NT * l + t + 1], None, ALU.mult).then_inc(x_n, 1)

            def layer_input(l):
                for e in range(24):
                    ch, k = divmod(e, KT)
                    a, w = CHUNKS[ch]
                    tmp = h_tmp[e % 4][:, 0:w]
                    if e % 2:
                        dve.wait_ge(h_full, 24 * l + e + 1)
                        link(nc.vector.tensor_copy(hT[0][:, k, a:a + w], tmp))
                    else:
                        dve.wait_ge(h_hi, 12 * l + e // 2 + 1)
                    tt_(hT[1][:, k, a:a + w], tmp, hT[0][:, k, a:a + w].bitcast(F32), ALU.subtract).then_inc(h_lo, 1)

            dve.wait_ge(wl_hi, 1)
            tt_(w_lat[1], w_lat_raw, w_lat[0].bitcast(F32), ALU.subtract).then_inc(wl_lo, 1)
            normalise(0, xs, xs)
            modulation()
            dve.wait_ge(mod_made, 2)
            layer_input(0)
            dve.wait_ge(small_in, 16 * 5)
            for t in range(NT):
                dve.wait_ge(l_rs, t + 1)
                if t >= 2:
                    dve.wait_ge(l_T, t)
                b = 2 * (t % 2)
                nc.vector.tensor_copy(kro[:, 1 + t, :], bank[:, b + 1, RANK:RANK + ROPE])
                for j in range(2):
                    last = stt(lat[t % 2][:, j * RANK:(j + 1) * RANK], bank[:, b + j, 0:RANK], rstd2[:, 2 * t + j:2 * t + j + 1],
                               lat_g[:, j * RANK:(j + 1) * RANK], ALU.mult, ALU.mult)
                last.then_inc(l_lat, 1)
            dve.wait_ge(l_lat, NT)
            swap = lambda a: a.rearrange("p t (x h f) -> p (t x) h f", x=2, h=2)
            for h in range(2):
                last = nc.vector.tensor_copy(swap(krs)[:, :, h, :], swap(kro[:, 1:9, :])[:, :, 1 - h, :])
            link(last)
            rt = lambda n: rope_t[:, n, :].rearrange("p (t f) -> p t f", t=8)
            nc.vector.tensor_copy(krr[:, 0, :], kro[:, 0, :])
            nc.vector.tensor_copy(krr[:, 9, :], kro[:, 9, :])
            tt_(krr[:, 1:9, :], kro[:, 1:9, :], rt(0), ALU.mult)
            link(tt_(krs, krs, rt(1), ALU.mult))
            tt_(krr[:, 1:9, :], krr[:, 1:9, :], krs, ALU.add).then_inc(kr_rot, 1)

            def w_split_lo(j, c):
                dve.wait_ge(w_his, c * 5 + (j + 1))
                tt_(w_lo[j % 3], w_raw[j % 3], w_hi[j % 3].bitcast(F32), ALU.subtract).then_inc(w_los, 1)

            def tap(dst, b, w, right):
                d, ps, r = split(dst, 3), bank[:, b:b + 3, 0:T3], int(right)
                add = lambda o, i: stt(o, i, w, o, ALU.mult, ALU.add)
                cut = LS - 2 * T3
                add(d[:, 0:2, 1 - r:T3 - r], ps[:, 0:2, r:T3 - 1 + r])
                add(d[:, 2, 1 - r:cut - r], ps[:, 2, r:cut - 1 + r])
                add(d[:, 2, cut + 1 - r:T3 - r], ps[:, 2, cut + r:T3 - 1 + r])
                if right:
                    return add(d[:, 0:2, T3 - 1], ps[:, 1:3, 0])
                return add(d[:, 1:3, 0], ps[:, 0:2, T3 - 1])

            w_split_lo(0, 0)

            def hyena_input(c, final):
                link.loop(c, 3)
                for j, (dst, m0) in enumerate(((u1, 4), (vt, 8), (x0, 0))):
                    w_split_lo(j + 1, c)
                    dve.wait_ge(d_mid[j], c + 1)
                    link(tap(dst, 3 * (j % 2), col[:, bass.ds(c + (R_CW + m0), 1)], False))
                    tap(dst, 3 * (j % 2), col[:, bass.ds(c + (R_CW + 24 + m0), 1)], True).then_inc(d_rel[j], 1)
                    if j == 1:
                        dve.wait_ge(d_rel[1], c + 1)
                        tt_(vt, vt, u1, ALU.mult).then_inc(v_ready, 1)
                w_split_lo(4, c)
                dve.wait_ge(d_rel[2], c + 1)
                dve.wait_ge(d_rel[3], c + 2)
                tt_(x0, x0, ga, ALU.mult).then_inc(xg_ready, 1)
                if not final:
                    w_split_lo(0, c + 1)

            with dve.Fori(0, CA - 1) as c:
                hyena_input(c, False)
            hyena_input(CA - 1, True)
            link.end(CA)

            for n in range(2):
                dve.wait_ge(f_mm, n + 1)
                link(tscal(f_x[0:FO, :], bank[0:FO, 0:3, :].rearrange("p a n -> p (a n)")[:, 0:TOK], fb[0:FO, n:n + 1], None, ALU.add))
                link(tscal(f_r[0:FO, :], f_x[0:FO, :], 1.0 / (2 * math.pi), MAGIC, ALU.mult, ALU.add))
                link(tscal(f_r[0:FO, :], f_r[0:FO, :], MAGIC, None, ALU.subtract))
                link(stt(f_x[0:FO, :], f_r[0:FO, :], -TWO_PI_HI, f_x[0:FO, :], ALU.mult, ALU.add))
                link(stt(f_x[0:FO, :], f_r[0:FO, :], -TWO_PI_LO, f_x[0:FO, :], ALU.mult, ALU.add))
                tscal(f_x[0:FO, :], f_x[0:FO, :], PI_IN, -PI_IN, ALU.min, ALU.max).then_inc(f_red, 1)
            dve.wait_ge(sp_v, 16 * (CA + 1))
            dve.wait_ge(sp_x, 16 * (CA + 1))
            link(nc.vector.memset(f_abs, 0.0))
            dve.wait_ge(dec_in, 16)
            for t in range(NT):
                w = int(t == PROMPT)
                dve.wait_ge(fh_mm, t + 1)
                if t >= 2:
                    dve.wait_ge(sd_made, t - 1)
                b = 2 * (t % 3)
                tt_(f_h[t % 2][:, 0, :], bank[:, b, :], decay[:, t, :], ALU.mult)
                link_made = tt_(f_h[t % 2][:, 1, :], bank[:, b + 1, :], decay[:, t, :], ALU.mult)
                link_made.then_inc(fh_made, 1)
                dve.wait_ge(fh_mag, t + 1)
                link(tt_(f_abs[:, w, :], f_mag[t % 2][:, 0, :], f_abs[:, w, :], ALU.add))
                last = tt_(f_abs[:, w, :], f_mag[t % 2][:, 1, :], f_abs[:, w, :], ALU.add)
                if t in (0, PROMPT):
                    link(last)
                    last = nc.vector.memset(f_h[t % 2][0:1, 1, :], 0.0)
                last.then_inc(fh_abs, 1)
                dve.wait_ge(fh_abs, t + 1)
            dve.wait_ge(nrm_mm, 1)
            nc.vector.reciprocal(rnorm[:, :], bank[:, 6, 0:2 * CA]).then_inc(nrm_made, 1)

            for kt in range(NK):
                dve.wait_ge(v_cp, kt + 1)
                tt_(vp[:, 0:2, :], vs[:, 0:2, :], vs[:, 2:4, :], ALU.add)
                link(tt_(vp[:, 2:4, :], vs[:, 0:2, :], vs[:, 2:4, :], ALU.subtract))
                dve.wait_ge(kp_made, kt + 1)
                four = lambda a: a.rearrange("p (s r) n -> p s r n", s=2)
                tt_(ks, vp, kp, ALU.mult)
                link(tt_(four(vs), four(vp), four(kp)[:, :, ::-1, :], ALU.mult))
                tt_(kp[:, 0:2, :], four(ks)[:, :, 0, :], four(ks)[:, :, 1, :], ALU.subtract)
                link(tt_(kp[:, 2:4, :], four(vs)[:, :, 0, :], four(vs)[:, :, 1, :], ALU.add))
                tt_(zz[:, kt, 0:2, :], kp[:, 0::2, :], kp[:, 1::2, :], ALU.add)
                tt_(zz[:, kt, 2:4, :], kp[:, 0::2, :], kp[:, 1::2, :], ALU.subtract).then_inc(z_made, 1)
            dve.wait_ge(k_cp, NK + 1)
            dve.wait_ge(z_made, NK)
            tt_(kp[:, 0:2, :], vs[:, 0:2, :], ks[:, 0:2, :], ALU.mult)
            link(tt_(kp[:, 2:4, :], vs[:, 0:2, :], ks[:, 1::-1, :], ALU.mult))
            tt_(yp[:, 0, :], kp[:, 0, :], kp[:, 1, :], ALU.subtract)
            tt_(yp[:, 1, :], kp[:, 2, :], kp[:, 3, :], ALU.add).then_inc(z_made, 1)

            for c in range(CA):
                s = c % 2
                vf = vf_in[s]
                dve.wait_ge(vf_in_s[s], 16 * (c // 2 + 1))
                dve.wait_ge(xg_in_s[s], 16 * (c // 2 + 1))
                link(tscal(vf, vf, col[:, R_SKIP + c:R_SKIP + c + 1], None, ALU.mult))
                dve.wait_ge(i_mm, c + 1)
                for odd in range(2):
                    stt(vf[:, odd:LS:2], bank[:, 3 * s + odd, :], rnorm[:, c:c + 1], vf[:, odd:LS:2], ALU.mult, ALU.add)
                link(stt(vf[:, LS:TOK], bank[:, 3 * s + 2, 0:P], rnorm[:, CA + c:CA + c + 1], vf[:, LS:TOK], ALU.mult, ALU.add))
                tt_(yT[:, c, :], vf, xg_in[s], ALU.mult).then_inc(i_done, 1)

            def gate_rows(l):
                for n in range(4):
                    grp, h = divmod(n, 2)
                    if n:
                        dve.wait_ge(dg_mm, 4 * l + n)
                    for a in range(4):
                        last = tscal(diag[:, a, :], ident[:, :], modc[:, 24 * l + 16 + 4 * h + a, grp:grp + 1], None, ALU.mult)
                    last.then_inc(dg_made, 1)
                    dve.wait_ge(dg_mm, 4 * l + n + 1)
                    nc.vector.tensor_copy(gateb[:, grp, h * 512:(h + 1) * 512], bank[:, 6, :]).then_inc(gb_cp, 1)

            dve.wait_ge(i_done, CA)
            dve.wait_ge(st_ckv, 16)
            gate_rows(0)

            with dve.Fori(0, HEADS // 2) as i:
                link.loop(i, 2 * (3 + 2 * NT))
                nc.vector.tensor_copy(vpair, vall[:, :, bass.ds(i * P, P)]).then_inc(v_pair, 1)

                def queries(s):
                    for n in range(3):
                        dve.wait_ge(pj_mm, i * 14 + (7 * s + 1 + n))
                        b, a = 3 + n, KS3 * n
                        w = min(KS3, LS - a)
                        if n:
                            dve.wait_ge(pj_q, i * 6 + (3 * s + n))
                        nc.vector.tensor_copy(qT[s][0:NOPE, a:a + KS3], bank[0:NOPE, b, 0:KS3])
                        if w < KS3:
                            nc.vector.tensor_copy(qT[s][64:96, a + w:a + KS3], bank[64:96, b, w:KS3])
                        tt_(qT[s][64:96, a:a + w], bank[64:96, b, 0:w], rope_q[64:96, a:a + w], ALU.mult)
                        link(tt_(rtmp[64:96, 0:w], bank[96:128, b, 0:w], rope_q[96:128, a:a + w], ALU.mult))
                        tt_(qT[s][64:96, a:a + w], qT[s][64:96, a:a + w], rtmp[64:96, 0:w], ALU.add).then_inc(pj_q, 1)

                queries(0)
                for s in range(2):
                    def maxima(t):
                        dve.wait_ge(s_mm, i * 18 + (9 * s + t + 1))
                        b0, m = 3 * (t % 2), t % 2
                        src = bank[:, b0:b0 + 3, 0:KS3] if t < PROMPT else bank[:, b0, 0:P]
                        link(nc.vector.tensor_reduce(amax[:, m:m + 1], src, mybir.AxisListType.XY if t < PROMPT else mybir.AxisListType.X, ALU.max))
                        tscal(nmax[:, m:m + 1], amax[:, m:m + 1], -SCALE, None, ALU.mult).then_inc(s_max, 1)

                    def norm(t):
                        m, w = t % 2, KEYS if t < PROMPT else P
                        dve.wait_ge(s_exp, i * 18 + (9 * s + t + 1))
                        link(nc.vector.reciprocal(rinv[:, m:m + 1], rsum[:, m:m + 1]))
                        tscal(px[m][:, 0:w], px[m][:, 0:w], rinv[:, m:m + 1], None, ALU.mult).then_inc(p_norm, 1)

                    def outputs(t):
                        dve.wait_ge(o_mm, i * 18 + (9 * s + t + 2))
                        r, a = slice(s * VD, (s + 1) * VD), t * P
                        tt_(yT[r, bass.ds(i + CA, 1), a:a + P].rearrange("p a n -> p (a n)"), bank[r, 5 - 3 * (t % 2), KS3:KS3 + P], sgate[r, a:a + P], ALU.mult).then_inc(o_cp, 1)

                    maxima(0)
                    norm(0)
                    dve.wait_ge(sg_in, i * 16 + 16)
                    for t in range(NT):
                        if t < PROMPT:
                            maxima(t + 1)
                            u = 9 * s + t
                            dve.wait_ge(pt_mm_d, i * 16 + (8 * s + t + 1))
                            dve.wait_ge(o_mm, i * 18 + (u if t >= 2 else 9 * s + 1))
                            nc.vector.tensor_copy(pT[t % 2][:, 7:9, :], bank[:, 3 * (t % 2):3 * (t % 2) + 2, KS3:KS3 + P]).then_inc(pt_cp_d, 1)
                        if t:
                            outputs(t - 1)
                        if t < PROMPT:
                            norm(t + 1)
                            if s == 0 and t == PROMPT - 1:
                                queries(1)
                    outputs(PROMPT)
            link.end(HEADS // 2)

            def out_los(l):
                def y_lo(t):
                    if t >= 2:
                        dve.wait_ge(g_mm, NT * l + t - 1)
                    dve.wait_ge(y_his, NT * l + t + 1)
                    hi, lo = y_sl[l][t % 2]
                    tt_(lo, y_in[l][:, :, t * P:(t + 1) * P], hi.bitcast(F32), ALU.subtract).then_inc(y_los, 1)

                y_lo(0)
                for h in range(2):
                    for k in range(0, KT, 2):
                        dve.wait_ge(wo_his, 8 * l + 4 * h + k // 2 + 1)
                        a = 512 * h
                        hi, lo = wo[l]
                        tt_(lo[:, k:k + 2, a:a + 512], wo_raw[l][:, k:k + 2, a:a + 512], hi[:, k:k + 2, a:a + 512].bitcast(F32), ALU.subtract).then_inc(wo_los, 1)
                    if h == 0:
                        y_lo(1)
                x = x_res[l]
                for t in range(NT):
                    if t + 2 < NT:
                        y_lo(t + 2)
                    grp = int(t == PROMPT)
                    dve.wait_ge(x_in[t], 32 * (l + 1))
                    dve.wait_ge(g_mm, NT * l + t + 1)
                    b = 2 * (t % 2)
                    g_y = gy[l][t % 2]
                    link(tt_(split(g_y, 2), bank[:, b:b + 2, :], split(gateb[:, grp, :], 2), ALU.mult))
                    tt_(x[:, t, :], x[:, t, :], g_y, ALU.add).then_inc(g_add, 1)

            out_los(0)
            dve.wait_ge(g_add, NT)
            gate_rows(1)
            for t in range(NT):
                dve.wait_ge(x_rs, NT + t + 1)
                dve.wait_ge(x_in[t], 48)
                tscal(xs[:, t, :], xs[:, t, :], rstd[:, NT + t:NT + t + 1], None, ALU.mult).then_inc(x_n, 1)
            layer_input(1)

            def o_split_lo(j, g):
                dve.wait_ge((uw_his, gw_his)[j], g + 1)
                tt_(o_lo[j], o_raw[j], o_hi[j].bitcast(F32), ALU.subtract).then_inc((uw_los, gw_los)[j], 1)

            o_split_lo(1, 0)
            o_split_lo(0, 0)

            def fourier(g, final):
                link.loop(g, 2)
                for n in (0, 2, 4):
                    dve.wait_ge(ab_mm, g * 5 + (n + 1))
                    w = 2 if n < 4 else 1
                    nc.vector.tensor_copy(ab[:, 2 * n:2 * n + w, :], split(bank[:, 6, 0:256 * w], w)).then_inc(ab_e, 1)
                dve.wait_ge(cd_cp, g + 1)
                for q in range(2):
                    tt_(tt[:, 2 * q, :], bank[:, q, 0:FQ], cd[:, q, :], ALU.add)
                    last = tt_(tt[:, 2 * q + 1, :], bank[:, q, 0:FQ], cd[:, q, :], ALU.subtract)
                link(last)
                tt_(y1T[:, bass.ds(g, 1), LS:TOK].rearrange("p a n -> p (a n)"), bank[:, 7, 0:P], sg[:, LS:TOK], ALU.mult).then_inc(y_rel, 1)
                if not final:
                    o_split_lo(1, g + 1)
                n = HALF // 2
                tt_(yt[:, 0:n + 1], tt[:, 0, 0:n + 1], tt[:, 2, 0:n + 1], ALU.add)
                tt_(yt[:, 2 * n:n:-1], tt[:, 1, 0:n], tt[:, 3, 0:n], ALU.subtract)
                tt_(yt[:, 2 * n + 1:3 * n + 1], tt[:, 1, 1:n + 1], tt[:, 3, 1:n + 1], ALU.add)
                link(tt_(yt[:, 4 * n - 1:3 * n:-1], tt[:, 0, 1:n], tt[:, 2, 1:n], ALU.subtract))
                tt_(y1T[:, bass.ds(g, 1), 0:LS].rearrange("p a n -> p (a n)"), yt[:, 0:LS], sg[:, 0:LS], ALU.mult).then_inc(y_done, 1)
                if not final:
                    o_split_lo(0, g + 1)

            with dve.Fori(0, GROUPS - 1) as g:
                fourier(g, False)
            fourier(GROUPS - 1, True)
            link.end(GROUPS)

            out_los(1)
            dve.wait_ge(fg_in, 16)
            for t in range(NT):
                dve.wait_ge(x_rs, 2 * NT + t + 1)
                stt(xo[:, t, :], xo[:, t, :], rstd[:, 2 * NT + t:2 * NT + t + 1], fgb, ALU.mult, ALU.mult).then_inc(out_ready, 1)

        @block.gpsimd
        def _(pool):
            link = Chain(pool, pool_done)
            link(nc.gpsimd.memset(ident[:, :], 0.0))
            nc.gpsimd.affine_select(out=ident[:, :], in_=ident[:, :], compare_op=ALU.not_equal, fill=1.0, base=0,
                                    pattern=[[-1, P]], channel_multiplier=1).then_inc(consts_made, 1)
            nc.gpsimd.memset(ones[:, :], 1.0).then_inc(consts_made, 1)
            nc.gpsimd.memset(half_neg[:, :], -0.5).then_inc(consts_made, 1)
            pool.wait_ge(consts_made, 3)

            def inverse_root(dst, src, n, width):
                link(nc.gpsimd.tensor_scalar(src, src, 1.0 / n, EPS, ALU.mult, ALU.add))
                return nc.gpsimd.tensor_tensor(dst, src, half_neg[:, 0:width], ALU.pow)

            def row_norms(l):
                for t in range(NT):
                    a = NT * l + t
                    pool.wait_ge(x_sq, a + 1)
                    inverse_root(rstd[:, a:a + 1], ssq[:, a:a + 1], D, 1).then_inc(x_rs, 1)

            row_norms(0)
            for t in range(NT):
                pool.wait_ge(l_sq, t + 1)
                inverse_root(rstd2[:, 2 * t:2 * t + 2], ssq2[:, 2 * t:2 * t + 2], RANK, 2).then_inc(l_rs, 1)
            for t in range(NT):
                pool.wait_ge(fh_abs, t + 1)
                nc.gpsimd.tensor_tensor(sd[:, t, 0, :], f_h[t % 2][:, 0, :], f_h[t % 2][:, 1, :], ALU.add)
                nc.gpsimd.tensor_tensor(sd[:, t, 1, :], f_h[t % 2][:, 0, :], f_h[t % 2][:, 1, :], ALU.subtract).then_inc(sd_made, 1)
            pool.wait_ge(sp_g, 16 * (CA + 1))
            for kt in range(NK):
                pool.wait_ge(k_cp, kt + 1)
                nc.gpsimd.tensor_tensor(kp[:, 0:2, :], ks[:, 0:2, :], ks[:, 2:4, :], ALU.add)
                nc.gpsimd.tensor_tensor(kp[:, 2:4, :], ks[:, 0:2, :], ks[:, 2:4, :], ALU.subtract).then_inc(kp_made, 1)
            pool.wait_ge(i_done, CA)
            for m in (qT[0], qT[1], kT[0], kT[1]):
                link(nc.gpsimd.memset(m[QK:P, :], 0.0))
            pool.sem_inc(pads_made, 1)
            row_norms(1)
            row_norms(2)


def tables():
    f = np.float32
    out = {}

    def positions(L):
        n = np.arange(L)
        t = np.linspace(0.0, 1.0, L)[:, None]
        w = 2 * math.pi * n[:, None] / L
        fr = np.linspace(1e-4, BANDS - 1, BANDS)[None, :]
        z = np.concatenate([t, np.cos(fr * w), -np.sin(fr * w)], axis=-1)
        lo, hi = math.log(1e-2) / 1.5, math.log(1e-2) / 0.3
        return z, np.exp(-t * np.abs(np.linspace(lo, hi, DA)))

    zs, ds = positions(LS)
    zp, dp = positions(LP)
    z = np.concatenate([zs[0::2], zs[1::2], zp])
    dec = np.concatenate([ds[0::2], ds[1::2], dp])
    out["zT"] = z.T.astype(f)
    out["decay"] = dec.reshape(NT, P, DA).transpose(1, 0, 2).astype(f)
    k = np.arange(HALF)
    par = [np.arange(0, LS, 2), np.arange(1, LS, 2)]
    ang = [np.outer(n, math.pi * (2 * k + 1) / (2 * LS)) for n in par]
    quad = np.stack([np.cos(ang[0]), -np.sin(ang[0]), np.cos(ang[1]), -np.sin(ang[1])])
    out["tf"] = quad.reshape(4, NK, P, NK, P).transpose(3, 2, 0, 1, 4).astype(f)
    out["ti"] = (quad / LS).transpose(2, 0, 1).reshape(NK, P, 4, HALF).transpose(1, 0, 2, 3).astype(f)
    n = np.arange(LP)
    a = np.outer(n, math.pi * (2 * n + 1) / (2 * LP))
    pair = np.stack([np.cos(a), -np.sin(a)])
    out["tp"] = pair.transpose(1, 0, 2).astype(f)
    out["tpi"] = (pair / LP).transpose(2, 0, 1).astype(f)
    t = np.arange(LS)
    inv = 10000.0 ** (-np.arange(0, ROPE // 2, 2) / (ROPE // 2))
    an = np.stack([(t // GRID_W)[:, None] * inv, (t % GRID_W)[:, None] * inv], axis=1)
    cos = np.repeat(np.cos(an)[:, :, None, :], 2, axis=2).reshape(LS, ROPE)
    sin = np.stack([-np.sin(an), np.sin(an)], axis=2).reshape(LS, ROPE)
    both = np.stack([cos, sin])
    out["rope_t"] = both.reshape(2, LS // P, P, ROPE).transpose(2, 0, 1, 3).reshape(P, 2, 256).astype(f)
    out["rope_q"] = both.transpose(0, 2, 1).reshape(2 * ROPE, LS).astype(f)
    kk = np.arange(FQ)
    quad = []
    for nn in par:
        x = 2 * math.pi * np.outer(nn, kk) / LS
        quad += [np.cos(x), -np.sin(x)]
    quad = np.stack(quad) / math.sqrt(LS * P)
    out["tl"] = quad.reshape(4, NK, P, FQ).transpose(2, 1, 0, 3).astype(f)
    x = 2 * math.pi * np.outer(n, n) / P
    out["cg"] = np.concatenate([np.cos(x), np.sin(x)], axis=1).astype(f)
    out["tlp"] = (np.stack([np.cos(x), -np.sin(x)]) / math.sqrt(LP * P)).transpose(1, 0, 2).astype(f)
    return {name: np.ascontiguousarray(v) for name, v in out.items()}


def layout(inputs):
    i = {k: np.asarray(v) for k, v in inputs.items()}
    out = {}
    out["x_sample"], out["x_prompt"] = i["x_sample"][0], i["x_prompt"][0]
    out["vecs"] = np.concatenate([i["b_mod"].reshape(48, P), i["norm_g"].reshape(16, P), i["conv_w"].reshape(36, P),
                                  i["conv_b"].reshape(12, P), i["hyena_skip"].reshape(4, P)])
    out["cond"] = np.concatenate([i["c"].reshape(8, P), i["c_ctx"].reshape(8, P)])
    out["w_mod"] = i["w_mod"].reshape(2, KT, P, 6, 512).transpose(0, 3, 2, 1, 4).reshape(12, P, KT, 512)
    w = i["w_in_e"][0].reshape(KT, P, -1).transpose(1, 0, 2)
    tile = lambda a, n: w[:, :, a:a + n * P].reshape(P, KT, n, P).transpose(2, 0, 1, 3)
    out["w_in"] = np.stack([tile(DA, CA), tile(2 * DA, CA), tile(0, CA), tile(3 * DA, CA), tile(4 * DA + LAT, CA)])
    out["w_lat"] = w[:, :, 4 * DA:4 * DA + LAT]
    out["qg"], out["kvg"], out["final_g"] = i["q_norm_g"][0], i["kv_norm_g"][0], i["final_g"]
    out["cache_ckv"], out["cache_krope"] = i["cache_ckv"][0, 0], i["cache_krope"][0, 0]
    out["f_w1"], out["f_w2"], out["f_w3"] = i["filt_w1"][0], i["filt_w2"][0], i["filt_w3"][0]
    out["f_b"] = np.stack([i["filt_b1"][0], i["filt_b2"][0]], axis=1)
    q = i["w_uq"][0].reshape(RANK, HEADS, QK)
    rope = q[:, :, NOPE:].reshape(RANK, HEADS, 2, 2, 8)[:, :, :, ::-1, :].reshape(RANK, HEADS, ROPE)
    q = np.concatenate([q, rope], axis=2)
    out["w_q"] = q.reshape(2, P, HEADS, P).transpose(2, 1, 0, 3)
    kv = i["w_ukv"][0].reshape(2, P, HEADS, NOPE + VD)
    out["w_k"] = kv[..., 0:NOPE].transpose(2, 1, 0, 3)
    out["w_v"] = kv[..., NOPE:].transpose(1, 0, 2, 3).reshape(P, 2, HEADS * VD)
    out["w_oe"] = i["w_out_e"][0].reshape(KT, P, D).transpose(1, 0, 2)
    out["w_io"] = i["w_in_o"][0].reshape(KT, P, 2, GROUPS, P).transpose(2, 3, 1, 0, 4)
    out["fnet_w"] = i["fnet_w"][0]
    out["w_oo"] = i["w_out_o"][0].reshape(KT, P, D).transpose(1, 0, 2)
    return {name: np.ascontiguousarray(v) for name, v in out.items()}


OUTS = {"y_prompt": (LP, D), "y_sample": (LS, D), "state_ckv": (LP, RANK), "state_krope": (LP, ROPE)}
SPILLS = ("sp_v", "sp_x", "sp_g")


def kernel(**inputs):
    import concourse.bacc as bacc
    from concourse.bass_utils import run_bass_kernel_spmd

    nc = bacc.Bacc("TRN2", target_bir_lowering=False, num_devices=1)
    arrays = {**layout(inputs), **tables()}
    T = {n: nc.dram_tensor(f"{n}_in", a.shape, F32, kind="ExternalInput").ap() for n, a in arrays.items()}
    for n, shape in OUTS.items():
        T[n] = nc.dram_tensor(f"{n}_out", shape, F32, kind="ExternalOutput").ap()
    for n in SPILLS:
        T[n] = nc.dram_tensor(f"{n}_rows", (CA, P, TOK), F32, kind="Internal").ap()
    T["sp_1"] = nc.dram_tensor("sp_1_rows", (NT, P, D), F32, kind="Internal").ap()
    build(nc, T)
    r = run_bass_kernel_spmd(nc, [{f"{n}_in": a for n, a in arrays.items()}], core_ids=[0]).results[0]
    return (r["y_prompt_out"].reshape(1, LP, D), r["y_sample_out"].reshape(1, LS, D),
            r["state_ckv_out"].reshape(1, 1, LP, RANK), r["state_krope_out"].reshape(1, 1, LP, ROPE))
```

```python
import math
from contextlib import ExitStack

import numpy as np

import concourse.bass as bass
from concourse import mybir

F32 = mybir.dt.float32
F32R = mybir.dt.float32r
ALU = mybir.AluOpType
ACT = mybir.ActivationFunctionType

P = 128
D = 1024
KT = D // P
LS, LP = 1024, 128
TOK = LS + LP
NT = TOK // P
PROMPT = NT - 1
CHUNKS = [(0, 512), (512, 512), (1024, 128)]
T3 = TOK // 3
EPS = 1e-6
DA = 512
CA = DA // P
BANDS = 16
EMB = 2 * BANDS + 1
FO = 64
HEADS, NOPE, ROPE, VD, RANK = 8, 64, 32, 64, 256
QK = NOPE + ROPE
SCALE = 1.0 / math.sqrt(QK)
PAST = 128
KEYS = PAST + LS
ALLKEYS = KEYS + LP
KS3 = KEYS // 3
GRID_W = 64
HALF = LS // 2
NK = HALF // P
GROUPS = 8
FQ = HALF // 2 + 2
LAT = 2 * RANK + ROPE
STEPS = [("q0", "k0", "k1", "k2", "k3", "q1", "q2"), ("k0", "q0", "q1", "q2", "k1", "k2", "k3")]
STEP_BANK = [{"q0": 3, "q1": 6, "q2": 7, "k0": 1, "k1": 0, "k2": 2, "k3": 3}, {"q0": 3, "q1": 4, "q2": 5, "k0": 1, "k1": 0, "k2": 2, "k3": 3}]
OUT_BANK = [[5, 2, 5, 2, 5, 2, 5, 6, 7], [5, 2, 5, 2, 5, 2, 5, 5, 4]]
R_BMOD, R_NG, R_CW, R_CB, R_SKIP, R_ALL = 0, 48, 64, 100, 112, 116
MAGIC = 1.5 * 2.0 ** 23
TWO_PI_HI = 6.28125
TWO_PI_LO = float(np.float32(2 * math.pi - 6.28125))
PI_IN = 3.1415925


def build(nc, T):
    ctx = ExitStack()
    with ctx:
        place = [0]

        def sb(name, width, also_rounded=False):
            base = (nc.sbuf_base + 63) // 64 * 64 + 4 * place[0]
            place[0] += (width + 7) // 8 * 8
            plain = nc.alloc_sbuf_tensor_at(name, [P, width], F32, offset=base)
            return (plain, nc.alloc_sbuf_tensor_at(name + "_r", [P, width], F32R, offset=base)) if also_rounded else plain

        def sem(name):
            return ctx.enter_context(nc.semaphore(name))

        def sems(name, n):
            return [sem(f"{name}{i}") for i in range(n)]

        def split(ap, a):
            return ap.rearrange("p (a b) -> p a b", a=a)

        H, H_r = sb("H", 18432, True)
        H2 = 9216
        SCR, SCR_r = sb("SCR", 9600, True)
        WR, WR_r = sb("WR", 5120, True)
        KV, KV_r = sb("KV", 12544, True)
        WX, WX_r = sb("WX", 1024, True)
        KR_, VR = KV[:, 0:7424], KV[:, 7424:12544]
        bank = ctx.enter_context(nc.psum_tensor("bank", [P, 8, 512], F32))

        def banks(b, n, lo, hi):
            return bank[:, b:b + n, :].rearrange("p a n -> p (a n)")[:, lo:hi]

        ident = sb("ident", P)
        ones = sb("ones", P)
        half_neg = sb("half_neg", 2)
        vec_rows, cond_rows = WX[:, 0:P], WX[:, P:2 * P]
        col = sb("col", R_ALL)
        cond = split(sb("cond", 16)[:, :], KT)
        modc = split(sb("modc", 96)[:, :], 48)
        gsc = split(sb("gsc", 32)[:, :], 16)
        LATS = sb("LATS", 2048)
        lat_g = LATS[:, 0:512]
        lat = [LATS[:, 512 * i:512 * (i + 1)] for i in (1, 2)]
        rope_t = split(LATS[:, 1536:2048], 2)
        rope_q = sb("rope_q", LS)
        kro = split(sb("kro", 10 * ROPE)[:, :], 10)
        krs = split(sb("krs", 8 * ROPE)[:, :], 8)
        krr = split(sb("krr", 10 * ROPE)[:, :], 10)
        fw1 = sb("fw1", FO)
        fw2 = sb("fw2", FO)
        fb = sb("fb", 2)
        fw3 = sb("fw3", 2 * DA)
        tp = split(sb("tp", 2 * P)[:, :], 2)
        tpi = split(sb("tpi", 2 * P)[:, :], 2)
        ssq = sb("ssq", 3 * NT)
        rstd = sb("rstd", 3 * NT)
        ssq2 = sb("ssq2", 2 * NT)
        rstd2 = sb("rstd2", 2 * NT)
        rnorm = sb("rnorm", 2 * CA)
        amax = sb("amax", 2)
        nmax = sb("nmax", 2)
        rsum = sb("rsum", 2)
        rinv = sb("rinv", 2)

        wm = [split(H[:, 4096 * i:4096 * (i + 1)], KT) for i in range(3)]
        mod_rows = KR_[64:66, 0:3 * D]
        wm2 = split(WR[:, 2048:4096], KT)
        mod_rows2 = LATS[0:2, 0:6 * P]
        hT = [split(H_r[:, a:a + KT * TOK], KT) for a in (0, H2)]
        h_tmp = [KR_[:, 512 * i:512 * (i + 1)] for i in range(4)]
        w_lat_raw = split(VR[:, 0:KT * LAT], KT)
        w_lat = [split(WR_r[:, 768:5120], KT), split(KV_r[:, 7424:7424 + KT * LAT], KT)]
        sd = H[:, 0:NT * 2 * DA].rearrange("p (t s n) -> p t s n", t=NT, s=2)
        zz = H[:, H2:H2 + NK * 4 * DA].rearrange("p (k q n) -> p k q n", k=NK, q=4)
        yT = split(H[:, 0:KT * TOK], KT)
        y1T = split(SCR[:, 0:KT * TOK], KT)
        wo_raw = [split(H[:, a:a + KT * D], KT) for a in (H2, 0)]
        wo_hi = [[KV_r[:, D * k:D * (k + 1)] for k in range(KT)], [H_r[:, D * k:D * (k + 1)] for k in range(KT, 2 * KT)]]
        wo_lo = [[SCR_r[:, 4096 + D * k:4096 + D * (k + 1)] for k in range(5)] + [WX_r[:, :], WR_r[:, 0:D], WR_r[:, D:2 * D]],
                 [H_r[:, D * k:D * (k + 1)] for k in range(KT)]]
        WO_EARLY = 6
        y_in = [yT, y1T]
        y_sl = [[[split(m[:, a + 2048 * i + 1024 * j:a + 2048 * i + 1024 * (j + 1)], KT) for j in range(2)] for i in range(2)]
                for m, a in ((KV_r, KT * D), (WR_r, 0))]

        xs = split(SCR[:, 0:NT * D], NT)
        xr = [SCR[:, D * i:D * (i + 1)] for i in range(4)]
        u1 = SCR[:, 0:TOK]
        vt = SCR[:, TOK:2 * TOK]
        x0 = SCR[:, 2 * TOK:3 * TOK]
        ga = SCR[:, 3 * TOK:4 * TOK]
        gb = SCR[:, 4 * TOK:5 * TOK]
        f_z = KR_[:, 4864:4864 + TOK]
        f_x = KR_[:, 6144:6144 + TOK]
        f_r = KR_[:, 0:TOK]
        f_h = [split(SCR[:, 1024 * i:1024 * (i + 1)], 2) for i in range(2)]
        f_mag = [split(SCR[:, 2048 + 1024 * i:3072 + 1024 * i], 2) for i in range(2)]
        norm_rows = WX[0:1, 0:2 * DA]
        ks = split(SCR[:, 0:2048], 4)
        vs = split(SCR[:, 2048:4096], 4)
        kp = split(SCR[:, 4096:6144], 4)
        vp = split(SCR[:, 6144:8192], 4)
        yp = split(WX[:, 0:1024], 2)
        ti = [split(m, 4) for m in (WR[:, 0:2048], WR[:, 2048:4096], SCR[:, 0:2048], SCR[:, 2048:4096])]
        qT = [SCR[:, TOK * i:TOK * (i + 1)] for i in range(2)]
        q_lo = [SCR_r[:, TOK * i:TOK * (i + 1)] for i in range(2)]

        def q_hi(s, a, b):
            if s == 0:
                return [(WR_r[:, a:b], a, b)]
            out = []
            if a < LS:
                e = min(b, LS)
                out.append((WX_r[:, a:e], a, e))
            if b > LS:
                out.append((WR_r[:, 4864:4864 + b - LS], LS, b))
            return out

        px = [SCR[:, TOK * (2 + i):TOK * (3 + i)] for i in range(2)]
        pT = [split(SCR[:, TOK * (4 + i):TOK * (5 + i)], NT) for i in range(2)]
        sgate = SCR[:, TOK * 6:TOK * 7]
        vpair = split(SCR[:, TOK * 7:TOK * 7 + 10 * P], 10)

        w_raw = [split(SCR[:, 5 * TOK + 1024 * i:5 * TOK + 1024 * (i + 1)], KT) for i in range(3)]
        w_lo = [split(SCR_r[:, 5 * TOK + 1024 * i:5 * TOK + 1024 * (i + 1)], KT) for i in range(3)]
        w_hi = [split(m, KT) for m in (WX_r[:, :], WR_r[:, 0:1024], WR_r[:, 1024:2048])]
        o_raw = [split(WR[:, 1024 * i:1024 * (i + 1)], KT) for i in (0, 2)]
        o_lo = [split(WR_r[:, 1024 * i:1024 * (i + 1)], KT) for i in (0, 2)]
        o_hi = [split(WR_r[:, 1024 * i:1024 * (i + 1)], KT) for i in (1, 3)]
        decay = [WR[:, 2048 + DA * t:2048 + DA * (t + 1)] for t in range(6)] + [VR[:, 4608:5120], SCR[:, 8832:8832 + DA], WX[:, 0:DA]]
        tf = [WR[:, 2048 * i:2048 * (i + 1)].rearrange("p (q n k) -> p q n k", q=4, n=NK) for i in range(2)]
        vf_in = [SCR[:, 4096 + TOK * i:4096 + TOK * (i + 1)] for i in range(2)]
        xg_in = [SCR[:, 4096 + TOK * (2 + i):4096 + TOK * (3 + i)] for i in range(2)]
        w_v = split(H[:, 17408:18432], 2)
        w_q = [split(WR[:, 4096 + 256 * i:4352 + 256 * i], 2) for i in range(2)]
        w_k = [split(WR[:, 4608 + 128 * i:4736 + 128 * i], 2) for i in range(2)]
        rtmp = WR[:, 3712:4096]
        k_hi = [WR_r[:, TOK + 1280 * i:TOK + 1280 * (i + 1)] for i in range(2)]
        fw = WR[:, 4096:4224]
        csw = WR[:, 4224:4480]
        gateb = split(LATS[:, :], 2)
        diag = [[SCR[:, 4608:5120], SCR[:, 5120:5632]], [WR[:, 4608:5120], VR[:, 4608:5120]]]

        junk = [H[:, 16384 + 1024 * i:16384 + 1024 * (i + 1)] for i in range(2)]
        junk_l = [SCR[:, 256 * i:256 * (i + 1)] for i in range(2)]
        ckc = VR[:, 4352:4608]
        vtm = split(VR[:, 0:NT * DA], NT)
        vall = split(VR[:, :], 10)
        uT = VR[:, 0:TOK]
        sg = VR[:, TOK:2 * TOK]
        ab = split(VR[:, 2304:4608], NT)
        xo = split(KV[:, 0:NT * D], NT)
        fgb = KV[:, 9216:10240]

        cqT = split(KR_[:, 0:2304], 2)
        keysT = split(KR_[:, 2304:4864], 2)
        kT = [KR_[:, 4864 + 1280 * i:6144 + 1280 * i] for i in range(2)]
        k_lo = [KV_r[:, 4864 + 1280 * i:6144 + 1280 * i] for i in range(2)]
        tl = KR_[:, 0:16 * FQ].rearrange("p (n q k) -> p n q k", n=NK, q=4)
        cd = split(KR_[:, 4128:4644], 2)
        tt = split(KR_[:, 4644:5676], 4)
        yt = KR_[:, 5676:6828]
        cg = SCR[:, 9216:9472]
        tlp = split(KR_[:, 7084:7340], 2)

        consts_made = sem("consts_made")
        vec_in, small_in, wlat_in, ckc_in = sem("vec_in"), sem("small_in"), sem("wlat_in"), sem("ckc_in")
        vec_T, cond_made = sem("vec_T"), sem("cond_made")
        wm_in, wm_used, mod_made = sems("wm_in", 3), sem("wm_used"), sem("mod_made")
        mr_cp, mod_T = sem("mr_cp"), sem("mod_T")
        x_in = sems("x_in", NT)
        x_sq, x_rs, x_n = sem("x_sq"), sem("x_rs"), sem("x_n")
        x_T, h_full, h_hi, h_lo = sem("x_T"), sem("h_full"), sem("h_hi"), sem("h_lo")
        wl_hi, wl_lo = sem("wl_hi"), sem("wl_lo")
        l_mm, l_sq, l_rs, l_lat, l_T, l_cp = (sem(n) for n in ("l_mm", "l_sq", "l_rs", "l_lat", "l_T", "l_cp"))
        kr_rot, kr_T, kr_cp = sem("kr_rot"), sem("kr_T"), sem("kr_cp")
        st_state = sem("st_state")
        wr_in, d_mm, d_mid, d_rel = sems("wr_in", 5), sem("d_mm"), sem("d_mid"), sems("d_rel", 5)
        v_ready, v_T6, v_T7, v_rel6, v_rel7 = (sem(n) for n in ("v_ready", "v_T6", "v_T7", "v_rel6", "v_rel7"))
        xg_ready = sem("xg_ready")
        w_his, w_los = sem("w_his"), sem("w_los")
        sp_v, sp_x, sp_g = sem("sp_v"), sem("sp_x"), sem("sp_g")
        f_in, f_mm, f_red, f_sin = sem("f_in"), sem("f_mm"), sem("f_red"), sem("f_sin")
        dec_in, fh_mm, fh_made, fh_zero, sd_made = (sem(n) for n in ("dec_in", "fh_mm", "fh_made", "fh_zero", "sd_made"))
        nrm_mm, nrm_made, nrm_cp, nrm_T, sd_diff, z_in = (sem(n) for n in ("nrm_mm", "nrm_made", "nrm_cp", "nrm_T", "sd_diff", "z_in"))
        tf_in = sems("tf_in", 2)
        k_mm, k_cp, v_mm, v_cp, kp_made, z_made = (sem(n) for n in ("k_mm", "k_cp", "v_mm", "v_cp", "kp_made", "z_made"))
        fh_mag = sem("fh_mag")
        ti_in, vx_in, i_mm, i_done = sems("ti_in", 2), sems("vx_in", 2), sem("i_mm"), sem("i_done")
        wv_in, wq_in, v_all_mm, v_all_cp = sem("wv_in"), sems("wq_in", 2), sem("v_all_mm"), sem("v_all_cp")
        dg_made, dg_mm, gb_cp = sem("dg_made"), sem("dg_mm"), sem("gb_cp")
        pj_mm, pj_q, pj_k = sem("pj_mm"), sem("pj_q"), sem("pj_k")
        pq_cp = sem("pq_cp")
        kv_set, pads_made = sem("kv_set"), sem("pads_made")
        pk_his, pq_his, pq_los = (sem(n) for n in ("pk_his", "pq_his", "pq_los"))
        s_mm, s_max, s_exp, p_norm = sem("s_mm"), sem("s_max"), sem("s_exp"), sem("p_norm")
        pt_mm_a, pt_mm_d, pt_cp_a, pt_cp_d = sem("pt_mm_a"), sem("pt_mm_d"), sem("pt_cp_a"), sem("pt_cp_d")
        o_mm, o_cp, sg_in = sem("o_mm"), sem("o_cp"), sem("sg_in")
        wo_in, wo_his, wo_los = sems("wo_in", 2), sem("wo_his"), sem("wo_los")
        y_his, y_los = sem("y_his"), sem("y_los")
        uw_his, uw_los, gw_his, gw_los = sem("uw_his"), sem("uw_los"), sem("gw_his"), sem("gw_los")
        g_mm, g_add = sem("g_mm"), sem("g_add")
        tl_in = sem("tl_in")
        ow_in, fw_in = sems("ow_in", 2), sem("fw_in")
        csw_mm, csw_cp, u_mm, u_cp, gt_mm, gt_cp = (sem(n) for n in ("csw_mm", "csw_cp", "u_mm", "u_cp", "gt_mm", "gt_cp"))
        ab_mm, ab_e, ab_o = sem("ab_mm"), sem("ab_e"), sem("ab_o")
        y_mm, cd_cp, y_rel, y_done = sem("y_mm"), sem("cd_cp"), sem("y_rel"), sem("y_done")
        fg_in = sem("fg_in")
        out_ready, st_out = sem("out_ready"), sem("st_out")
        dve_done, pool_done = sem("dve_done"), sem("pool_done")

        block = ctx.enter_context(nc.Block())

        class Chain:
            def __init__(self, eng, s):
                self.eng, self.s, self.n, self.i, self.per, self.k = eng, s, 0, None, 0, 0

            def loop(self, i, per):
                self.i, self.per, self.k = i, per, 0

            def end(self, trips):
                assert self.k == self.per, self.k
                self.n += trips * self.per
                self.i = None

            def __call__(self, ins):
                ins.then_inc(self.s, 1)
                if self.i is None:
                    self.n += 1
                    self.eng.wait_ge(self.s, self.n)
                else:
                    self.k += 1
                    self.eng.wait_ge(self.s, self.i * self.per + self.n + self.k)

        @block.sync
        def _(sp):
            sp.dma_start(vec_rows[0:R_ALL, :], T["vecs"]).then_inc(vec_in, 16)
            sp.dma_start(cond_rows[0:16, :], T["cond"]).then_inc(vec_in, 16)
            for d, src in ((fw1[0:EMB, :], T["f_w1"]), (fw2[0:FO, :], T["f_w2"]), (fb[0:FO, :], T["f_b"]), (f_z[0:EMB, :], T["zT"])):
                sp.dma_start(d, src).then_inc(z_in, 16)
            for i in range(3):
                sp.dma_start(wm[i], T["w_mod"][i]).then_inc(wm_in[i], 16)
            for t in range(NT):
                src = T["x_prompt"] if t == PROMPT else T["x_sample"][t * P:(t + 1) * P, :]
                sp.dma_start(xs[:, t, :], src).then_inc(x_in[t], 16)
            for s in range(3):
                sp.wait_ge(wm_used, s + 1)
                sp.dma_start(wm[s], T["w_mod"][3 + s]).then_inc(wm_in[s], 16)
            sp.dma_start(w_lat_raw, T["w_lat"]).then_inc(wlat_in, 16)
            sp.dma_start(ckc, T["cache_ckv"]).then_inc(ckc_in, 16)
            smalls = [
                (lat_g[:, 0:RANK], T["qg"].partition_broadcast(P)), (lat_g[:, RANK:], T["kvg"].partition_broadcast(P)),
                (rope_t, T["rope_t"]), (rope_q[64:128, :], T["rope_q"]), (kro[:, 0, :], T["cache_krope"]),
            ]
            for d, s in smalls:
                sp.dma_start(d, s).then_inc(small_in, 16)
            sp.wait_ge(x_T, 24)
            for j in range(3):
                sp.dma_start(w_raw[j], T["w_in"][j, 0]).then_inc(wr_in[j], 16)
            fsm = [(fw3[0:FO, :], T["f_w3"]), (tp, T["tp"]), (tpi, T["tpi"])]
            for d, s in fsm:
                sp.dma_start(d, s).then_inc(f_in, 16)
            sp.wait_ge(l_lat, NT)
            sp.dma_start(T["state_ckv"], lat[PROMPT % 2][:, RANK:]).then_inc(st_state, 16)
            sp.dma_start(T["state_krope"], kro[:, 9, :]).then_inc(st_state, 16)
            def w_load(j, ahead, used, c):
                src = T["w_in"][j, ahead:CA][bass.ds(c, 1)].rearrange("a p k n -> p a k n")
                sp.wait_ge(d_mm, c * 5 + (used + 1))
                sp.dma_start(w_raw[j % 3].unsqueeze(1), src).then_inc(wr_in[j], 16)

            def m_load(m, ahead, c):
                src = T["w_mod2"][ahead:CA, m][bass.ds(c, 1)].rearrange("a p k n -> p a k n")
                sp.wait_ge(wm_used, c * 3 + (6 + m + 3 * ahead))
                sp.dma_start(wm2.unsqueeze(1), src).then_inc(wm_in[0], 16)

            sp.wait_ge(l_mm, NT)
            sp.dma_start(wm2, T["w_mod2"][0, 0]).then_inc(wm_in[0], 16)

            with sp.Fori(0, CA - 1) as i:
                w_load(3, 0, 0, i)
                m_load(1, 0, i)
                w_load(4, 0, 1, i)
                m_load(2, 0, i)
                w_load(2, 1, 2, i)
                w_load(0, 1, 3, i)
                m_load(0, 1, i)
                w_load(1, 1, 4, i)
            w_load(3, 0, 0, CA - 1)
            m_load(1, 0, CA - 1)
            w_load(4, 0, 1, CA - 1)
            m_load(2, 0, CA - 1)
            sp.wait_ge(wm_used, 6 + 3 * CA)
            for a, b in ((0, 6), (6, 7), (7, 8)):
                sp.dma_start(decay[a] if b == a + 1 else WR[:, 2048:5120], T["decay"][:, a:b, :].rearrange("p t n -> p (t n)")).then_inc(dec_in, 16)
            sp.wait_ge(d_mm, 5 * CA - 1)
            sp.dma_start(decay[PROMPT], T["decay"][:, PROMPT, :]).then_inc(dec_in, 16)
            sp.wait_ge(d_mm, 5 * CA)
            sp.dma_start(tf[0], T["tf"][0]).then_inc(tf_in[0], 16)
            sp.dma_start(w_v, T["w_v"]).then_inc(wv_in, 16)
            sp.wait_ge(fh_made, 4)
            sp.dma_start(tf[1], T["tf"][1]).then_inc(tf_in[1], 16)
            for s in range(2):
                sp.wait_ge(v_mm, s + 1)
                sp.dma_start(tf[s], T["tf"][2 + s]).then_inc(tf_in[s], 16)
            sp.wait_ge(fh_made, NT)
            for s in range(2):
                sp.dma_start(w_q[s], T["w_q"][s]).then_inc(wq_in[s], 16)
                sp.dma_start(w_k[s], T["w_k"][s]).then_inc(wq_in[s], 16)
            for s in range(2):
                sp.wait_ge(v_mm, NK - 1 + s)
                sp.dma_start(ti[s], T["ti"][:, s]).then_inc(ti_in[0], 16)
            sp.wait_ge(z_made, NK + 1)
            for s in (2, 3):
                sp.dma_start(ti[s], T["ti"][:, s]).then_inc(ti_in[1], 16)
            for m in (sp_v, sp_x, sp_g):
                sp.wait_ge(m, 16 * (CA + 1))
            for c in range(2):
                sp.dma_start(vf_in[c], T["sp_v"][c]).then_inc(vx_in[c], 16)
                sp.dma_start(xg_in[c], T["sp_x"][c]).then_inc(vx_in[c], 16)
            for c in range(2, CA):
                sp.wait_ge(i_done, c - 1)
                sp.dma_start(vf_in[c % 2], T["sp_v"][c]).then_inc(vx_in[c % 2], 16)
                sp.dma_start(xg_in[c % 2], T["sp_x"][c]).then_inc(vx_in[c % 2], 16)
            sp.wait_ge(i_done, CA)
            sp.dma_start(sgate, T["sp_g"][0]).then_inc(sg_in, 16)
            for h in range(2):
                sp.dma_start(wo_raw[0][:, :, 512 * h:512 * (h + 1)], T["w_oe"][:, :, 512 * h:512 * (h + 1)]).then_inc(wo_in[h], 16)
            with sp.Fori(1, HEADS // 2) as i:
                for s in range(2):
                    sp.wait_ge(pj_mm, i * 14 + (7 * s - 7))
                    sp.dma_start(w_q[s].unsqueeze(1), T["w_q"][bass.ds(i * 2 + s, 1)].rearrange("a p k n -> p a k n")).then_inc(wq_in[s], 16)
                    sp.dma_start(w_k[s].unsqueeze(1), T["w_k"][bass.ds(i * 2 + s, 1)].rearrange("a p k n -> p a k n")).then_inc(wq_in[s], 16)
                sp.wait_ge(o_cp, i * 18 + 1)
                sp.dma_start(sgate.unsqueeze(1), T["sp_g"][bass.ds(i, 1)].rearrange("a p n -> p a n")).then_inc(sg_in, 16)
            sp.wait_ge(o_cp, NT * HEADS + 1)

            def x_load(t):
                src = T["x_prompt"] if t == PROMPT else T["x_sample"][t * P:(t + 1) * P, :]
                sp.dma_start(xr[t % 4], src).then_inc(x_in[t], 16)

            for t in range(4):
                x_load(t)
            sp.dma_start(o_raw[1], T["w_io"][1, 0]).then_inc(ow_in[1], 16)
            sp.dma_start(cg, T["cg"]).then_inc(fw_in, 16)
            sp.dma_start(fw, T["fnet_w"][0]).then_inc(fw_in, 16)
            for t in range(NT):
                sp.wait_ge(g_add, t + 1)
                sp.dma_start(T["sp_1"][t], xr[t % 4]).then_inc(x_in[t], 16)
                if 4 <= t + 3 < NT:
                    sp.wait_ge(h_lo, 24 + t)
                    x_load(t + 3)
            sp.wait_ge(g_mm, NT)
            sp.dma_start(o_raw[0], T["w_io"][0, 0]).then_inc(ow_in[0], 16)
            for d, s in ((tl, T["tl"]), (tlp, T["tlp"])):
                sp.dma_start(d, s).then_inc(tl_in, 16)
            with sp.Fori(1, GROUPS) as i:
                for j in range(2):
                    sp.wait_ge((u_mm, gt_mm)[j], i)
                    sp.dma_start(o_raw[j].unsqueeze(1), T["w_io"][j, bass.ds(i, 1)].rearrange("a p k n -> p a k n")).then_inc(ow_in[j], 16)
                    if j == 0:
                        sp.wait_ge(csw_mm, i)
                        sp.dma_start(fw.unsqueeze(1), T["fnet_w"][bass.ds(i, 1)].rearrange("a p n -> p a n")).then_inc(fw_in, 16)
            sp.wait_ge(gt_mm, GROUPS)
            for h in range(2):
                sp.dma_start(wo_raw[1][:, :, 512 * h:512 * (h + 1)], T["w_oo"][:, :, 512 * h:512 * (h + 1)]).then_inc(wo_in[h], 16)
            sp.wait_ge(y_done, GROUPS + 1)
            for t in range(NT):
                sp.dma_start(xo[:, t, :], T["sp_1"][t]).then_inc(x_in[t], 16)
            sp.dma_start(fgb, T["final_g"].partition_broadcast(P)).then_inc(fg_in, 16)
            for t in range(NT):
                sp.wait_ge(out_ready, t + 1)
                dst = T["y_prompt"] if t == PROMPT else T["y_sample"][t * P:(t + 1) * P, :]
                sp.dma_start(dst, xo[:, t, :]).then_inc(st_out, 16)
            sp.wait_ge(st_out, 16 * NT)
            sp.wait_ge(st_state, 32)

        @block.tensor
        def _(pe):
            def product(out, pairs):
                for n, (l, r) in enumerate(pairs):
                    last = nc.tensor.matmul(out, l, r, start=(n == 0), stop=(n == len(pairs) - 1))
                return last

            def product3(out, pairs):
                return product(out, [(l[a], r[b]) for l, r in pairs for a, b in ((0, 0), (0, 1), (1, 0))])

            pe.wait_ge(consts_made, 3)
            pe.wait_ge(vec_in, 32)
            nc.tensor.transpose(bank[:, 7, 0:R_ALL], vec_rows[0:R_ALL, :], ident[0:R_ALL, 0:R_ALL])
            nc.tensor.transpose(bank[:, 7, P:P + 16], cond_rows[0:16, :], ident[0:16, 0:16]).then_inc(vec_T, 1)
            pe.wait_ge(z_in, 64)
            def hidden(w, rows):
                for n, (a, width) in enumerate(CHUNKS):
                    last = nc.tensor.matmul(bank[0:FO, 4 + n, 0:width], w[0:rows, :], f_z[0:rows, a:a + width], start=True, stop=True)
                last.then_inc(f_mm, 1)

            hidden(fw1, EMB)
            pe.wait_ge(cond_made, 1)
            for n in range(6):
                if n == 1:
                    pe.wait_ge(f_sin, 1)
                    hidden(fw2, FO)
                pe.wait_ge(wm_in[n % 3], 16 * (n // 3 + 1))
                if n >= 3:
                    pe.wait_ge(mr_cp, n - 2)
                product(bank[0:2, n % 3, :], [(cond[:, k, :], wm[n % 3][:, k, :]) for k in range(KT)]).then_inc(wm_used, 1)
            pe.wait_ge(mr_cp, 6)
            for n in range(24):
                last = nc.tensor.transpose(bank[:, 0, 2 * n:2 * n + 2], mod_rows[:, n * P:(n + 1) * P], ident[64:66, 64:66])
            last.then_inc(mod_T, 1)

            def layer_input_T():
                e = 0
                for ch, (_, width) in enumerate(CHUNKS):
                    tiles = range(4 * ch, 4 * ch + width // P)
                    pe.wait_ge(x_n, tiles[-1] + 1)
                    for k in range(KT):
                        if e >= 6:
                            pe.wait_ge(h_full, e - 5)
                        for n, t in enumerate(tiles):
                            last = nc.tensor.transpose(bank[:, 1 + e % 6, n * P:(n + 1) * P], xs[:, t, k * P:(k + 1) * P], ident[:, :])
                        last.then_inc(x_T, 1)
                        e += 1

            layer_input_T()
            pe.wait_ge(h_lo, 24)
            pe.wait_ge(wl_lo, 1)
            pe.wait_ge(ckc_in, 16)
            for j in range(2):
                last = nc.tensor.transpose(bank[:, 6, j * P:(j + 1) * P], ckc[:, j * P:(j + 1) * P], ident[:, :])
            last.then_inc(l_T, 1)

            def lat_T(t):
                pe.wait_ge(l_lat, t + 1)
                if t >= 2:
                    pe.wait_ge(l_cp, t)
                for j in range(4):
                    last = nc.tensor.transpose(bank[:, 4 + t % 2, j * P:(j + 1) * P], lat[t % 2][:, j * P:(j + 1) * P], ident[:, :])
                last.then_inc(l_T, 1)

            for t in range(NT):
                if t >= 2:
                    pe.wait_ge(l_lat, t - 1)
                for j, (a, b) in enumerate(((0, RANK), (RANK, LAT))):
                    last = product3(bank[:, 2 * (t % 2) + j, 0:b - a],
                                    [([m[:, k, t * P:(t + 1) * P] for m in hT], [m[:, k, a:b] for m in w_lat]) for k in range(KT)])
                last.then_inc(l_mm, 1)
                if t:
                    lat_T(t - 1)
            lat_T(NT - 1)
            pe.wait_ge(kr_rot, 1)
            for t in range(10):
                last = nc.tensor.transpose(bank[0:ROPE, t // 4, (t % 4) * P:(t % 4 + 1) * P], krr[:, t, :], ident[:, :])
            last.then_inc(kr_T, 1)
            pe.wait_ge(l_cp, NT + 1)
            pe.wait_ge(kr_cp, 1)

            for s in (d_rel[3], d_rel[4], v_rel6, v_rel7):
                pe.sem_inc(s, 1)
            with pe.Fori(0, CA) as c:
                for j in range(5):
                    pe.wait_ge(w_los, c * 5 + (j + 1))
                    if j < 2:
                        pe.wait_ge(d_rel[4 - j], c + 1)
                    else:
                        pe.wait_ge(d_rel[j - 2], c + 1)
                    for n in range(3):
                        if j == 4 and n == 2:
                            pe.wait_ge(mr_cp, c * 3 + 9)
                        last = product3(bank[:, 3 * (j % 2) + n, 0:T3], [([m[j % 3][:, k, :] for m in (w_hi, w_lo)],
                                                                          [m[:, k, T3 * n:T3 * (n + 1)] for m in hT]) for k in range(KT)])
                    last.then_inc(d_mm, 1)
                    if j in (0, 1, 3):
                        m = (0, 1, None, 2)[j]
                        pe.wait_ge(wm_in[0], c * 48 + (48 + 16 * m))
                        pe.wait_ge(mr_cp, c * 3 + (6 + m))
                        if m < 2:
                            pe.wait_ge(v_rel7, c + 1)
                        else:
                            pe.wait_ge(v_rel7, c + 2)
                        if m == 0:
                            pe.wait_ge(mod_made, c + 2)
                        product(bank[0:2, 7, 0:2 * P], [(cond[:, k, :], wm2[:, k, :]) for k in range(KT)]).then_inc(wm_used, 1)
                    if j == 3:
                        pe.wait_ge(v_rel6, c * 2 + 2)
                        nc.tensor.transpose(bank[:, 6, 0:P], vt[:, LS:TOK], ident[:, :]).then_inc(v_T6, 1)
                    if j == 4:
                        for n in range(6):
                            last = nc.tensor.transpose(bank[:, 7, 2 * n:2 * n + 2], mod_rows2[:, n * P:(n + 1) * P], ident[0:2, 0:2])
                        last.then_inc(mod_T, 1)
                    if j == 2:
                        pe.wait_ge(v_ready, c + 1)
                        pe.wait_ge(mr_cp, c * 3 + 8)
                        for odd in range(2):
                            pe.wait_ge((v_rel6, v_rel7)[odd], c * (2 - odd) + 1)
                            for n in range(NK):
                                last = nc.tensor.transpose(bank[:, 6 + odd, n * P:(n + 1) * P], vt[:, 2 * P * n + odd:2 * P * (n + 1):2], ident[:, :])
                            last.then_inc((v_T6, v_T7)[odd], 1)

            pe.wait_ge(d_rel[4], CA + 1)
            pe.wait_ge(d_rel[3], CA + 1)
            pe.wait_ge(f_in, 48)
            pe.wait_ge(mod_made, 2 + CA)
            pe.wait_ge(f_sin, 2)
            pe.wait_ge(v_rel6, 2 * CA + 1)
            pe.wait_ge(v_rel7, CA + 1)

            def magnitude_sums(t):
                pe.wait_ge(fh_mag, t + 1)
                for j in range(2):
                    last = nc.tensor.matmul(bank[0:1, 6 + t // PROMPT, :], ones[:, 0:1], f_mag[t % 2][:, j, :],
                                            start=(t in (0, PROMPT) and j == 0), stop=(t >= PROMPT - 1 and j == 1))
                last.then_inc(nrm_mm, 1)

            for t in range(NT):
                if t >= 3:
                    pe.wait_ge(fh_made, t - 2)
                for j in range(2):
                    last = nc.tensor.matmul(bank[:, 2 * (t % 3) + j, :], f_z[0:FO, t * P:(t + 1) * P], fw3[0:FO, j * DA:(j + 1) * DA], start=True, stop=True)
                last.then_inc(fh_mm, 1)
                if t:
                    magnitude_sums(t - 1)
            magnitude_sums(PROMPT)

            pe.wait_ge(fh_made, NT)
            pe.wait_ge(sd_made, NT)
            pe.wait_ge(sd_diff, NT)
            for kt in range(NK):
                s = kt % 2
                pe.wait_ge(tf_in[s], 16 * (kt // 2 + 1))
                if kt:
                    pe.wait_ge(k_cp, kt)
                for q in range(4):
                    last = product(bank[:, q, :], [(tf[s][:, q, n, :], sd[:, n + NK * (q // 2), q % 2, :]) for n in range(NK)])
                last.then_inc(k_mm, 1)
                if kt:
                    pe.wait_ge(v_cp, kt)
                else:
                    pe.wait_ge(nrm_cp, 1)
                    for n in range(2 * CA):
                        last = nc.tensor.transpose(bank[:, 7, n:n + 1], norm_rows[:, n * P:(n + 1) * P], ident[0:1, 0:1])
                    last.then_inc(nrm_T, 1)
                    pe.wait_ge(nrm_made, 1)
                for q in range(4):
                    last = product(bank[:, 4 + q, :], [(tf[s][:, q, n, :], vtm[:, n + NK * (q // 2), :]) for n in range(NK)])
                last.then_inc(v_mm, 1)
            pe.wait_ge(k_cp, NK)
            for q in range(2):
                nc.tensor.matmul(bank[:, q, :], tp[:, q, :], sd[:, PROMPT, q, :], start=True, stop=True)
            for q in range(2):
                last = nc.tensor.matmul(bank[:, 2 + q, :], tp[:, q, :], vtm[:, PROMPT, :], start=True, stop=True)
            last.then_inc(k_mm, 1)

            def inverse(c, kts):
                b0 = (4, 0)[c % 2]
                for odd in range(2):
                    for kt in kts:
                        for q in range(2):
                            nc.tensor.matmul(bank[:, b0 + odd, :], zz[:, kt, 2 * odd + q, c * P:(c + 1) * P], ti[kt][:, 2 * odd + q, :],
                                             start=(kt == 0 and q == 0), stop=(kt == NK - 1 and q == 1))
                if kts[-1] == NK - 1:
                    product(bank[:, b0 + 2, 0:P], [(yp[:, q, c * P:(c + 1) * P], tpi[:, q, :]) for q in range(2)]).then_inc(i_mm, 1)

            pe.wait_ge(v_cp, NK)
            pe.wait_ge(z_made, NK - 1)
            pe.wait_ge(ti_in[0], 32)
            inverse(0, (0, 1))
            pe.wait_ge(k_cp, NK + 1)
            inverse(1, (0, 1))
            pe.wait_ge(z_made, NK + 1)
            pe.wait_ge(ti_in[1], 32)
            inverse(0, (2, 3))
            inverse(1, (2, 3))
            for c in range(2, CA):
                pe.wait_ge(i_done, c - 1)
                inverse(c, range(NK))

            pe.wait_ge(i_done, CA - 1)
            pe.wait_ge(wv_in, 16)
            def gate_row(l, n, b):
                pe.wait_ge(dg_made, 4 * l + n + 1)
                nc.tensor.matmul(bank[:, b, :], ones[:, :], diag[l][n % 2], start=True, stop=True).then_inc(dg_mm, 1)

            for t in range(10):
                if t >= 2:
                    pe.wait_ge(v_all_cp, t - 1)
                product(bank[:, 6 + t % 2, :], [(keysT[:, k, t * P:(t + 1) * P], w_v[:, k, :]) for k in range(2)]).then_inc(v_all_mm, 1)
                if t % 2 and t < 8:
                    gate_row(0, t // 2, t // 2)
            pe.wait_ge(v_all_cp, 10)
            pe.wait_ge(gb_cp, 4)

            for m in (pt_cp_a, o_cp, o_mm):
                pe.sem_inc(m, 1)
            with pe.Fori(0, HEADS // 2) as i:
                for s in range(2):
                    def project(s, *steps):
                        for name in steps:
                            if name == STEPS[s][0]:
                                pe.wait_ge(wq_in[s], i * 32 + 32)
                            if name == "q2" and s:
                                pe.wait_ge(o_cp, i * 18 + 8)
                            if name == "k2" and s:
                                pe.wait_ge(o_cp, i * 18 + 7)
                            if name == "k3":
                                pe.wait_ge(pj_q, i * 6 + (3 * s + 1))
                            n = int(name[1])
                            wt, src, m = (w_q[s], cqT, P) if name[0] == "q" else (w_k[s], keysT, NOPE)
                            a, w = KS3 * n, KS3 if n < 3 else P
                            product(bank[0:m, STEP_BANK[s][name], 0:w], [(wt[:, k, 0:m], src[:, k, a:a + w]) for k in range(2)]).then_inc(pj_mm, 1)

                    def scores(t):
                        if t >= 2:
                            pe.wait_ge(s_exp, i * 18 + (9 * s + t - 1))
                            pe.wait_ge(pt_cp_d, i * 16 + (8 * s + t - 1))
                        b0 = 3 * (t % 2)
                        if t % 3 == 0:
                            pe.wait_ge(pq_los, i * 6 + (3 * s + t // 3 + 1))
                        a = slice(t * P, (t + 1) * P)
                        q = (q_hi(s, a.start, a.stop)[0][0], q_lo[s][:, a])
                        k = (k_hi[s], k_lo[s])
                        if t < PROMPT:
                            for n in range(3):
                                if t == 0 and n != 1:
                                    pe.wait_ge(pj_k, i * 8 + (4 * s + max(n + 1, 2)))
                                if t == 1 and n and s:
                                    pe.wait_ge(pj_q, i * 6 + (4 + n))
                                if n == 1 and t == 1 and s == 0:
                                    pe.wait_ge(o_cp, i * 18 + (9 * s + 1))
                                if n == 2 and t > 2:
                                    pe.wait_ge(o_cp, i * 18 + (9 * s + t - 1))
                                last = product3(bank[:, b0 + n, 0:KS3], [(q, [m[:, n * KS3:(n + 1) * KS3] for m in k])])
                        else:
                            last = product3(bank[:, b0, 0:P], [(q, [m[:, KEYS:ALLKEYS] for m in k])])
                        last.then_inc(s_mm, 1)

                    def probs_T(t):
                        u = 9 * s + t
                        pe.wait_ge(p_norm, i * 18 + (u + 1))
                        pe.wait_ge(pt_cp_a, i * 18 + (u + 1))
                        if t < PROMPT:
                            for n in range(7, 9):
                                last = nc.tensor.transpose(bank[:, 3 * (t % 2) + n - 7, KS3:KS3 + P], px[t % 2][:, n * P:(n + 1) * P], ident[:, :])
                            last.then_inc(pt_mm_d, 1)
                        if t == 0 and s == 0:
                            pe.wait_ge(pj_q, i * 6 + 3)
                        elif t == 0:
                            pe.wait_ge(o_cp, i * 18 + 10)
                        for n in range(7 if t < PROMPT else 1):
                            last = nc.tensor.transpose(bank[:, 6 + n // 4, n % 4 * P:(n % 4 + 1) * P], px[t % 2][:, n * P:(n + 1) * P], ident[:, :])
                        last.then_inc(pt_mm_a, 1)

                    def outputs(s, t):
                        u = 9 * s + t
                        pe.wait_ge(pt_cp_a, i * 18 + (u + 2))
                        if t == 7:
                            if s == 0:
                                pe.wait_ge(pt_cp_a, i * 18 + (u + 3))
                            else:
                                pe.wait_ge(o_cp, i * 18 + (u + 1))
                        o = bank[:, OUT_BANK[s][t], KS3:KS3 + P]
                        if t < PROMPT:
                            pe.wait_ge(pt_cp_d, i * 16 + (8 * s + t + 1))
                            last = product(o, [(vpair[:, kt, :], pT[t % 2][:, kt, :]) for kt in range(9)])
                        else:
                            last = product(o, [(vpair[:, 9, :], pT[t % 2][:, 0, :])])
                        last.then_inc(o_mm, 1)

                    if s == 0:
                        project(0, "q0", "k0", "k1", "k2")
                        pe.wait_ge(kv_set, 2)
                        pe.wait_ge(pads_made, 7)
                    scores(0)
                    if s == 0:
                        project(0, "k3", "q1", "q2")
                    pe.wait_ge(pj_k, i * 8 + (4 * s + 4))
                    scores(1)
                    if s:
                        outputs(0, PROMPT - 1)
                        outputs(0, PROMPT)
                    probs_T(0)
                    for t in range(1, NT):
                        if t + 1 < NT:
                            scores(t + 1)
                        if s == 0 and t == PROMPT - 1:
                            project(1, "k0")
                        if s == 0 and t == PROMPT:
                            pe.wait_ge(pt_cp_d, i * 16 + 8)
                            project(1, "q0", "q1", "q2")
                        probs_T(t)
                        if t == 1 and s == 0:
                            pe.wait_ge(kv_set, i + 3)
                        if s == 0 and t == PROMPT:
                            project(1, "k1", "k2", "k3")
                        else:
                            outputs(s, t - 1)
                    if s:
                        outputs(1, PROMPT)
            pe.wait_ge(o_cp, NT * HEADS + 1)

            def next_input_T(t):
                pe.wait_ge(x_n, NT + t + 1)
                if t >= 2:
                    pe.wait_ge(h_full, 24 + t - 1)
                for k in range(KT):
                    last = nc.tensor.transpose(bank[:, 6 - 2 * (t % 2) + k // 4, k % 4 * P:(k % 4 + 1) * P], xr[t % 4][:, k * P:(k + 1) * P], ident[:, :])
                last.then_inc(x_T, 1)

            def out_product(l):
                for t in range(NT):
                    if t >= 2:
                        pe.wait_ge(g_add, NT * l + t - 1)
                        pe.wait_ge(x_sq, NT * (l + 1) + t - 1)
                    pe.wait_ge(y_los, NT * l + t + 1 + (l if t else 0))
                    for j in range(2):
                        for k in range(KT):
                            if l and t == j == 0 and k == KT - 1:
                                pe.wait_ge(y_los, NT + 2)
                            if t == 0:
                                pe.wait_ge(wo_los, 16 * l + 8 * j + k + 1)
                            for a, w in ((0, wo_hi), (0, wo_lo), (1, wo_hi)):
                                last = nc.tensor.matmul(bank[:, 2 * (t % 2) + j, :], y_sl[l][t % 2][a][:, k, :], w[l][k][:, j * 512:(j + 1) * 512],
                                                        start=(k == 0 and a == 0 and w is wo_hi), stop=(k == KT - 1 and a == 1))
                    last.then_inc(g_mm, 1)
                    if l == 0 and t:
                        next_input_T(t - 1)

            out_product(0)

            for m in (gt_cp, y_rel, y_done):
                pe.sem_inc(m, 1)

            def fourier(g, first=False, final=False):
                def third(j, n):
                    if first:
                        pe.wait_ge(h_lo, 24 + 3 * n + 3)
                    return product3(bank[:, 3 * j + n, 0:T3], [([m[j][:, k, :] for m in (o_hi, o_lo)],
                                                                [m[:, k, T3 * n:T3 * (n + 1)] for m in hT]) for k in range(KT)])

                pe.wait_ge(gw_los, g + 1)
                pe.wait_ge(gt_cp, g + 1)
                third(1, 0)
                if first:
                    pe.wait_ge(h_full, 24 + NT - 1)
                    third(1, 1)
                pe.wait_ge(fw_in, g * 16 + 32)
                pe.wait_ge(y_rel, g + 1)
                for q in range(2):
                    last = nc.tensor.matmul(bank[:, 7, q * P:(q + 1) * P], cg[:, q * P:(q + 1) * P], fw[:, :], start=True, stop=True)
                last.then_inc(csw_mm, 1)
                pe.wait_ge(uw_los, g + 1)
                for n in range(3):
                    if first and n == 1:
                        pe.wait_ge(csw_cp, 1)
                        next_input_T(PROMPT)
                    last = third(0, n)
                last.then_inc(u_mm, 1)
                if final:
                    pe.wait_ge(csw_cp, g + 1)
                    gate_row(1, 0, 6)
                    gate_row(1, 1, 7)
                for n in (1, 2):
                    if not (first and n == 1):
                        last = third(1, n)
                    if final and n == 1:
                        for m in (2, 3):
                            pe.wait_ge(gb_cp, 4 + m - 1)
                            gate_row(1, m, 4 + m)
                last.then_inc(gt_mm, 1)
                if final:
                    pe.wait_ge(gb_cp, 8)
                pe.wait_ge(u_cp, g + 1)
                pe.wait_ge(csw_cp, g + 1)
                for n in range(5):
                    if n >= 2:
                        pe.wait_ge(*((ab_e, g * 3 + n // 2) if n % 2 == 0 else (ab_o, g * 2 + 1)))
                    for m_ in range(2 if n < 4 else 1):
                        t = 2 * n + m_
                        if t < PROMPT:
                            odd, q = divmod(t, NK)
                            lhs = uT[:, 2 * P * q + odd:2 * P * (q + 1):2]
                        else:
                            lhs = uT[:, LS:TOK]
                        last = nc.tensor.matmul(bank[:, 6 + n % 2, m_ * 256:(m_ + 1) * 256], lhs, csw[:, :], start=True, stop=True)
                    last.then_inc(ab_mm, 1)
                pe.wait_ge(ab_e, g * 3 + 3)
                pe.wait_ge(ab_o, g * 2 + 2)
                if first:
                    pe.wait_ge(tl_in, 32)
                for q in range(4):
                    product(bank[:, (0, 1, 2, 6)[q], 0:FQ], [(ab[:, n + NK * (q // 2), (q % 2) * P:(q % 2 + 1) * P], tl[:, n, q, :]) for n in range(NK)])
                product(bank[:, 7, 0:P], [(ab[:, PROMPT, q * P:(q + 1) * P], tlp[:, q, :]) for q in range(2)]).then_inc(y_mm, 1)

            fourier(0, first=True)
            with pe.Fori(1, GROUPS - 1) as g:
                fourier(g)
            fourier(GROUPS - 1, final=True)
            pe.wait_ge(y_rel, GROUPS + 1)
            out_product(1)

        @block.scalar
        def _(act):
            act.wait_ge(vec_T, 1)
            nc.scalar.activation(cond.rearrange("p k g -> p g k"), split(bank[:, 7, P:P + 16], 2), ACT.Silu).then_inc(cond_made, 1)
            for n in range(2):
                act.wait_ge(f_red, n + 1)
                nc.scalar.activation(f_z[0:FO, :], f_x[0:FO, :], ACT.Sin).then_inc(f_sin, 1)

            def square(l, t, src, dump):
                nc.scalar.activation(dump, src, ACT.Square, accum_out=ssq[:, NT * l + t:NT * l + t + 1]).then_inc(x_sq, 1)

            def layer_input():
                for e in range(24):
                    ch, k = divmod(e, KT)
                    a, w = CHUNKS[ch]
                    grp = ch // 2
                    act.wait_ge(x_T, e + 1)
                    if e >= 4:
                        act.wait_ge(h_lo, e - 3)
                    tmp = h_tmp[e % 4][:, 0:w]
                    nc.scalar.activation(tmp, bank[:, 1 + e % 6, 0:w], ACT.Identity, scale=gsc[:, k, grp:grp + 1],
                                         bias=modc[:, k, grp:grp + 1]).then_inc(h_full, 1)
                    if e % 2 == 0:
                        act.wait_ge(h_full, e + 1)
                        nc.scalar.copy(hT[0][:, k, a:a + w], tmp).then_inc(h_hi, 1)

            def next_input(t):
                grp = int(t == PROMPT)
                act.wait_ge(mod_made, 3 + CA)
                act.wait_ge(x_T, 24 + t + 1)
                for k in range(KT):
                    last = nc.scalar.activation(xr[t % 4][:, k * P:(k + 1) * P], bank[:, 6 - 2 * (t % 2) + k // 4, k % 4 * P:(k % 4 + 1) * P], ACT.Identity,
                                                scale=gsc[:, 8 + k, grp:grp + 1], bias=modc[:, 24 + k, grp:grp + 1])
                last.then_inc(h_full, 1)
                act.wait_ge(h_full, 24 + t + 1)
                nc.scalar.copy(hT[0][:, :, t * P:(t + 1) * P], split(xr[t % 4], KT)).then_inc(h_hi, 1)

            def o_split_hi(j, g):
                act.wait_ge(ow_in[j], g * 16 + 16)
                nc.scalar.copy(o_hi[j], o_raw[j]).then_inc((uw_his, gw_his)[j], 1)

            def wo_split_hi(l, h, ks):
                act.wait_ge(wo_in[h], 16 * l + 16)
                a = slice(512 * h, 512 * (h + 1))
                for k in ks:
                    nc.scalar.copy(wo_hi[l][k][:, a], wo_raw[l][:, k, a]).then_inc(wo_his, 1)

            def y_split_hi(l, t, k0, k1):
                nc.scalar.copy(y_sl[l][t % 2][0][:, k0:k1, :], y_in[l][:, k0:k1, t * P:(t + 1) * P]).then_inc(y_his, 1)

            def out_his(l):
                def y_hi(t):
                    if t >= 2:
                        act.wait_ge(g_mm, NT * l + t - 1)
                    y_split_hi(l, t, 0, KT)

                if l:
                    wo_split_hi(l, 0, range(WO_EARLY, KT))
                    act.wait_ge(y_done, GROUPS + 1)
                    y_split_hi(l, 0, KT - 1, KT)
                else:
                    y_hi(0)
                    wo_split_hi(l, 0, range(KT))
                y_hi(1)
                wo_split_hi(l, 1, range(KT))
                for t in range(NT):
                    if t + 2 < NT:
                        y_hi(t + 2)
                    if l == 0 and t:
                        next_input(t - 1)
                    if l == 0 and t == 4:
                        o_split_hi(1, 0)
                    act.wait_ge(g_add, NT * l + t + 1)
                    b = 2 * (t % 2)
                    square(l + 1, t, split((xr[t % 4], xo[:, t, :])[l], 2), bank[:, b:b + 2, :])

            for t in range(NT):
                act.wait_ge(x_in[t], 16)
                if t >= 2:
                    act.wait_ge(x_sq, t - 1)
                square(0, t, xs[:, t, :], junk[t % 2])
            for n in range(6):
                act.wait_ge(wm_used, n + 1)
                nc.scalar.copy(mod_rows[:, n * 512:(n + 1) * 512], bank[0:2, n % 3, :]).then_inc(mr_cp, 1)
            act.wait_ge(mod_made, 2)
            layer_input()
            def w_split_hi(j, c, used):
                act.wait_ge(wr_in[j], c * 16 + 16)
                if j >= 3 or used == 3:
                    act.wait_ge(d_mm, (c - (j < 3)) * 5 + (used + 1))
                nc.scalar.copy(w_hi[j % 3], w_raw[j % 3]).then_inc(w_his, 1)

            act.wait_ge(l_T, 1)
            nc.scalar.copy(keysT[:, :, 0:P], split(bank[:, 6, 0:2 * P], 2)).then_inc(l_cp, 1)
            for t in range(NT + 1):
                if t < NT:
                    act.wait_ge(l_mm, t + 1)
                    if t:
                        act.wait_ge(l_sq, t)
                    for j in range(2):
                        last = nc.scalar.activation(junk_l[j], bank[:, 2 * (t % 2) + j, 0:RANK], ACT.Square,
                                                    accum_out=ssq2[:, 2 * t + j:2 * t + j + 1])
                    last.then_inc(l_sq, 1)
                if t:
                    act.wait_ge(l_T, t + 1)
                    src = bank[:, 4 + (t - 1) % 2, :].rearrange("p (a k n) -> p a k n", a=2, k=2)
                    nc.scalar.copy(cqT[:, :, (t - 1) * P:t * P], src[:, 0])
                    nc.scalar.copy(keysT[:, :, t * P:(t + 1) * P], src[:, 1]).then_inc(l_cp, 1)
            w_split_hi(0, 0, None)
            act.wait_ge(kr_T, 1)
            nc.scalar.copy(kT[0][64:96, :], bank[0:ROPE, 0:3, :].rearrange("p a n -> p (a n)")[:, 0:ALLKEYS])
            nc.scalar.copy(kT[1][64:96, :], bank[0:ROPE, 0:3, :].rearrange("p a n -> p (a n)")[:, 0:ALLKEYS]).then_inc(kr_cp, 1)

            def spill(c, ready, n, buf, dst, s):
                act.wait_ge(ready, c + n)
                act.dma_start(T[dst][bass.ds(c, 1)].rearrange("a p n -> p a n"), buf.unsqueeze(1)).then_inc(s, 16)

            for s in (sp_v, sp_x, sp_g):
                act.sem_inc(s, 16)

            act.wait_ge(st_state, 32)

            def mod_row(c, m):
                act.wait_ge(wm_used, c * 3 + (7 + m))
                nc.scalar.copy(mod_rows2[:, 2 * P * m:2 * P * (m + 1)], bank[0:2, 7, 0:2 * P]).then_inc(mr_cp, 1)

            def hyena_input(c, last):
                for j, (dst, m0) in enumerate(((u1, 4), (vt, 8), (x0, 0))):
                    if j == 0:
                        w_split_hi(1, c, None)
                    elif j == 1:
                        w_split_hi(2, c, None)
                    else:
                        w_split_hi(3, c, 0)
                    act.wait_ge(d_mm, c * 5 + (j + 1))
                    if j == 1:
                        act.wait_ge(sp_v, c * 16 + 16)
                    if j == 2:
                        act.wait_ge(sp_x, c * 16 + 16)
                    nc.scalar.activation(split(dst, 3), bank[:, 3 * (j % 2):3 * (j % 2) + 3, 0:T3], ACT.Identity, scale=col[:, bass.ds(c + (R_CW + 12 + m0), 1)],
                                         bias=col[:, bass.ds(c + (R_CB + m0), 1)]).then_inc(d_mid, 1)
                    if j < 2:
                        mod_row(c, j)
                for odd in range(2):
                    act.wait_ge((v_T6, v_T7)[odd], c * (2 - odd) + 1)
                    nc.scalar.copy(vtm[:, NK * odd:NK * (odd + 1), bass.ds(c * P, P)], split(bank[:, 6 + odd, :], NK)).then_inc((v_rel6, v_rel7)[odd], 1)
                spill(c, v_ready, 1, vt, "sp_v", sp_v)
                w_split_hi(4, c, 1)
                act.wait_ge(d_mm, c * 5 + 4)
                nc.scalar.activation(split(ga, 3), bank[:, 3:6, 0:T3], ACT.Silu).then_inc(d_rel[3], 1)
                mod_row(c, 2)
                act.wait_ge(v_T6, c * 2 + 2)
                nc.scalar.copy(vtm[:, PROMPT, bass.ds(c * P, P)], bank[:, 6, 0:P]).then_inc(v_rel6, 1)
                if not last:
                    w_split_hi(0, c + 1, 3)
                act.wait_ge(d_mm, c * 5 + 5)
                act.wait_ge(sp_g, c * 16 + 16)
                nc.scalar.activation(split(gb, 3), bank[:, 0:3, 0:T3], ACT.Silu).then_inc(d_rel[4], 1)
                spill(c, xg_ready, 1, x0, "sp_x", sp_x)
                spill(c, d_rel[4], 2, gb, "sp_g", sp_g)

            with act.Fori(0, CA - 1) as c:
                hyena_input(c, False)
            hyena_input(CA - 1, True)

            for t in range(NT):
                act.wait_ge(fh_made, t + 1)
                if t >= 2:
                    act.wait_ge(nrm_mm, t - 1)
                nc.scalar.activation(f_mag[t % 2], f_h[t % 2], ACT.Abs).then_inc(fh_mag, 1)
            act.wait_ge(nrm_mm, NT)
            act.wait_ge(fh_made, NT)
            nc.scalar.copy(split(norm_rows, 2), bank[0:1, 6:8, :]).then_inc(nrm_cp, 1)
            for kt in range(NK):
                act.wait_ge(k_mm, kt + 1)
                if kt:
                    act.wait_ge(z_made, kt)
                else:
                    act.wait_ge(sd_made, NT)
                    act.wait_ge(sd_diff, NT)
                nc.scalar.copy(ks, bank[:, 0:4, :]).then_inc(k_cp, 1)
                act.wait_ge(v_mm, kt + 1)
                nc.scalar.copy(vs, bank[:, 4:8, :]).then_inc(v_cp, 1)
            act.wait_ge(k_mm, NK + 1)
            act.wait_ge(z_made, NK)
            nc.scalar.copy(ks[:, 0:2, :], bank[:, 0:2, :])
            nc.scalar.copy(vs[:, 0:2, :], bank[:, 2:4, :]).then_inc(k_cp, 1)

            for t in range(10):
                act.wait_ge(v_all_mm, t + 1)
                nc.scalar.copy(vall[:, t, :], bank[:, 6 + t % 2, :]).then_inc(v_all_cp, 1)
                if t in (1, 3):
                    act.wait_ge(consts_made, 5)
                    act.wait_ge(i_mm, CA)
                    nc.scalar.copy(k_hi[t // 2][64:P, :], kT[t // 2][64:P, :]).then_inc(kr_cp, 1)
            act.wait_ge(pads_made, 7)
            with act.Fori(0, HEADS // 2) as i:
                def keys(s, *parts):
                    for n in parts:
                        name = f"k{n}"
                        act.wait_ge(pj_mm, i * 14 + (7 * s + 1 + STEPS[s].index(name)))
                        a, w = KS3 * n, KS3 if n < 3 else P
                        nc.scalar.copy(k_hi[s][0:NOPE, a:a + w], bank[0:NOPE, STEP_BANK[s][name], 0:w]).then_inc(pk_his, 1)

                def query_rows(s, *parts):
                    for n in parts:
                        name = f"q{n}"
                        act.wait_ge(pj_mm, i * 14 + (7 * s + 1 + STEPS[s].index(name)))
                        nc.scalar.copy(qT[s][0:NOPE, KS3 * n:KS3 * (n + 1)], bank[0:NOPE, STEP_BANK[s][name], 0:KS3]).then_inc(pq_cp, 1)

                def query_his(s, *parts):
                    for n in parts:
                        act.wait_ge(pj_q, i * 6 + (3 * s + n + 1))
                        for m, a, b in q_hi(s, KS3 * n, KS3 * (n + 1)):
                            last = nc.scalar.copy(m[0:QK], qT[s][0:QK, a:b])
                        last.then_inc(pq_his, 1)

                query_rows(0, 0)
                keys(0, 0)
                query_his(0, 0)
                keys(0, 1, 2)
                for s in range(2):
                    def exps(t):
                        act.wait_ge(s_max, i * 18 + (9 * s + t + 1))
                        b0 = 3 * (t % 2)
                        src, dst = (bank[:, b0:b0 + 3, 0:KS3], split(px[t % 2], 3)) if t < PROMPT else (bank[:, b0, 0:P], px[t % 2][:, 0:P])
                        nc.scalar.activation(dst, src, ACT.Exp, scale=SCALE, bias=nmax[:, t % 2:t % 2 + 1],
                                             accum_out=rsum[:, t % 2:t % 2 + 1]).then_inc(s_exp, 1)

                    if s == 0:
                        keys(0, 3)
                        query_rows(0, 1)
                    exps(0)
                    if s == 0:
                        query_rows(0, 2)
                    if s:
                        exps(1)
                    for t in range(NT):
                        u = 9 * s + t
                        if t == 0:
                            act.wait_ge(pt_mm_d, i * 16 + (8 * s + 1))
                            act.wait_ge(o_mm, i * 18 + (9 * s + 1))
                            nc.scalar.copy(pT[0][:, 7:9, :], bank[:, 0:2, KS3:KS3 + P]).then_inc(pt_cp_d, 1)
                        if s == 0 and t == PROMPT:
                            query_rows(1, 0, 1)
                        if 0 < t < PROMPT or t == s == 0:
                            exps(t + 1)
                        act.wait_ge(pt_mm_a, i * 18 + (u + 1))
                        act.wait_ge(o_mm, i * 18 + (u if t >= 2 else 9 * s + 1))
                        if t < PROMPT:
                            nc.scalar.copy(pT[t % 2][:, 0:7, :].rearrange("p a n -> p (a n)"), banks(6, 2, 0, 7 * P)).then_inc(pt_cp_a, 1)
                        else:
                            nc.scalar.copy(pT[t % 2][:, 0, :], bank[:, 6, 0:P]).then_inc(pt_cp_a, 1)
                        if t == 0:
                            query_his(s, 1, 2)
                        if s == 0 and t == PROMPT - 1:
                            keys(1, 0)
                    if s == 0:
                        query_his(1, 0)
                        keys(1, 1, 2)
                        keys(1, 3)
                        query_rows(1, 2)

            act.wait_ge(o_cp, NT * HEADS + 1)
            out_his(0)
            o_split_hi(0, 0)

            def fourier(g, first=False, last=False):
                act.wait_ge(csw_mm, g + 1)
                nc.scalar.copy(csw[:, :], bank[:, 7, 0:256]).then_inc(csw_cp, 1)
                if first:
                    next_input(PROMPT)
                act.wait_ge(u_mm, g + 1)
                nc.scalar.copy(split(uT, 3), bank[:, 0:3, 0:T3]).then_inc(u_cp, 1)
                if not last:
                    o_split_hi(0, g + 1)
                act.wait_ge(gt_mm, g + 1)
                act.wait_ge(y_done, g + 1)
                nc.scalar.activation(split(sg, 3), bank[:, 3:6, 0:T3], ACT.Silu).then_inc(gt_cp, 1)
                for n in (1, 3):
                    act.wait_ge(ab_mm, g * 5 + (n + 1))
                    nc.scalar.copy(ab[:, 2 * n:2 * n + 2, :], split(bank[:, 7, :], 2)).then_inc(ab_o, 1)
                if not last:
                    o_split_hi(1, g + 1)
                if last:
                    wo_split_hi(1, 0, range(4))
                    y_split_hi(1, 0, 0, KT - 1)
                    wo_split_hi(1, 0, range(4, WO_EARLY))
                act.wait_ge(y_mm, g + 1)
                nc.scalar.copy(cd[:, 0, :], bank[:, 2, 0:FQ])
                nc.scalar.copy(cd[:, 1, :], bank[:, 6, 0:FQ]).then_inc(cd_cp, 1)

            fourier(0, first=True)
            with act.Fori(1, GROUPS - 1) as g:
                fourier(g)
            fourier(GROUPS - 1, last=True)

            out_his(1)

        @block.vector
        def _(dve):
            link = Chain(dve, dve_done)
            tscal, stt, tt_ = nc.vector.tensor_scalar, nc.vector.scalar_tensor_tensor, nc.vector.tensor_tensor
            dve.wait_ge(vec_T, 1)
            dve.wait_ge(cond_made, 1)
            link(nc.vector.tensor_copy(col[:, :], bank[:, 7, 0:R_ALL]))
            def modulation():
                dve.wait_ge(mod_T, 1)
                tt_(modc[:, 0:24, :], split(bank[:, 0, 0:48], 24), col[:, R_BMOD:R_BMOD + 24].unsqueeze(2).broadcast_to([P, 24, 2]),
                    ALU.add).then_inc(mod_made, 1)
                dve.wait_ge(mod_made, 1)
                gains(0)

            def gains(l):
                stt(gsc[:, 8 * l:8 * l + 8, :], modc[:, 24 * l + 8:24 * l + 16, :], 1.0,
                    col[:, R_NG + 8 * l:R_NG + 8 * l + 8].unsqueeze(2).broadcast_to([P, KT, 2]), ALU.add, ALU.mult).then_inc(mod_made, 1)

            dve.wait_ge(z_in, 64)
            for n in range(2):
                dve.wait_ge(f_mm, n + 1)
                link(tscal(f_x[0:FO, :], banks(4, 3, 0, TOK)[0:FO], fb[0:FO, n:n + 1], None, ALU.add))
                link(tscal(f_r[0:FO, :], f_x[0:FO, :], 1.0 / (2 * math.pi), MAGIC, ALU.mult, ALU.add))
                link(tscal(f_r[0:FO, :], f_r[0:FO, :], MAGIC, None, ALU.subtract))
                link(stt(f_x[0:FO, :], f_r[0:FO, :], -TWO_PI_HI, f_x[0:FO, :], ALU.mult, ALU.add))
                link(stt(f_x[0:FO, :], f_r[0:FO, :], -TWO_PI_LO, f_x[0:FO, :], ALU.mult, ALU.add))
                tscal(f_x[0:FO, :], f_x[0:FO, :], PI_IN, -PI_IN, ALU.min, ALU.max).then_inc(f_red, 1)

            def normalise(l, dst, src):
                for t in range(NT):
                    dve.wait_ge(x_rs, NT * l + t + 1)
                    tscal(dst[:, t, :], src[:, t, :], rstd[:, NT * l + t:NT * l + t + 1], None, ALU.mult).then_inc(x_n, 1)

            def layer_input():
                for e in range(24):
                    ch, k = divmod(e, KT)
                    a, w = CHUNKS[ch]
                    tmp = h_tmp[e % 4][:, 0:w]
                    if e % 2:
                        dve.wait_ge(h_full, e + 1)
                        link(nc.vector.tensor_copy(hT[0][:, k, a:a + w], tmp))
                    else:
                        dve.wait_ge(h_hi, e // 2 + 1)
                    tt_(hT[1][:, k, a:a + w], tmp, hT[0][:, k, a:a + w].bitcast(F32), ALU.subtract).then_inc(h_lo, 1)

            normalise(0, xs, xs)
            modulation()
            dve.wait_ge(mod_made, 2)
            layer_input()
            dve.wait_ge(small_in, 16 * 5)
            for t in range(NT):
                dve.wait_ge(l_rs, t + 1)
                if t >= 2:
                    dve.wait_ge(l_T, t)
                b = 2 * (t % 2)
                nc.vector.tensor_copy(kro[:, 1 + t, :], bank[:, b + 1, RANK:RANK + ROPE])
                for j in range(2):
                    last = stt(lat[t % 2][:, j * RANK:(j + 1) * RANK], bank[:, b + j, 0:RANK], rstd2[:, 2 * t + j:2 * t + j + 1],
                               lat_g[:, j * RANK:(j + 1) * RANK], ALU.mult, ALU.mult)
                last.then_inc(l_lat, 1)
            dve.wait_ge(l_lat, NT)
            swap = lambda a: a.rearrange("p t (x h f) -> p (t x) h f", x=2, h=2)
            for h in range(2):
                last = nc.vector.tensor_copy(swap(krs)[:, :, h, :], swap(kro[:, 1:9, :])[:, :, 1 - h, :])
            link(last)
            rt = lambda n: rope_t[:, n, :].rearrange("p (t f) -> p t f", t=8)
            nc.vector.tensor_copy(krr[:, 0, :], kro[:, 0, :])
            nc.vector.tensor_copy(krr[:, 9, :], kro[:, 9, :])
            tt_(krr[:, 1:9, :], kro[:, 1:9, :], rt(0), ALU.mult)
            link(tt_(krs, krs, rt(1), ALU.mult))
            tt_(krr[:, 1:9, :], krr[:, 1:9, :], krs, ALU.add).then_inc(kr_rot, 1)

            def w_split_lo(j, c):
                dve.wait_ge(w_his, c * 5 + (j + 1))
                tt_(w_lo[j % 3], w_raw[j % 3], w_hi[j % 3].bitcast(F32), ALU.subtract).then_inc(w_los, 1)

            def tap(dst, b, w, right):
                d, ps, r = split(dst, 3), bank[:, b:b + 3, 0:T3], int(right)
                add = lambda o, i: stt(o, i, w, o, ALU.mult, ALU.add)
                cut = LS - 2 * T3
                add(d[:, 0:2, 1 - r:T3 - r], ps[:, 0:2, r:T3 - 1 + r])
                add(d[:, 2, 1 - r:cut - r], ps[:, 2, r:cut - 1 + r])
                add(d[:, 2, cut + 1 - r:T3 - r], ps[:, 2, cut + r:T3 - 1 + r])
                if right:
                    return add(d[:, 0:2, T3 - 1], ps[:, 1:3, 0])
                return add(d[:, 1:3, 0], ps[:, 0:2, T3 - 1])

            w_split_lo(0, 0)

            def hyena_input(c, final):
                link.loop(c, 3)
                for j, (dst, m0) in enumerate(((u1, 4), (vt, 8), (x0, 0))):
                    w_split_lo(j + 1, c)
                    dve.wait_ge(d_mid, c * 3 + (j + 1))
                    link(tap(dst, 3 * (j % 2), col[:, bass.ds(c + (R_CW + m0), 1)], False))
                    tap(dst, 3 * (j % 2), col[:, bass.ds(c + (R_CW + 24 + m0), 1)], True).then_inc(d_rel[j], 1)
                    if j == 1:
                        dve.wait_ge(d_rel[1], c + 1)
                        tt_(vt, vt, u1, ALU.mult).then_inc(v_ready, 1)
                w_split_lo(4, c)
                dve.wait_ge(d_rel[2], c + 1)
                dve.wait_ge(d_rel[3], c + 2)
                tt_(x0, x0, ga, ALU.mult).then_inc(xg_ready, 1)
                if not final:
                    w_split_lo(0, c + 1)
                dve.wait_ge(mod_T, c + 2)
                tt_(modc[:, bass.ds(c * 6 + 24, 6), :], split(bank[:, 7, 0:12], 6),
                    col[:, bass.ds(c * 6 + (R_BMOD + 24), 6)].unsqueeze(2).broadcast_to([P, 6, 2]), ALU.add).then_inc(mod_made, 1)

            with dve.Fori(0, CA - 1) as c:
                hyena_input(c, False)
            hyena_input(CA - 1, True)
            link.end(CA)
            dve.wait_ge(mod_made, 2 + CA)
            gains(1)

            dve.wait_ge(sp_v, 16 * (CA + 1))
            dve.wait_ge(sp_x, 16 * (CA + 1))
            dve.wait_ge(dec_in, 64)
            for t in range(NT):
                dve.wait_ge(fh_mm, t + 1)
                if t >= 2:
                    dve.wait_ge(sd_made, t - 1)
                    dve.wait_ge(fh_mag, t - 1)
                    dve.wait_ge(sd_diff, t - 1)
                b, f = 2 * (t % 3), f_h[t % 2]
                tt_(f, bank[:, b:b + 2, :], decay[t].unsqueeze(1).broadcast_to([P, 2, DA]), ALU.mult).then_inc(fh_made, 1)
                dve.wait_ge(fh_made, t + 1)
                if t in (0, PROMPT):
                    dve.wait_ge(fh_mag, t + 1)
                    nc.vector.memset(f[0:1, 1, :], 0.0).then_inc(fh_zero, 1)
                    dve.wait_ge(fh_zero, 1 + t // PROMPT)
                tt_(sd[:, t, 1, :], f[:, 0, :], f[:, 1, :], ALU.subtract).then_inc(sd_diff, 1)
            dve.wait_ge(nrm_T, 1)
            nc.vector.reciprocal(rnorm[:, :], bank[:, 7, 0:2 * CA]).then_inc(nrm_made, 1)

            for kt in range(NK):
                dve.wait_ge(v_cp, kt + 1)
                tt_(vp[:, 0:2, :], vs[:, 0:2, :], vs[:, 2:4, :], ALU.add)
                link(tt_(vp[:, 2:4, :], vs[:, 0:2, :], vs[:, 2:4, :], ALU.subtract))
                dve.wait_ge(kp_made, kt + 1)
                four = lambda a: a.rearrange("p (s r) n -> p s r n", s=2)
                tt_(ks, vp, kp, ALU.mult)
                link(tt_(four(vs), four(vp), four(kp)[:, :, ::-1, :], ALU.mult))
                tt_(kp[:, 0:2, :], four(ks)[:, :, 0, :], four(ks)[:, :, 1, :], ALU.subtract)
                link(tt_(kp[:, 2:4, :], four(vs)[:, :, 0, :], four(vs)[:, :, 1, :], ALU.add))
                tt_(zz[:, kt, 0:2, :], kp[:, 0::2, :], kp[:, 1::2, :], ALU.add)
                tt_(zz[:, kt, 2:4, :], kp[:, 0::2, :], kp[:, 1::2, :], ALU.subtract).then_inc(z_made, 1)
            dve.wait_ge(k_cp, NK + 1)
            dve.wait_ge(z_made, NK)
            tt_(kp[:, 0:2, :], vs[:, 0:2, :], ks[:, 0:2, :], ALU.mult)
            link(tt_(kp[:, 2:4, :], vs[:, 0:2, :], ks[:, 1::-1, :], ALU.mult))
            tt_(yp[:, 0, :], kp[:, 0, :], kp[:, 1, :], ALU.subtract)
            tt_(yp[:, 1, :], kp[:, 2, :], kp[:, 3, :], ALU.add).then_inc(z_made, 1)

            for c in range(CA):
                s = c % 2
                vf = vf_in[s]
                dve.wait_ge(vx_in[s], 32 * (c // 2 + 1))
                link(tscal(vf, vf, col[:, R_SKIP + c:R_SKIP + c + 1], None, ALU.mult))
                dve.wait_ge(i_mm, c + 1)
                for odd in range(2):
                    stt(vf[:, odd:LS:2], bank[:, 4 - 4 * s + odd, :], rnorm[:, c:c + 1], vf[:, odd:LS:2], ALU.mult, ALU.add)
                link(stt(vf[:, LS:TOK], bank[:, 4 - 4 * s + 2, 0:P], rnorm[:, CA + c:CA + c + 1], vf[:, LS:TOK], ALU.mult, ALU.add))
                tt_(yT[:, c, :], vf, xg_in[s], ALU.mult).then_inc(i_done, 1)

            def gate_diag(l, n):
                if n >= 2:
                    dve.wait_ge(dg_mm, 4 * l + n - 1)
                for a in range(4):
                    last = tscal(diag[l][n % 2][:, a * P:(a + 1) * P], ident[:, :], modc[:, 24 * l + 16 + 4 * (n % 2) + a, n // 2:n // 2 + 1], None, ALU.mult)
                last.then_inc(dg_made, 1)

            def gate_rows(l, b):
                for n in range(6):
                    if n >= 2:
                        dve.wait_ge(dg_mm, 4 * l + n - 1)
                        nc.vector.tensor_copy(gateb[:, (n - 2) // 2, n % 2 * 512:(n % 2 + 1) * 512], bank[:, b[n - 2], :]).then_inc(gb_cp, 1)
                    if n < 4:
                        gate_diag(l, n)

            dve.wait_ge(i_done, CA)
            dve.wait_ge(st_state, 32)
            gate_rows(0, range(4))
            for m in range(2):
                dve.wait_ge(kr_cp, m + 2)
                tt_(k_lo[m][64:P, :], kT[m][64:P, :], k_hi[m][64:P, :].bitcast(F32), ALU.subtract).then_inc(kv_set, 1)
            dve.wait_ge(v_all_cp, 10)

            with dve.Fori(0, HEADS // 2) as i:
                link.loop(i, 2 * (3 + 2 * NT))
                def queries(s, *parts):
                    for n in parts:
                        name = f"q{n}"
                        dve.wait_ge(pj_mm, i * 14 + (7 * s + 1 + STEPS[s].index(name)))
                        b, a = STEP_BANK[s][name], KS3 * n
                        w = min(KS3, LS - a)
                        if n:
                            dve.wait_ge(pj_q, i * 6 + (3 * s + n))
                        if w < KS3:
                            nc.vector.tensor_copy(qT[s][64:96, a + w:a + KS3], bank[64:96, b, w:KS3])
                        tt_(qT[s][64:96, a:a + w], bank[64:96, b, 0:w], rope_q[64:96, a:a + w], ALU.mult)
                        link(tt_(rtmp[64:96, 0:w], bank[96:128, b, 0:w], rope_q[96:128, a:a + w], ALU.mult))
                        dve.wait_ge(pq_cp, i * 6 + (3 * s + n + 1))
                        tt_(qT[s][64:96, a:a + w], qT[s][64:96, a:a + w], rtmp[64:96, 0:w], ALU.add).then_inc(pj_q, 1)

                def query_los(s, *parts):
                    for n in parts:
                        dve.wait_ge(pq_his, i * 6 + (3 * s + n + 1))
                        for m, a, b in q_hi(s, KS3 * n, KS3 * (n + 1)):
                            last = tt_(q_lo[s][0:QK, a:b], qT[s][0:QK, a:b], m[0:QK].bitcast(F32), ALU.subtract)
                        last.then_inc(pq_los, 1)

                def key_los(s, *parts):
                    for n in parts:
                        dve.wait_ge(pk_his, i * 8 + (4 * s + n + 1))
                        a, w = KS3 * n, KS3 if n < 3 else P
                        tt_(k_lo[s][0:NOPE, a:a + w], bank[0:NOPE, STEP_BANK[s][f"k{n}"], 0:w], k_hi[s][0:NOPE, a:a + w].bitcast(F32), ALU.subtract).then_inc(pj_k, 1)

                queries(0, 0)
                key_los(0, 0)
                query_los(0, 0)
                key_los(0, 1, 2)
                nc.vector.tensor_copy(vpair, vall[:, :, bass.ds(i * P, P)]).then_inc(kv_set, 1)
                for s in range(2):
                    def maxima(t):
                        dve.wait_ge(s_mm, i * 18 + (9 * s + t + 1))
                        b0, m = 3 * (t % 2), t % 2
                        src = bank[:, b0:b0 + 3, 0:KS3] if t < PROMPT else bank[:, b0, 0:P]
                        link(nc.vector.tensor_reduce(amax[:, m:m + 1], src, mybir.AxisListType.XY if t < PROMPT else mybir.AxisListType.X, ALU.max))
                        tscal(nmax[:, m:m + 1], amax[:, m:m + 1], -SCALE, None, ALU.mult).then_inc(s_max, 1)

                    def norm(t):
                        m, w = t % 2, KEYS if t < PROMPT else P
                        dve.wait_ge(s_exp, i * 18 + (9 * s + t + 1))
                        link(nc.vector.reciprocal(rinv[:, m:m + 1], rsum[:, m:m + 1]))
                        tscal(px[m][:, 0:w], px[m][:, 0:w], rinv[:, m:m + 1], None, ALU.mult).then_inc(p_norm, 1)

                    def outputs(s, t):
                        dve.wait_ge(o_mm, i * 18 + (9 * s + t + 2))
                        r, a = slice(s * VD, (s + 1) * VD), t * P
                        tt_(yT[r, bass.ds(i + CA, 1), a:a + P].rearrange("p a n -> p (a n)"), bank[r, OUT_BANK[s][t], KS3:KS3 + P], sgate[r, a:a + P], ALU.mult).then_inc(o_cp, 1)

                    maxima(0)
                    if s == 0:
                        key_los(0, 3)
                        queries(0, 1)
                        norm(0)
                        queries(0, 2)
                        dve.wait_ge(sg_in, i * 16 + 16)
                        maxima(1)
                    else:
                        maxima(1)
                        norm(0)
                        outputs(0, PROMPT - 1)
                        outputs(0, PROMPT)
                    norm(1)
                    for t in range(1, PROMPT):
                        maxima(t + 1)
                        u = 9 * s + t
                        dve.wait_ge(pt_mm_d, i * 16 + (8 * s + t + 1))
                        dve.wait_ge(o_mm, i * 18 + (u if t >= 2 else 9 * s + 1))
                        nc.vector.tensor_copy(pT[t % 2][:, 7:9, :], bank[:, 3 * (t % 2):3 * (t % 2) + 2, KS3:KS3 + P]).then_inc(pt_cp_d, 1)
                        if t <= 2:
                            query_los(s, t)
                        if t == PROMPT - 1:
                            norm(PROMPT)
                            outputs(s, t - 1)
                        else:
                            outputs(s, t - 1)
                            norm(t + 1)
                    if s == 0:
                        key_los(1, 0)
                        queries(1, 0, 1)
                        query_los(1, 0)
                        key_los(1, 1, 2)
                        key_los(1, 3)
                        queries(1, 2)
                    else:
                        outputs(1, PROMPT - 1)
                        outputs(1, PROMPT)
            link.end(HEADS // 2)

            def wo_split_lo(l, h, ks):
                a = slice(512 * h, 512 * (h + 1))
                for k in ks:
                    dve.wait_ge(wo_his, 16 * l + 8 * h + k + 1)
                    tt_(wo_lo[l][k][:, a], wo_raw[l][:, k, a], wo_hi[l][k][:, a].bitcast(F32), ALU.subtract).then_inc(wo_los, 1)

            def y_split_lo(l, t, k0, k1, his):
                dve.wait_ge(y_his, his)
                hi, lo = (m[:, k0:k1, :] for m in y_sl[l][t % 2])
                tt_(lo, y_in[l][:, k0:k1, t * P:(t + 1) * P], hi.bitcast(F32), ALU.subtract).then_inc(y_los, 1)

            def final_norm(t):
                dve.wait_ge(fg_in, 16)
                dve.wait_ge(x_rs, 2 * NT + t + 1)
                stt(xo[:, t, :], xo[:, t, :], rstd[:, 2 * NT + t:2 * NT + t + 1], fgb, ALU.mult, ALU.mult).then_inc(out_ready, 1)

            def out_los(l):
                def y_lo(t):
                    if t >= 2:
                        dve.wait_ge(g_mm, NT * l + t - 1)
                    y_split_lo(l, t, 0, KT, NT * l + t + 1 + l)

                if l:
                    y_split_lo(1, 0, KT - 1, KT, NT + 2)
                else:
                    y_lo(0)
                wo_split_lo(l, 0, range(WO_EARLY * l, KT))
                y_lo(1)
                wo_split_lo(l, 1, range(KT))
                for t in range(NT):
                    x = (xr[t % 4], xo[:, t, :])[l]
                    if l and t:
                        final_norm(t - 1)
                    if t + 2 < NT:
                        y_lo(t + 2)
                    grp = int(t == PROMPT)
                    dve.wait_ge(x_in[t], 32 * (l + 1))
                    dve.wait_ge(g_mm, NT * l + t + 1)
                    b = 2 * (t % 2)
                    y = bank[:, b:b + 2, :]
                    link(tt_(y, y, split(gateb[:, grp, :], 2), ALU.mult))
                    tt_(split(x, 2), split(x, 2), y, ALU.add).then_inc(g_add, 1)
                    if l == 0:
                        if t:
                            next_lo(t - 1)
                        if t == 4:
                            o_split_lo(1, 0)
                        dve.wait_ge(x_rs, NT + t + 1)
                        dve.wait_ge(x_in[t], 48)
                        tscal(x, x, rstd[:, NT + t:NT + t + 1], None, ALU.mult).then_inc(x_n, 1)

            def next_lo(t):
                dve.wait_ge(h_hi, 12 + t + 1)
                a = slice(t * P, (t + 1) * P)
                tt_(hT[1][:, :, a], split(xr[t % 4], KT), hT[0][:, :, a].bitcast(F32), ALU.subtract).then_inc(h_lo, 1)

            def o_split_lo(j, g):
                dve.wait_ge((uw_his, gw_his)[j], g + 1)
                tt_(o_lo[j], o_raw[j], o_hi[j].bitcast(F32), ALU.subtract).then_inc((uw_los, gw_los)[j], 1)

            out_los(0)
            o_split_lo(0, 0)

            def fourier(g, first=False, final=False):
                link.loop(g, 2)
                if first:
                    next_lo(PROMPT)
                if final:
                    gate_rows(1, (6, 7, 6, 7))
                if not final:
                    o_split_lo(0, g + 1)
                for n in (0, 2, 4):
                    dve.wait_ge(ab_mm, g * 5 + (n + 1))
                    w = 2 if n < 4 else 1
                    nc.vector.tensor_copy(ab[:, 2 * n:2 * n + w, :], split(bank[:, 6, 0:256 * w], w)).then_inc(ab_e, 1)
                if not final:
                    o_split_lo(1, g + 1)
                if final:
                    wo_split_lo(1, 0, range(4))
                    y_split_lo(1, 0, 0, KT - 1, NT + 1)
                    wo_split_lo(1, 0, range(4, WO_EARLY))
                dve.wait_ge(cd_cp, g + 1)
                for q in range(2):
                    tt_(tt[:, 2 * q, :], bank[:, q, 0:FQ], cd[:, q, :], ALU.add)
                    last = tt_(tt[:, 2 * q + 1, :], bank[:, q, 0:FQ], cd[:, q, :], ALU.subtract)
                link(last)
                tt_(y1T[:, bass.ds(g, 1), LS:TOK].rearrange("p a n -> p (a n)"), bank[:, 7, 0:P], sg[:, LS:TOK], ALU.mult).then_inc(y_rel, 1)
                n = HALF // 2
                tt_(yt[:, 0:n + 1], tt[:, 0, 0:n + 1], tt[:, 2, 0:n + 1], ALU.add)
                tt_(yt[:, 2 * n:n:-1], tt[:, 1, 0:n], tt[:, 3, 0:n], ALU.subtract)
                tt_(yt[:, 2 * n + 1:3 * n + 1], tt[:, 1, 1:n + 1], tt[:, 3, 1:n + 1], ALU.add)
                link(tt_(yt[:, 4 * n - 1:3 * n:-1], tt[:, 0, 1:n], tt[:, 2, 1:n], ALU.subtract))
                tt_(y1T[:, bass.ds(g, 1), 0:LS].rearrange("p a n -> p (a n)"), yt[:, 0:LS], sg[:, 0:LS], ALU.mult).then_inc(y_done, 1)

            fourier(0, first=True)
            with dve.Fori(1, GROUPS - 1) as g:
                fourier(g)
            fourier(GROUPS - 1, final=True)
            link.end(GROUPS)

            out_los(1)
            final_norm(NT - 1)

        @block.gpsimd
        def _(pool):
            link = Chain(pool, pool_done)
            link(nc.gpsimd.memset(ident[:, :], 0.0))
            nc.gpsimd.affine_select(out=ident[:, :], in_=ident[:, :], compare_op=ALU.not_equal, fill=1.0, base=0,
                                    pattern=[[-1, P]], channel_multiplier=1).then_inc(consts_made, 1)
            nc.gpsimd.memset(ones[:, :], 1.0).then_inc(consts_made, 1)
            nc.gpsimd.memset(half_neg[:, :], -0.5).then_inc(consts_made, 1)
            for n, m in enumerate(kT):
                pool.wait_ge(consts_made, 3 + n)
                nc.gpsimd.memset(m[QK:P, :], 0.0).then_inc(consts_made, 1)
            pool.wait_ge(consts_made, 5)

            def inverse_root(dst, src, n, width):
                link(nc.gpsimd.tensor_scalar(src, src, 1.0 / n, EPS, ALU.mult, ALU.add))
                return nc.gpsimd.tensor_tensor(dst, src, half_neg[:, 0:width], ALU.pow)

            def row_norms(l):
                for t in range(NT):
                    a = NT * l + t
                    pool.wait_ge(x_sq, a + 1)
                    inverse_root(rstd[:, a:a + 1], ssq[:, a:a + 1], D, 1).then_inc(x_rs, 1)

            row_norms(0)
            pool.wait_ge(wlat_in, 16)
            nc.gpsimd.tensor_copy(w_lat[0], w_lat_raw).then_inc(wl_hi, 1)
            pool.wait_ge(wl_hi, 1)
            nc.gpsimd.tensor_tensor(w_lat[1], w_lat_raw, w_lat[0].bitcast(F32), ALU.subtract).then_inc(wl_lo, 1)
            for t in range(NT):
                pool.wait_ge(l_sq, t + 1)
                inverse_root(rstd2[:, 2 * t:2 * t + 2], ssq2[:, 2 * t:2 * t + 2], RANK, 2).then_inc(l_rs, 1)
            for t in range(NT):
                pool.wait_ge(fh_made, t + 1)
                if t in (0, PROMPT):
                    pool.wait_ge(fh_zero, 1 + t // PROMPT)
                nc.gpsimd.tensor_tensor(sd[:, t, 0, :], f_h[t % 2][:, 0, :], f_h[t % 2][:, 1, :], ALU.add).then_inc(sd_made, 1)
            pool.wait_ge(sp_g, 16 * (CA + 1))
            for kt in range(NK):
                pool.wait_ge(k_cp, kt + 1)
                nc.gpsimd.tensor_tensor(kp[:, 0:2, :], ks[:, 0:2, :], ks[:, 2:4, :], ALU.add)
                nc.gpsimd.tensor_tensor(kp[:, 2:4, :], ks[:, 0:2, :], ks[:, 2:4, :], ALU.subtract).then_inc(kp_made, 1)
            pool.wait_ge(i_mm, CA)
            zeros = [(m[QK:P, :], None) for m in qT]
            zeros += [(m[QK:P], qT[h][QK:P, a:b]) for h in range(2) for m, a, b in q_hi(h, 0, TOK)]
            zeros += [(q_lo[h][QK:P, :], qT[h][QK:P, :]) for h in range(2)]
            for n, (dst, src) in enumerate(zeros):
                if n:
                    pool.wait_ge(pads_made, n)
                ins = nc.gpsimd.tensor_copy(dst, src) if src is not None else nc.gpsimd.memset(dst, 0.0)
                ins.then_inc(pads_made, 1)
            pool.wait_ge(pads_made, len(zeros))
            row_norms(1)
            row_norms(2)


def tables():
    f = np.float32
    out = {}

    def positions(L):
        n = np.arange(L)
        t = np.linspace(0.0, 1.0, L)[:, None]
        w = 2 * math.pi * n[:, None] / L
        fr = np.linspace(1e-4, BANDS - 1, BANDS)[None, :]
        z = np.concatenate([t, np.cos(fr * w), -np.sin(fr * w)], axis=-1)
        lo, hi = math.log(1e-2) / 1.5, math.log(1e-2) / 0.3
        return z, np.exp(-t * np.abs(np.linspace(lo, hi, DA)))

    zs, ds = positions(LS)
    zp, dp = positions(LP)
    z = np.concatenate([zs[0::2], zs[1::2], zp])
    dec = np.concatenate([ds[0::2], ds[1::2], dp])
    out["zT"] = z.T.astype(f)
    out["decay"] = dec.reshape(NT, P, DA).transpose(1, 0, 2).astype(f)
    k = np.arange(HALF)
    par = [np.arange(0, LS, 2), np.arange(1, LS, 2)]
    ang = [np.outer(n, math.pi * (2 * k + 1) / (2 * LS)) for n in par]
    quad = np.stack([np.cos(ang[0]), -np.sin(ang[0]), np.cos(ang[1]), -np.sin(ang[1])])
    out["tf"] = quad.reshape(4, NK, P, NK, P).transpose(3, 2, 0, 1, 4).astype(f)
    out["ti"] = (quad / LS).transpose(2, 0, 1).reshape(NK, P, 4, HALF).transpose(1, 0, 2, 3).astype(f)
    n = np.arange(LP)
    a = np.outer(n, math.pi * (2 * n + 1) / (2 * LP))
    pair = np.stack([np.cos(a), -np.sin(a)])
    out["tp"] = pair.transpose(1, 0, 2).astype(f)
    out["tpi"] = (pair / LP).transpose(2, 0, 1).astype(f)
    t = np.arange(LS)
    inv = 10000.0 ** (-np.arange(0, ROPE // 2, 2) / (ROPE // 2))
    an = np.stack([(t // GRID_W)[:, None] * inv, (t % GRID_W)[:, None] * inv], axis=1)
    cos = np.repeat(np.cos(an)[:, :, None, :], 2, axis=2).reshape(LS, ROPE)
    sin = np.stack([-np.sin(an), np.sin(an)], axis=2).reshape(LS, ROPE)
    both = np.stack([cos, sin])
    out["rope_t"] = both.reshape(2, LS // P, P, ROPE).transpose(2, 0, 1, 3).reshape(P, 2, 256).astype(f)
    out["rope_q"] = both.transpose(0, 2, 1).reshape(2 * ROPE, LS).astype(f)
    kk = np.arange(FQ)
    quad = []
    for nn in par:
        x = 2 * math.pi * np.outer(nn, kk) / LS
        quad += [np.cos(x), -np.sin(x)]
    quad = np.stack(quad) / math.sqrt(LS * P)
    out["tl"] = quad.reshape(4, NK, P, FQ).transpose(2, 1, 0, 3).astype(f)
    x = 2 * math.pi * np.outer(n, n) / P
    out["cg"] = np.concatenate([np.cos(x), np.sin(x)], axis=1).astype(f)
    out["tlp"] = (np.stack([np.cos(x), -np.sin(x)]) / math.sqrt(LP * P)).transpose(1, 0, 2).astype(f)
    return {name: np.ascontiguousarray(v) for name, v in out.items()}


def layout(inputs):
    i = {k: np.asarray(v) for k, v in inputs.items()}
    out = {}
    out["x_sample"], out["x_prompt"] = i["x_sample"][0], i["x_prompt"][0]
    out["vecs"] = np.concatenate([i["b_mod"].reshape(48, P), i["norm_g"].reshape(16, P), i["conv_w"].reshape(36, P),
                                  i["conv_b"].reshape(12, P), i["hyena_skip"].reshape(4, P)])
    out["cond"] = np.concatenate([i["c"].reshape(8, P), i["c_ctx"].reshape(8, P)])
    out["w_mod"] = i["w_mod"][0].reshape(KT, P, 6, 512).transpose(2, 1, 0, 3)
    out["w_mod2"] = i["w_mod"][1].reshape(KT, P, CA, 3, 2 * P).transpose(2, 3, 1, 0, 4)
    w = i["w_in_e"][0].reshape(KT, P, -1).transpose(1, 0, 2)
    tile = lambda a, n: w[:, :, a:a + n * P].reshape(P, KT, n, P).transpose(2, 0, 1, 3)
    out["w_in"] = np.stack([tile(DA, CA), tile(2 * DA, CA), tile(0, CA), tile(3 * DA, CA), tile(4 * DA + LAT, CA)])
    out["w_lat"] = w[:, :, 4 * DA:4 * DA + LAT]
    out["qg"], out["kvg"], out["final_g"] = i["q_norm_g"][0], i["kv_norm_g"][0], i["final_g"]
    out["cache_ckv"], out["cache_krope"] = i["cache_ckv"][0, 0], i["cache_krope"][0, 0]
    out["f_w1"], out["f_w2"], out["f_w3"] = i["filt_w1"][0], i["filt_w2"][0], i["filt_w3"][0]
    out["f_b"] = np.stack([i["filt_b1"][0], i["filt_b2"][0]], axis=1)
    q = i["w_uq"][0].reshape(RANK, HEADS, QK)
    rope = q[:, :, NOPE:].reshape(RANK, HEADS, 2, 2, 8)[:, :, :, ::-1, :].reshape(RANK, HEADS, ROPE)
    q = np.concatenate([q, rope], axis=2)
    out["w_q"] = q.reshape(2, P, HEADS, P).transpose(2, 1, 0, 3)
    kv = i["w_ukv"][0].reshape(2, P, HEADS, NOPE + VD)
    out["w_k"] = kv[..., 0:NOPE].transpose(2, 1, 0, 3)
    out["w_v"] = kv[..., NOPE:].transpose(1, 0, 2, 3).reshape(P, 2, HEADS * VD)
    out["w_oe"] = i["w_out_e"][0].reshape(KT, P, D).transpose(1, 0, 2)
    out["w_io"] = i["w_in_o"][0].reshape(KT, P, 2, GROUPS, P).transpose(2, 3, 1, 0, 4)
    out["fnet_w"] = i["fnet_w"][0]
    out["w_oo"] = i["w_out_o"][0].reshape(KT, P, D).transpose(1, 0, 2)
    return {name: np.ascontiguousarray(v) for name, v in out.items()}


OUTS = {"y_prompt": (LP, D), "y_sample": (LS, D), "state_ckv": (LP, RANK), "state_krope": (LP, ROPE)}
SPILLS = ("sp_v", "sp_x", "sp_g")


def kernel(**inputs):
    import concourse.bacc as bacc
    from concourse.bass_utils import run_bass_kernel_spmd

    nc = bacc.Bacc("TRN2", target_bir_lowering=False, num_devices=1)
    arrays = {**layout(inputs), **tables()}
    T = {n: nc.dram_tensor(f"{n}_in", a.shape, F32, kind="ExternalInput").ap() for n, a in arrays.items()}
    for n, shape in OUTS.items():
        T[n] = nc.dram_tensor(f"{n}_out", shape, F32, kind="ExternalOutput").ap()
    for n in SPILLS:
        T[n] = nc.dram_tensor(f"{n}_rows", (CA, P, TOK), F32, kind="Internal").ap()
    T["sp_1"] = nc.dram_tensor("sp_1_rows", (NT, P, D), F32, kind="Internal").ap()
    build(nc, T)
    r = run_bass_kernel_spmd(nc, [{f"{n}_in": a for n, a in arrays.items()}], core_ids=[0]).results[0]
    return (r["y_prompt_out"].reshape(1, LP, D), r["y_sample_out"].reshape(1, LS, D),
            r["state_ckv_out"].reshape(1, 1, LP, RANK), r["state_krope_out"].reshape(1, 1, LP, ROPE))
```
